# Optimizing a Trainium2 kernel written in Bass

```python
import jax, jax.numpy as jnp
from jax import lax
import numpy as np

D_MODEL = 1024
BATCH = 1
SEQ = 1024
DEPTH = 1

D_MIX = D_MODEL
N_MIXERS = 4
GROUP_WIDTH = D_MIX // N_MIXERS
HEAD_DIM = 64
EPS = 1e-6
MASK_VALUE = -1e30

FOX_HEADS = GROUP_WIDTH // HEAD_DIM
FOX_BLOCK = 128

SSD_HEADS = GROUP_WIDTH // HEAD_DIM
SSD_GROUPS = 2
SSD_STATE = 64
SSD_CONV = 4
SSD_CHUNK = 128
SSD_CONV_DIM = GROUP_WIDTH + 2 * SSD_GROUPS * SSD_STATE

GLA_HEADS = 4
GLA_KEY_DIM = GROUP_WIDTH // 2
GLA_HEAD_K = GLA_KEY_DIM // GLA_HEADS
GLA_HEAD_V = GROUP_WIDTH // GLA_HEADS
GLA_GATE_RANK = 16
GLA_TAU = 16.0
GLA_CHUNK = 64

HGRN_HEADS = 4
HGRN_EXPAND = 64
HGRN_FDIM = HGRN_HEADS * HGRN_EXPAND
HGRN_HEAD_V = GROUP_WIDTH // HGRN_HEADS
HGRN_CHUNK = 16

N_MEM = 256
XA_HEADS = 4
XA_HEAD_DIM = D_MODEL // XA_HEADS

D_FF = 256 * ((8 * D_MODEL // 3 + 255) // 256)
FFN_CONV = 3

IN_SPLITS = (
    GROUP_WIDTH, GROUP_WIDTH, GROUP_WIDTH, FOX_HEADS,
    GROUP_WIDTH, SSD_CONV_DIM, SSD_HEADS,
    GLA_KEY_DIM, GLA_KEY_DIM, GROUP_WIDTH, GLA_GATE_RANK, GROUP_WIDTH,
    HGRN_FDIM, HGRN_FDIM, GROUP_WIDTH, GROUP_WIDTH,
)
D_IN = sum(IN_SPLITS)

kernel_name = 'hybrid_fox_ssd_gla_hgrn2_block'

def rms_norm(x, w):
    xf = x.astype(jnp.float32)
    y = xf * lax.rsqrt(jnp.mean(xf * xf, axis=-1, keepdims=True) + EPS)
    return (y * w.astype(jnp.float32)).astype(x.dtype)

def split_columns(t, sizes):
    cuts = np.cumsum(np.asarray(sizes))[:-1].tolist()
    return jnp.split(t, cuts, axis=-1)

def causal_depthwise_conv(x, w, bias):
    k_width, c = w.shape
    y = lax.conv_general_dilated(
        x, w[:, None, :].astype(x.dtype), window_strides=(1,), padding=((k_width - 1, 0),),
        dimension_numbers=('NWC', 'WIO', 'NWC'), feature_group_count=c)
    return y + bias.astype(y.dtype)

def scan_chunk_states(d_state, decay):
    def step(s, inp):
        ds, g = inp
        return s * g + ds, s
    s0 = jnp.zeros_like(d_state[:, 0])
    _, s_in = lax.scan(step, s0, (jnp.moveaxis(d_state, 1, 0), jnp.moveaxis(decay, 1, 0)))
    return jnp.moveaxis(s_in, 0, 1)

def chunked_gated_linear_attention(q, k, v, log_decay, chunk):
    b, t, h, dk = q.shape
    dv = v.shape[-1]
    n = t // chunk
    f32 = jnp.float32
    q = q.astype(f32).reshape(b, n, chunk, h, dk)
    k = k.astype(f32).reshape(b, n, chunk, h, dk)
    v = v.astype(f32).reshape(b, n, chunk, h, dv)
    g_cs = jnp.cumsum(log_decay.astype(f32).reshape(b, n, chunk, h, dk), axis=2)
    q_dec = q * jnp.exp(g_cs)
    k_inv = k * jnp.exp(-g_cs)
    k_end = k * jnp.exp(g_cs[:, :, -1:] - g_cs)
    causal = jnp.tril(jnp.ones((chunk, chunk), bool))
    att = jnp.where(causal, jnp.einsum('bnihd,bnjhd->bnhij', q_dec, k_inv), 0.0)
    o = jnp.einsum('bnhij,bnjhv->bnihv', att, v)
    d_state = jnp.einsum('bnjhd,bnjhv->bnhdv', k_end, v)
    s_in = scan_chunk_states(d_state, jnp.exp(g_cs[:, :, -1])[..., None])
    o = o + jnp.einsum('bnihd,bnhdv->bnihv', q_dec, s_in)
    return o.reshape(b, t, h, dv)

def forgetting_attention(q, k, v, f_logit, q_norm, k_norm, o_norm):
    b, t, _ = q.shape
    q = rms_norm(q.reshape(b, t, FOX_HEADS, HEAD_DIM), q_norm)
    k = rms_norm(k.reshape(b, t, FOX_HEADS, HEAD_DIM), k_norm)
    v = v.reshape(b, t, FOX_HEADS, HEAD_DIM)
    cum_log_f = jnp.cumsum(jax.nn.log_sigmoid(f_logit.astype(jnp.float32)), axis=1)
    cum_log_f = jnp.transpose(cum_log_f, (0, 2, 1))
    scale = HEAD_DIM ** -0.5
    pos = jnp.arange(t)
    outs = []
    for start in range(0, t, FOX_BLOCK):
        end = start + FOX_BLOCK
        logits = jnp.einsum('bqhd,bkhd->bhqk', q[:, start:end], k[:, :end]).astype(jnp.float32) * scale
        logits = logits + cum_log_f[:, :, start:end, None] - cum_log_f[:, :, None, :end]
        causal = pos[start:end, None] >= pos[None, :end]
        probs = jax.nn.softmax(jnp.where(causal, logits, MASK_VALUE), axis=-1)
        outs.append(jnp.einsum('bhqk,bkhd->bqhd', probs.astype(v.dtype), v[:, :end]))
    o = rms_norm(jnp.concatenate(outs, axis=1), o_norm)
    return o.reshape(b, t, GROUP_WIDTH)

def ssd_chunked_scan(x, dt, a, bm, cm):
    b, t, h, p = x.shape
    n = t // SSD_CHUNK
    rep = h // bm.shape[2]
    cs = (b, n, SSD_CHUNK)
    bh = jnp.repeat(bm.astype(jnp.float32), rep, axis=2).reshape(*cs, h, SSD_STATE)
    ch = jnp.repeat(cm.astype(jnp.float32), rep, axis=2).reshape(*cs, h, SSD_STATE)
    xdt = (x * dt[..., None]).reshape(*cs, h, p)
    a_cs = jnp.cumsum((dt * a).reshape(*cs, h), axis=2)
    causal = jnp.tril(jnp.ones((SSD_CHUNK, SSD_CHUNK), bool))[:, :, None]
    seg = a_cs[:, :, :, None, :] - a_cs[:, :, None, :, :]
    decay = jnp.where(causal, jnp.exp(jnp.where(causal, seg, 0.0)), 0.0)
    scores = jnp.einsum('bnihs,bnjhs->bnijh', ch, bh) * decay
    y = jnp.einsum('bnijh,bnjhp->bnihp', scores, xdt)
    to_end = jnp.exp(a_cs[:, :, -1:, :] - a_cs)
    d_state = jnp.einsum('bnjhs,bnjhp->bnhps', bh * to_end[..., None], xdt)
    s_in = scan_chunk_states(d_state, jnp.exp(a_cs[:, :, -1, :])[..., None, None])
    y = y + jnp.einsum('bnihs,bnhps->bnihp', ch * jnp.exp(a_cs)[..., None], s_in)
    return y.reshape(b, t, h, p)

def mamba2_mixer(z, xbc, dt_raw, conv_w, conv_b, dt_bias, a_log, d_skip, g_norm):
    b, t, _ = z.shape
    f32 = jnp.float32
    xbc = jax.nn.silu(causal_depthwise_conv(xbc, conv_w, conv_b))
    xs, bm, cm = split_columns(xbc, (GROUP_WIDTH, SSD_GROUPS * SSD_STATE, SSD_GROUPS * SSD_STATE))
    xs = xs.reshape(b, t, SSD_HEADS, HEAD_DIM).astype(f32)
    dt = jax.nn.softplus(dt_raw.astype(f32) + dt_bias.astype(f32))
    a = -jnp.exp(a_log.astype(f32))
    y = ssd_chunked_scan(xs, dt, a, bm.reshape(b, t, SSD_GROUPS, SSD_STATE),
                         cm.reshape(b, t, SSD_GROUPS, SSD_STATE))
    y = y + xs * d_skip.astype(f32)[:, None]
    y = y.reshape(b, t, GROUP_WIDTH) * jax.nn.silu(z.astype(f32))
    y = rms_norm(y.reshape(b, t, SSD_GROUPS, GROUP_WIDTH // SSD_GROUPS),
                 g_norm.reshape(SSD_GROUPS, GROUP_WIDTH // SSD_GROUPS))
    return y.reshape(b, t, GROUP_WIDTH).astype(z.dtype)

def gla_mixer(q, k, v, gate_lr, r, w_gate_up, b_gate, o_norm):
    b, t, _ = q.shape
    log_alpha = jax.nn.log_sigmoid((gate_lr @ w_gate_up + b_gate).astype(jnp.float32)) / GLA_TAU
    shp = (b, t, GLA_HEADS, GLA_HEAD_K)
    o = chunked_gated_linear_attention(q.reshape(shp) * GLA_HEAD_K ** -0.5, k.reshape(shp),
                                       v.reshape(b, t, GLA_HEADS, GLA_HEAD_V), log_alpha.reshape(shp), GLA_CHUNK)
    o = rms_norm(o, o_norm).reshape(b, t, GROUP_WIDTH)
    return (o * jax.nn.silu(r.astype(jnp.float32))).astype(q.dtype)

def hgrn2_mixer(q, f_logit, inp, g, lower_bound, o_norm):
    b, t, _ = q.shape
    z = f_logit.astype(jnp.float32)
    lb = lower_bound.astype(jnp.float32)
    log_f = jnp.log(lb + (1.0 - lb) * jax.nn.sigmoid(z))
    one_minus_f = (1.0 - lb) * jax.nn.sigmoid(-z)
    shp = (b, t, HGRN_HEADS, HGRN_EXPAND)
    o = chunked_gated_linear_attention(q.reshape(shp), one_minus_f.reshape(shp),
                                       inp.reshape(b, t, HGRN_HEADS, HGRN_HEAD_V), log_f.reshape(shp), HGRN_CHUNK)
    o = rms_norm(o, o_norm).reshape(b, t, GROUP_WIDTH)
    return (o * jax.nn.silu(g.astype(jnp.float32))).astype(q.dtype)

def memory_cross_attention(h, mem_n, w_q, w_kv, w_o, q_norm, k_norm):
    b, t, _ = h.shape
    m = mem_n.shape[1]
    q = rms_norm((h @ w_q).reshape(b, t, XA_HEADS, XA_HEAD_DIM), q_norm)
    k, v = jnp.split(mem_n @ w_kv, 2, axis=-1)
    k = rms_norm(k.reshape(b, m, XA_HEADS, XA_HEAD_DIM), k_norm)
    v = v.reshape(b, m, XA_HEADS, XA_HEAD_DIM)
    logits = jnp.einsum('bthd,bmhd->bhtm', q, k).astype(jnp.float32) * XA_HEAD_DIM ** -0.5
    probs = jax.nn.softmax(logits, axis=-1).astype(v.dtype)
    o = jnp.einsum('bhtm,bmhd->bthd', probs, v).reshape(b, t, D_MODEL)
    return o @ w_o

def conv_glu_ffn(h, w_up, conv_w, conv_b, w_down):
    gate, val = jnp.split(h @ w_up, 2, axis=-1)
    gate = causal_depthwise_conv(gate, conv_w, conv_b)
    return (jax.nn.silu(gate) * val) @ w_down

def setup_inputs(seed: int = 0) -> dict:
    key = jax.random.key(seed)
    ks = iter(jax.random.split(key, 48))
    f32 = jnp.float32
    L = DEPTH

    def nrm(shape, scale):
        return jax.random.normal(next(ks), shape, f32) * scale

    def gain(shape):
        return 1.0 + nrm(shape, 0.02)

    def unif(shape, lo, hi):
        return jax.random.uniform(next(ks), shape, f32, lo, hi)

    x = nrm((BATCH, SEQ, D_MODEL), 1.0)
    mem = nrm((BATCH, N_MEM, D_MODEL), 1.0)
    ln_mix = gain((L, D_MODEL))
    w_in = nrm((L, D_MODEL, D_IN), D_MODEL ** -0.5)
    w_out = nrm((L, D_MIX, D_MODEL), D_MIX ** -0.5)
    fox_f_bias = unif((L, FOX_HEADS), 1.0, 4.0)
    fox_qn = gain((L, HEAD_DIM))
    fox_kn = gain((L, HEAD_DIM))
    fox_on = gain((L, HEAD_DIM))
    ssd_conv_w = nrm((L, SSD_CONV, SSD_CONV_DIM), SSD_CONV ** -0.5)
    ssd_conv_b = nrm((L, SSD_CONV_DIM), 0.02)
    dt0 = jnp.exp(unif((L, SSD_HEADS), float(np.log(1e-3)), float(np.log(1e-1))))
    ssd_dt_bias = dt0 + jnp.log(-jnp.expm1(-dt0))
    ssd_a_log = jnp.log(unif((L, SSD_HEADS), 1.0, 16.0))
    ssd_d = gain((L, SSD_HEADS))
    ssd_norm = gain((L, GROUP_WIDTH))
    gla_w_g2 = nrm((L, GLA_GATE_RANK, GLA_KEY_DIM), GLA_GATE_RANK ** -0.5)
    gla_b_g2 = nrm((L, GLA_KEY_DIM), 0.02)
    gla_norm = gain((L, GLA_HEAD_V))
    hgrn_lb_logits = nrm((L, HGRN_FDIM), 0.5)
    hgrn_norm = gain((L, HGRN_HEAD_V))
    ln_xattn = gain((L, D_MODEL))
    mem_norm = gain((D_MODEL,))
    xa_wq = nrm((L, D_MODEL, D_MODEL), D_MODEL ** -0.5)
    xa_wkv = nrm((L, D_MODEL, 2 * D_MODEL), D_MODEL ** -0.5)
    xa_wo = nrm((L, D_MODEL, D_MODEL), D_MODEL ** -0.5)
    xa_qn = gain((L, XA_HEAD_DIM))
    xa_kn = gain((L, XA_HEAD_DIM))
    ln_ffn = gain((L, D_MODEL))
    ffn_w_up = nrm((L, D_MODEL, 2 * D_FF), D_MODEL ** -0.5)
    ffn_conv_w = nrm((L, FFN_CONV, D_FF), FFN_CONV ** -0.5)
    ffn_conv_b = nrm((L, D_FF), 0.02)
    ffn_w_down = nrm((L, D_FF, D_MODEL), D_FF ** -0.5)
    return {
        'x': x, 'mem': mem, 'ln_mix': ln_mix, 'w_in': w_in, 'w_out': w_out,
        'fox_f_bias': fox_f_bias, 'fox_qn': fox_qn, 'fox_kn': fox_kn, 'fox_on': fox_on,
        'ssd_conv_w': ssd_conv_w, 'ssd_conv_b': ssd_conv_b, 'ssd_dt_bias': ssd_dt_bias,
        'ssd_a_log': ssd_a_log, 'ssd_d': ssd_d, 'ssd_norm': ssd_norm,
        'gla_w_g2': gla_w_g2, 'gla_b_g2': gla_b_g2, 'gla_norm': gla_norm,
        'hgrn_lb_logits': hgrn_lb_logits, 'hgrn_norm': hgrn_norm,
        'ln_xattn': ln_xattn, 'mem_norm': mem_norm, 'xa_wq': xa_wq, 'xa_wkv': xa_wkv,
        'xa_wo': xa_wo, 'xa_qn': xa_qn, 'xa_kn': xa_kn,
        'ln_ffn': ln_ffn, 'ffn_w_up': ffn_w_up, 'ffn_conv_w': ffn_conv_w,
        'ffn_conv_b': ffn_conv_b, 'ffn_w_down': ffn_w_down,
    }

def reference(x, mem, ln_mix, w_in, w_out, fox_f_bias, fox_qn, fox_kn, fox_on,
              ssd_conv_w, ssd_conv_b, ssd_dt_bias, ssd_a_log, ssd_d, ssd_norm,
              gla_w_g2, gla_b_g2, gla_norm, hgrn_lb_logits, hgrn_norm,
              ln_xattn, mem_norm, xa_wq, xa_wkv, xa_wo, xa_qn, xa_kn,
              ln_ffn, ffn_w_up, ffn_conv_w, ffn_conv_b, ffn_w_down):
    mem_n = rms_norm(mem, mem_norm)
    s = jax.nn.softmax(hgrn_lb_logits.astype(jnp.float32), axis=0)
    lower_bounds = jnp.concatenate([jnp.zeros_like(s[:1]), jnp.cumsum(s[1:], axis=0)], axis=0)
    lower_bounds = jnp.clip(lower_bounds, 0.0, 1.0 - 1e-6)
    for l in range(DEPTH):
        h = rms_norm(x, ln_mix[l])
        (fq, fk, fv, ff, sz, sxbc, sdt, gq, gk, gv, ga, gr, hq, hf, hi, hg) = split_columns(h @ w_in[l], IN_SPLITS)
        y_fox = forgetting_attention(fq, fk, fv, ff + fox_f_bias[l], fox_qn[l], fox_kn[l], fox_on[l])
        y_ssd = mamba2_mixer(sz, sxbc, sdt, ssd_conv_w[l], ssd_conv_b[l], ssd_dt_bias[l],
                             ssd_a_log[l], ssd_d[l], ssd_norm[l])
        y_gla = gla_mixer(gq, gk, gv, ga, gr, gla_w_g2[l], gla_b_g2[l], gla_norm[l])
        y_hgrn = hgrn2_mixer(hq, hf, hi, hg, lower_bounds[l], hgrn_norm[l])
        mixed = jnp.concatenate([y_fox.astype(x.dtype), y_ssd.astype(x.dtype),
                                 y_gla.astype(x.dtype), y_hgrn.astype(x.dtype)], axis=-1)
        x = x + mixed @ w_out[l]
        x = x + memory_cross_attention(rms_norm(x, ln_xattn[l]), mem_n, xa_wq[l], xa_wkv[l],
                                       xa_wo[l], xa_qn[l], xa_kn[l])
        x = x + conv_glu_ffn(rms_norm(x, ln_ffn[l]), ffn_w_up[l], ffn_conv_w[l], ffn_conv_b[l], ffn_w_down[l])
    return x


_drawn_inputs = setup_inputs


def setup_inputs(seed=0):
    import zlib

    import numpy as np

    out = dict(_drawn_inputs(seed))
    spreads = {}
    factors = {'fox_qn': 6.85,
     'fox_kn': 7.451,
     'fox_on': 7.083,
     'ssd_conv_b': 5.288,
     'ssd_d': 8.0,
     'ssd_norm': 6.986,
     'gla_b_g2': 8.0,
     'gla_norm': 8.0,
     'hgrn_norm': 8.0,
     'ln_xattn': 8.0,
     'mem_norm': 8.0,
     'xa_qn': 8.0,
     'xa_kn': 8.0,
     'ln_ffn': 5.084,
     'ffn_conv_b': 6.63}
    for name, (base, spread) in spreads.items():
        noise = np.random.default_rng([zlib.crc32(name.encode()), seed]).standard_normal(out[name].shape)
        drawn = base * np.exp(spread * noise) if base else spread * noise
        out[name] = __import__('jax').numpy.asarray(drawn.astype(out[name].dtype))
    for name, factor in factors.items():
        out[name] = (out[name] * factor).astype(out[name].dtype)
    return out
```

```python
from contextlib import ExitStack

import concourse.bass as bass
from concourse import mybir

F32 = mybir.dt.float32
F32R = mybir.dt.float32r
ACT = mybir.ActivationFunctionType
ALU = mybir.AluOpType
AX = mybir.AxisListType

P = 128
D = 1024
T = 1024
KT = D // P
NT = T // P
NW = 512
EPS = 1e-6
LN_EXP = "natural_log_exp_and_others"
N_MEM = 256
XA_HEADS = 4
XA_DIM = D // XA_HEADS
D_FF = 2816
NF = D_FF // P


MIXERS = True


class Phase:

    def __init__(self, nc, name):
        self.nc, self.name, self.sems = nc, name, []
        self.stack, self.inner = ExitStack(), ExitStack()

    def __enter__(self):
        return self

    def sem(self, s):
        one = self.stack.enter_context(self.nc.semaphore(f"{self.name}_{s}"))
        self.sems.append(one)
        return one

    def sb(self, s, shape, dtype=F32):
        return self.stack.enter_context(self.nc.sbuf_tensor(f"{self.name}_{s}", shape, dtype))

    def ps(self, s, shape):
        return self.stack.enter_context(self.nc.psum_tensor(f"{self.name}_{s}", shape, F32))

    def __exit__(self, *error):
        self.inner.__exit__(*error)
        if error[0] is None:
            with self.nc.Block() as block:
                @block.gpsimd
                def _(pool):
                    for one in self.sems:
                        pool.sem_clear(one)
        self.stack.__exit__(*error)


def split_matmuls(pe, out, hi_w, lo_w, hi_x, lo_x, first, last):
    pe.matmul(out, hi_w, hi_x, start=first, stop=False)
    pe.matmul(out, hi_w, lo_x, start=False, stop=False)
    return pe.matmul(out, lo_w, hi_x, start=False, stop=last)


def norm_block(nc, name, cst, XR, HH, HL, ln, tiles, x_dram=None):
    n = len(tiles)
    with Phase(nc, name) as ph, ExitStack() as ctx:
        sem = ph.sem
        LNB = ctx.enter_context(nc.sbuf_tensor(f"{name}_lnb", [P, D], F32))
        XS = ctx.enter_context(nc.sbuf_tensor(f"{name}_xs", [P, 2, D], F32))
        SQ = ctx.enter_context(nc.sbuf_tensor(f"{name}_sq", [P, D], F32))
        SS = ctx.enter_context(nc.sbuf_tensor(f"{name}_ss", [P, n], F32))
        LG = ctx.enter_context(nc.sbuf_tensor(f"{name}_lg", [P, n], F32))
        RS = ctx.enter_context(nc.sbuf_tensor(f"{name}_rs", [P, n], F32))
        tr_bank = [ctx.enter_context(nc.psum_tensor(f"{name}_tr{i}", [P, 4, P], F32)) for i in range(4)]
        ln_loaded = sem("ln_loaded")
        x_loaded = [sem(f"x_loaded{i}") for i in range(n)] if x_dram is not None else None
        squared, logged, rstd_ready, scaled, transposed, hi_ready, lo_ready = (
            sem(s) for s in ("squared", "logged", "rstd", "scaled", "transposed", "hi", "lo"))
        block = ctx.enter_context(nc.Block())

        @block.sync
        def _(sp):
            if x_dram is not None:
                for i, t in enumerate(tiles):
                    sp.dma_start(XR[:, t, :], x_dram[t * P:(t + 1) * P, :]).then_inc(x_loaded[i], 16)
            sp.dma_start(LNB[:], ln.partition_broadcast(P)).then_inc(ln_loaded, 16)

        @block.scalar
        def _(act):
            act.preload_act_table_set(LN_EXP)

            def stats(i):
                if x_dram is not None:
                    act.wait_ge(x_loaded[i], 16)
                act.activation(SQ[:], XR[:, tiles[i], :], ACT.Square, accum_out=SS[:, i:i + 1]).then_inc(squared, 1)
                act.wait_ge(squared, i + 1)
                act.activation(LG[:, i:i + 1], SS[:, i:i + 1], ACT.Ln, scale=1.0 / D,
                               bias=cst["eps"]).then_inc(logged, 1)
                act.wait_ge(logged, i + 1)
                act.activation(RS[:, i:i + 1], LG[:, i:i + 1], ACT.Exp, scale=-0.5).then_inc(rstd_ready, 1)

            stats(0)
            for i in range(n):
                if i + 1 < n:
                    stats(i + 1)
                for g in range(2):
                    u = 2 * i + g
                    act.wait_ge(transposed, u + 1)
                    act.activation(HH[:, 4 * g:4 * g + 4, i * P:(i + 1) * P], tr_bank[u % 4][:], ACT.Copy)\
                       .then_inc(hi_ready, 1)

        @block.vector
        def _(dve):
            def scale(i):
                if i == 0:
                    dve.wait_ge(ln_loaded, 16)
                dve.wait_ge(rstd_ready, i + 1)
                if i >= 2:
                    dve.wait_ge(transposed, 2 * (i - 1))
                dve.scalar_tensor_tensor(XS[:, i % 2, :], XR[:, tiles[i], :], RS[:, i:i + 1], LNB[:],
                                         ALU.mult, ALU.mult).then_inc(scaled, 1)

            scale(0)
            for i in range(n):
                if i + 1 < n:
                    scale(i + 1)
                for g in range(2):
                    u = 2 * i + g
                    dve.wait_ge(hi_ready, u + 1)
                    dve.tensor_tensor(HL[:, 4 * g:4 * g + 4, i * P:(i + 1) * P], tr_bank[u % 4][:],
                                      HH[:, 4 * g:4 * g + 4, i * P:(i + 1) * P], ALU.subtract).then_inc(lo_ready, 1)

        @block.tensor
        def _(pe):
            for i in range(n):
                pe.wait_ge(scaled, i + 1)
                for g in range(2):
                    u = 2 * i + g
                    if u >= 4:
                        pe.wait_ge(lo_ready, u - 3)
                    for k in range(4):
                        c = (4 * g + k) * P
                        last = pe.transpose(tr_bank[u % 4][:, k, :], XS[:, i % 2, c:c + P], cst["ident"])
                    last.then_inc(transposed, 1)


def token_major_product(nc, name, HH, HL, w, n_tok, chunks, evac, presplit=None, extra=None):
    RAW, PART = 4, 3
    steps = [(c, k) for c in range(chunks) for k in range(KT)]
    with Phase(nc, name) as ph, ExitStack() as ctx:
        sem = ph.sem
        WR = ctx.enter_context(nc.sbuf_tensor(f"{name}_wr", [P, RAW, NW], F32))
        WH = ctx.enter_context(nc.sbuf_tensor(f"{name}_wh", [P, PART, NW], F32R))
        WL = ctx.enter_context(nc.sbuf_tensor(f"{name}_wl", [P, PART, NW], F32R))
        bank = [ctx.enter_context(nc.psum_tensor(f"{name}_acc{i}", [P, NW], F32)) for i in range(8)]
        w_loaded = [sem(f"w_loaded{i}") for i in range(RAW)]
        w_hi, w_lo, step_done, bank_done, evacuated, src_hi, src_lo = (
            sem(s) for s in ("w_hi", "w_lo", "step_done", "bank_done", "evacuated", "src_hi", "src_lo"))
        ev = evac(ctx, sem, bank, bank_done, evacuated)
        block = ctx.enter_context(nc.Block())
        per = 8 // n_tok

        def wait_step(eng, s):
            c, k = steps[s]
            if k == KT - 1:
                eng.wait_ge(bank_done, n_tok * (c + 1))
            else:
                eng.wait_ge(step_done, s - c + 1)

        @block.sync
        def _(sp):
            for s, (c, k) in enumerate(steps):
                if s >= RAW:
                    sp.wait_ge(w_lo, s - RAW + 1)
                sp.dma_start(WR[:, s % RAW, :], w[k * P:(k + 1) * P, c * NW:(c + 1) * NW])\
                  .then_inc(w_loaded[s % RAW], 16)
            if "sync" in ev:
                ev["sync"](sp)

        @block.scalar
        def _(act):
            act.preload_act_table_set(LN_EXP)
            if "act_start" in ev:
                ev["act_start"](act)
            for s in range(len(steps)):
                if presplit is not None and s < KT:
                    act.activation(HH[:, s, :], presplit[:, s, :], ACT.Copy).then_inc(src_hi, 1)
                act.wait_ge(w_loaded[s % RAW], 16 * (s // RAW + 1))
                if s >= PART:
                    wait_step(act, s - PART)
                act.activation(WH[:, s % PART, :], WR[:, s % RAW, :], ACT.Copy).then_inc(w_hi, 1)
                if s == KT and "act_load" in ev:
                    if presplit is not None:
                        act.wait_ge(src_lo, KT)
                    ev["act_load"](act)
                if s >= KT + 1 and s % KT == 1 and "act" in ev:
                    ev["act"](act, s // KT - 1)
            if "act" in ev:
                ev["act"](act, chunks - 1)

        @block.vector
        def _(dve):
            if "dve_start" in ev:
                ev["dve_start"](dve)
            for s in range(len(steps)):
                if presplit is not None and s < KT:
                    dve.wait_ge(src_hi, s + 1)
                    dve.tensor_tensor(HL[:, s, :], presplit[:, s, :], HH[:, s, :], ALU.subtract).then_inc(src_lo, 1)
                dve.wait_ge(w_hi, s + 1)
                dve.tensor_tensor(WL[:, s % PART, :], WR[:, s % RAW, :], WH[:, s % PART, :], ALU.subtract)\
                   .then_inc(w_lo, 1)
                if s >= KT + 1 and s % KT == 1 and "dve" in ev:
                    ev["dve"](dve, s // KT - 1)
            if "dve" in ev:
                ev["dve"](dve, chunks - 1)

        @block.tensor
        def _(pe):
            for s, (c, k) in enumerate(steps):
                if presplit is not None and s < KT:
                    pe.wait_ge(src_lo, s + 1)
                pe.wait_ge(w_lo, s + 1)
                for t in range(n_tok):
                    if k == 0 and c >= per:
                        pe.wait_ge(evacuated, n_tok * (c - per) + t + 1)
                    tok = slice(t * P, (t + 1) * P)
                    mm = split_matmuls(pe, bank[(c % per) * n_tok + t][:], HH[:, k, tok], HL[:, k, tok],
                                       WH[:, s % PART, :], WL[:, s % PART, :], k == 0, k == KT - 1)
                    if k == KT - 1:
                        mm.then_inc(bank_done, 1)
                if k < KT - 1:
                    mm.then_inc(step_done, 1)


def residual_evac(XR, x_dram=None):
    def make(ctx, sem, bank, bank_done, evacuated):
        x_loaded = sem("x_loaded")

        def dve(eng, c):
            if x_dram is not None and c == 0:
                eng.wait_ge(x_loaded, 16)
            for t in range(NT):
                eng.wait_ge(bank_done, NT * c + t + 1)
                xs = XR[:, t, c * NW:(c + 1) * NW]
                eng.tensor_tensor(xs, bank[t][:], xs, ALU.add).then_inc(evacuated, 1)

        def act_load(eng):
            if x_dram is not None:
                eng.dma_start(XR[:], x_dram.rearrange("(t p) d -> p t d", p=P)).then_inc(x_loaded, 16)
        return {"dve": dve, "act_load": act_load}
    return make


def head_norm_evac(nc, name, cst, OUT, n_tok, w_norm, scale, norm_chunks, plain=None):
    HPC = NW // XA_DIM

    def make(ctx, sem, bank, bank_done, evacuated):
        n = n_tok * norm_chunks
        WB = ctx.enter_context(nc.sbuf_tensor(f"{name}_wb", [P, XA_DIM], F32))
        WS = ctx.enter_context(nc.sbuf_tensor(f"{name}_ws", [P, XA_DIM], F32))
        SQ = ctx.enter_context(nc.sbuf_tensor(f"{name}_sq", [P, XA_DIM], F32))
        SS = ctx.enter_context(nc.sbuf_tensor(f"{name}_ss", [P, n, HPC], F32))
        LG = ctx.enter_context(nc.sbuf_tensor(f"{name}_lg", [P, n, HPC], F32))
        RS = ctx.enter_context(nc.sbuf_tensor(f"{name}_rs", [P, n, HPC], F32))
        w_loaded, w_scaled, squared, logged, rstd = (sem(s) for s in ("nw", "nws", "sq", "lg", "rs"))

        def act_start(eng):
            eng.dma_start(WB[:], w_norm.partition_broadcast(P)).then_inc(w_loaded, 16)

        def dve_start(eng):
            eng.wait_ge(w_loaded, 16)
            eng.tensor_scalar(WS[:], WB[:], scale, None, ALU.mult).then_inc(w_scaled, 1)
            eng.wait_ge(w_scaled, 1)

        def act(eng, c):
            for t in range(n_tok):
                u = n_tok * c + t
                eng.wait_ge(bank_done, u + 1)
                b = bank[(c % (8 // n_tok)) * n_tok + t]
                if c >= norm_chunks:
                    eng.activation(plain[:, t, (c - norm_chunks) * NW:(c - norm_chunks + 1) * NW], b[:],
                                   ACT.Copy).then_inc(evacuated, 1)
                    continue
                for h in range(HPC):
                    eng.activation(SQ[:], b[:, h * XA_DIM:(h + 1) * XA_DIM], ACT.Square,
                                   accum_out=SS[:, u, h:h + 1]).then_inc(squared, 1)
                    eng.wait_ge(squared, HPC * u + h + 1)
                eng.activation(LG[:, u, :], SS[:, u, :], ACT.Ln, scale=1.0 / XA_DIM, bias=cst["eps"]).then_inc(logged, 1)
                eng.wait_ge(logged, u + 1)
                eng.activation(RS[:, u, :], LG[:, u, :], ACT.Exp, scale=-0.5).then_inc(rstd, 1)

        def dve(eng, c):
            if c >= norm_chunks:
                return
            for t in range(n_tok):
                u = n_tok * c + t
                eng.wait_ge(rstd, u + 1)
                b = bank[(c % (8 // n_tok)) * n_tok + t]
                for h in range(HPC):
                    o = c * NW + h * XA_DIM
                    ins = eng.scalar_tensor_tensor(OUT[:, t, o:o + XA_DIM], b[:, h * XA_DIM:(h + 1) * XA_DIM],
                                                   RS[:, u, h:h + 1], WS[:], ALU.mult, ALU.mult)
                ins.then_inc(evacuated, 1)
        return {"act_start": act_start, "dve_start": dve_start, "act": act, "dve": dve}
    return make


def memory_attention_block(nc, cst, QN, KN, V, OH, OL):
    with Phase(nc, "xa") as ph, ExitStack() as ctx:
        sem = ph.sem
        sb = lambda s, shape: ctx.enter_context(nc.sbuf_tensor(f"xa_{s}", shape, F32))
        KTR = sb("ktr", [P, KT, N_MEM])
        QT = sb("qt", [P, 2, KT, P])
        PR = sb("pr", [P, 2, XA_HEADS, N_MEM])
        PT = sb("pt", [P, 2, 2, XA_HEADS, P])
        NM = sb("nm", [P, NT, XA_HEADS])
        SM = sb("sm", [P, NT, XA_HEADS])
        RI = sb("ri", [P, NT, XA_HEADS])
        ps = lambda s: ctx.enter_context(nc.psum_tensor(f"xa_{s}", [P, 4, P], F32))
        q_bank, s_bank, p_bank, o_bank = ([ps(f"{s}{i}") for i in range(2)] for s in "qspo")
        k_tr, k_ready, q_tr, q_ready, scored, neg_max, expd, inv, normed, p_tr, p_ready, o_done, o_hi, o_lo = (
            sem(s) for s in ("k_tr", "k_ready", "q_tr", "q_ready", "scored", "neg_max", "expd", "inv", "normed",
                             "p_tr", "p_ready", "o_done", "o_hi", "o_lo"))
        block = ctx.enter_context(nc.Block())

        @block.tensor
        def _(pe):
            for u in range(4):
                if u >= 2:
                    pe.wait_ge(k_ready, u - 1)
                for j in range(4):
                    last = pe.transpose(q_bank[u % 2][:, j, :], KN[:, u // 2, ((u % 2) * 4 + j) * P:((u % 2) * 4 + j + 1) * P],
                                        cst["ident"])
                last.then_inc(k_tr, 1)

            def queries(i):
                for g in range(2):
                    if i == 0:
                        pe.wait_ge(k_ready, 3 + g)
                    else:
                        pe.wait_ge(q_ready, 2 * (i - 1) + g + 1)
                    for j in range(4):
                        c = (4 * g + j) * P
                        last = pe.transpose(q_bank[g][:, j, :], QN[:, i, c:c + P], cst["ident"])
                    last.then_inc(q_tr, 1)

            def scores(i):
                pe.wait_ge(q_ready, 2 * i + 2)
                for g in range(2):
                    if i >= 1:
                        pe.wait_ge(expd, 4 * (i - 1) + 2 * g + 2)
                    for hh in range(2):
                        h = 2 * g + hh
                        for kk in range(2):
                            mm = pe.matmul(s_bank[g][:].rearrange("p a b -> p (a b)")[:, hh * N_MEM:(hh + 1) * N_MEM],
                                           QT[:, i % 2, 2 * h + kk, :], KTR[:, 2 * h + kk, :],
                                           start=(kk == 0), stop=(kk == 1))
                    mm.then_inc(scored, 1)

            def outputs(i):
                pe.wait_ge(normed, i + 1)
                for m in range(2):
                    if i >= 1:
                        pe.wait_ge(p_ready, 2 * (i - 1) + m + 1)
                    for h in range(XA_HEADS):
                        last = pe.transpose(p_bank[m][:, h, :], PR[:, i % 2, h, m * P:(m + 1) * P], cst["ident"])
                    last.then_inc(p_tr, 1)
                pe.wait_ge(p_ready, 2 * i + 2)
                for g in range(2):
                    if i >= 1:
                        pe.wait_ge(o_lo, 2 * (i - 1) + g + 1)
                    for j in range(4):
                        d = 4 * g + j
                        for m in range(2):
                            mm = pe.matmul(o_bank[g][:, j, :], V[:, m, d * P:(d + 1) * P], PT[:, i % 2, m, d // 2, :],
                                           start=(m == 0), stop=(m == 1))
                    mm.then_inc(o_done, 1)

            queries(0)
            for i in range(NT):
                scores(i)
                if i + 1 < NT:
                    queries(i + 1)
                if i >= 1:
                    outputs(i - 1)
            outputs(NT - 1)

        @block.scalar
        def _(act):
            for u in range(4):
                act.wait_ge(k_tr, u + 1)
                act.activation(KTR[:, (u % 2) * 4:(u % 2) * 4 + 4, (u // 2) * P:(u // 2 + 1) * P], q_bank[u % 2][:],
                               ACT.Copy).then_inc(k_ready, 1)

            def queries(i):
                for g in range(2):
                    act.wait_ge(q_tr, 2 * i + g + 1)
                    if i >= 2:
                        act.wait_ge(scored, 2 * (i - 1))
                    act.activation(QT[:, i % 2, 4 * g:4 * g + 4, :], q_bank[g][:], ACT.Copy).then_inc(q_ready, 1)

            def exps(i):
                for g in range(2):
                    act.wait_ge(neg_max, 2 * i + g + 1)
                    if i >= 2:
                        act.wait_ge(p_tr, 2 * (i - 1))
                    for hh in range(2):
                        h = 2 * g + hh
                        act.activation(PR[:, i % 2, h, :], s_bank[g][:].rearrange("p a b -> p (a b)")[:, hh * N_MEM:(hh + 1) * N_MEM],
                                       ACT.Exp, bias=NM[:, i, h:h + 1], accum_out=SM[:, i, h:h + 1]).then_inc(expd, 1)

            def out_hi(i):
                for g in range(2):
                    act.wait_ge(o_done, 2 * i + g + 1)
                    act.activation(OH[:, 4 * g:4 * g + 4, i * P:(i + 1) * P], o_bank[g][:], ACT.Copy).then_inc(o_hi, 1)

            queries(0)
            for i in range(NT):
                exps(i)
                if i + 1 < NT:
                    queries(i + 1)
                if i >= 1:
                    out_hi(i - 1)
            out_hi(NT - 1)

        @block.vector
        def _(dve):
            def softmax(i):
                for g in range(2):
                    dve.wait_ge(scored, 2 * i + g + 1)
                    dve.tensor_reduce(NM[:, i, 2 * g:2 * g + 2],
                                      s_bank[g][:].rearrange("p (h a) b -> p h (a b)", h=2), AX.X, ALU.max,
                                      negate=True).then_inc(neg_max, 1)
                dve.wait_ge(expd, 4 * i + 4)
                dve.reciprocal(RI[:, i, :], SM[:, i, :]).then_inc(inv, 1)
                dve.wait_ge(inv, i + 1)
                for h in range(XA_HEADS):
                    ins = dve.tensor_scalar(PR[:, i % 2, h, :], PR[:, i % 2, h, :], RI[:, i, h:h + 1], None, ALU.mult)
                ins.then_inc(normed, 1)

            def out(i):
                for m in range(2):
                    dve.wait_ge(p_tr, 2 * i + m + 1)
                    if i >= 2:
                        dve.wait_ge(o_done, 2 * (i - 1))
                    dve.tensor_copy(PT[:, i % 2, m, :, :], p_bank[m][:]).then_inc(p_ready, 1)
                for g in range(2):
                    dve.wait_ge(o_hi, 2 * i + g + 1)
                    o = (slice(None), slice(4 * g, 4 * g + 4), slice(i * P, (i + 1) * P))
                    dve.tensor_tensor(OL[o], o_bank[g][:], OH[o], ALU.subtract).then_inc(o_lo, 1)

            for i in range(NT):
                softmax(i)
                if i >= 1:
                    out(i - 1)
            out(NT - 1)


def ffn_block(nc, u, cst, XR, HH, HL, HALO, CW, CB, w_up, w_down, out, stored):
    RAW, PART = 4, 3
    HT = T // 2
    NTH = HT // P
    UP = 2 * NF
    ITEMS = UP + 2 * NF
    with Phase(nc, f"ff{u}") as ph, ExitStack() as ctx:
        sem = ph.sem
        WR = ctx.enter_context(nc.sbuf_tensor(f"ff{u}_wr", [P, RAW, KT, P], F32))
        WH = ctx.enter_context(nc.sbuf_tensor(f"ff{u}_wh", [P, PART, KT, P], F32R))
        WL = ctx.enter_context(nc.sbuf_tensor(f"ff{u}_wl", [P, PART, KT, P], F32R))
        AH = ctx.enter_context(nc.sbuf_tensor(f"ff{u}_ah", [P, NF, HT], F32R))
        AL = ctx.enter_context(nc.sbuf_tensor(f"ff{u}_al", [P, NF, HT], F32R))
        G = ctx.enter_context(nc.sbuf_tensor(f"ff{u}_g", [P, HT + 2], F32))
        Y = ctx.enter_context(nc.sbuf_tensor(f"ff{u}_y", [P, 2, HT], F32))
        TH = ctx.enter_context(nc.sbuf_tensor(f"ff{u}_th", [P, HT], F32))
        AF = ctx.enter_context(nc.sbuf_tensor(f"ff{u}_af", [P, HT], F32))
        bank = [ctx.enter_context(nc.psum_tensor(f"ff{u}_b{i}", [P, NW], F32)) for i in range(8)]
        w_loaded = [sem(f"w_loaded{i}") for i in range(RAW)]
        w_hi, w_lo, item_done, g_copied, g_scaled, halo_set, conv, tanh_ready, gated, act_f, act_hi, act_lo, evac = (
            sem(s) for s in ("w_hi", "w_lo", "item_done", "g_copied", "g_scaled", "halo", "conv", "tanh", "gated",
                             "act_f", "act_hi", "act_lo", "evac"))
        block = ctx.enter_context(nc.Block())

        def part(buf, ring, n):
            if n < UP:
                return buf[:, n % ring, :, :]
            return buf[:, n % ring, 0:NW // P, :]

        @block.sync
        def _(sp):
            for n in range(ITEMS):
                if n >= RAW:
                    sp.wait_ge(w_lo, n - RAW + 1)
                if n < UP:
                    col = (n % 2) * D_FF + (n // 2) * P
                    src = w_up[:, col:col + P].rearrange("(k p) c -> p k c", p=P)
                else:
                    c, k = divmod(n - UP, NF)
                    src = w_down[k * P:(k + 1) * P, c * NW:(c + 1) * NW].rearrange("p (a b) -> p a b", b=P)
                sp.dma_start(part(WR, RAW, n), src).then_inc(w_loaded[n % RAW], 16)
            for c in range(2):
                for t in range(NTH):
                    row = (u * NTH + t) * P
                    sp.wait_ge(evac, c * NTH + t + 1)
                    sp.dma_start(out[row:row + P, c * NW:(c + 1) * NW], XR[:, u * NTH + t, c * NW:(c + 1) * NW])\
                      .then_inc(stored, 16)
            sp.wait_ge(stored, 16 * 2 * NTH * (u + 1))

        def hi(act, n):
            if n >= ITEMS:
                return
            act.wait_ge(w_loaded[n % RAW], 16 * (n // RAW + 1))
            if n >= PART:
                act.wait_ge(item_done, n - PART + 1)
            act.activation(part(WH, PART, n), part(WR, RAW, n), ACT.Copy).then_inc(w_hi, 1)

        def lo(dve, n):
            if n >= ITEMS:
                return
            dve.wait_ge(w_hi, n + 1)
            dve.tensor_tensor(part(WL, PART, n), part(WR, RAW, n), part(WH, PART, n), ALU.subtract).then_inc(w_lo, 1)

        @block.scalar
        def _(act):
            hi(act, 0)
            hi(act, 1)
            for f in range(NF + 1):
                hi(act, 2 * f + 2)
                if f >= 1:
                    g = f - 1
                    act.wait_ge(item_done, 2 * g + 1)
                    if g >= 1:
                        act.wait_ge(conv, 2 * g)
                        act.wait_ge(halo_set, 2 * g)
                    act.activation(G[:, 2:HT + 2], bank[(2 * g) % 4][:], ACT.Copy).then_inc(g_copied, 1)
                    if g >= 2:
                        act.wait_ge(gated, g - 1)
                    act.activation(Y[:, g % 2, :], bank[(2 * g) % 4][:], ACT.Identity, scale=CW[:, g, 2:3],
                                   bias=CB[:, g:g + 1]).then_inc(g_scaled, 1)
                hi(act, 2 * f + 3)
                if f >= 1:
                    act.wait_ge(conv, 2 * g + 2)
                    if g >= 1:
                        act.wait_ge(gated, g)
                    act.activation(TH[:], Y[:, g % 2, :], ACT.Tanh, scale=0.5).then_inc(tanh_ready, 1)
                    act.wait_ge(act_f, g + 1)
                    act.activation(AH[:, g, :], AF[:], ACT.Copy).then_inc(act_hi, 1)
            for n in range(2 * NF + 4, ITEMS):
                hi(act, n)

        @block.vector
        def _(dve):
            lo(dve, 0)
            lo(dve, 1)
            for f in range(NF + 1):
                lo(dve, 2 * f + 2)
                if f >= 1:
                    g = f - 1
                    if u == 0 and g == 0:
                        dve.memset(G[:, 0:2], 0.0).then_inc(halo_set, 1)
                    elif u == 0:
                        dve.nop().then_inc(halo_set, 1)
                    else:
                        if g >= 1:
                            dve.wait_ge(conv, 2 * g)
                        dve.tensor_copy(G[:, 0:2], HALO[:, g, :]).then_inc(halo_set, 1)
                    dve.wait_ge(halo_set, 2 * g + 1)
                    dve.wait_ge(g_copied, g + 1)
                    dve.wait_ge(g_scaled, g + 1)
                    y = Y[:, g % 2, :]
                    dve.scalar_tensor_tensor(y, G[:, 1:HT + 1], CW[:, g, 1:2], y, ALU.mult, ALU.add).then_inc(conv, 1)
                    dve.wait_ge(conv, 2 * g + 1)
                    dve.scalar_tensor_tensor(y, G[:, 0:HT], CW[:, g, 0:1], y, ALU.mult, ALU.add).then_inc(conv, 1)
                    if u == 0:
                        dve.tensor_copy(HALO[:, g, :], G[:, HT:HT + 2]).then_inc(halo_set, 1)
                    else:
                        dve.nop().then_inc(halo_set, 1)
                lo(dve, 2 * f + 3)
                if f >= 1:
                    dve.wait_ge(tanh_ready, g + 1)
                    dve.scalar_tensor_tensor(y, TH[:], 1.0, y, ALU.add, ALU.mult).then_inc(gated, 1)
                    dve.wait_ge(gated, g + 1)
                    dve.wait_ge(item_done, 2 * g + 2)
                    dve.scalar_tensor_tensor(AF[:], y, 0.5, bank[(2 * g + 1) % 4][:], ALU.mult, ALU.mult)\
                       .then_inc(act_f, 1)
                    dve.wait_ge(act_f, g + 1)
                    dve.wait_ge(act_hi, g + 1)
                    dve.tensor_tensor(AL[:, g, :], AF[:], AH[:, g, :], ALU.subtract).then_inc(act_lo, 1)

            def residual(c):
                dve.wait_ge(item_done, UP + NF * (c + 1))
                for t in range(NTH):
                    xs = XR[:, u * NTH + t, c * NW:(c + 1) * NW]
                    dve.tensor_tensor(xs, bank[4 * (1 - c) + t][:], xs, ALU.add).then_inc(evac, 1)

            for n in range(2 * NF + 4, ITEMS):
                lo(dve, n)
                if n == UP + NF + 1:
                    residual(0)
            residual(1)

        @block.tensor
        def _(pe):
            for n in range(UP):
                pe.wait_ge(w_lo, n + 1)
                if n >= 4:
                    pe.wait_ge(act_f if n % 2 else g_scaled, (n - 4) // 2 + 1)
                for k in range(KT):
                    mm = split_matmuls(pe, bank[n % 4][:], WH[:, n % PART, k, :], WL[:, n % PART, k, :],
                                       HH[:, k, :], HL[:, k, :], k == 0, k == KT - 1)
                mm.then_inc(item_done, 1)
            for n in range(UP, ITEMS):
                c, k = divmod(n - UP, NF)
                pe.wait_ge(w_lo, n + 1)
                if c == 0:
                    pe.wait_ge(act_lo, k + 1)
                for t in range(NTH):
                    tok = slice(t * P, (t + 1) * P)
                    mm = split_matmuls(pe, bank[4 * (1 - c) + t][:], AH[:, k, tok], AL[:, k, tok],
                                       part(WH, PART, n).rearrange("p a b -> p (a b)"),
                                       part(WL, PART, n).rearrange("p a b -> p (a b)"), k == 0, k == NF - 1)
                mm.then_inc(item_done, 1)


NEG = -1e30
N_PAR = 7 + 4 + 10 + 4

OFF_FOX, OFF_FF = 0, 768
OFF_SZ, OFF_SX, OFF_DT = 772, 1028, 1540
OFF_GQ, OFF_GV, OFF_GA, OFF_GR = 1544, 1800, 2056, 2072
OFF_HQ = 2328
FOX_ITEMS = [OFF_FOX + P * j for j in range(6)]
SSD_ITEMS = [OFF_SZ + P * j for j in range(2)] + [OFF_SX + P * j for j in range(4)]
GLA_ITEMS = [OFF_GQ + P * j for j in range(4)] + [OFF_GR + P * j for j in range(2)]
HGRN_ITEMS = [OFF_HQ + P * j for j in range(8)]
COLS = [None] + HGRN_ITEMS + FOX_ITEMS + SSD_ITEMS + GLA_ITEMS
N_ITEMS = len(COLS)
H0, F0, S0, G0 = 1, 9, 15, 21
PAD = 4
SW = PAD + T
SMALL, W1, A, B = 0, 1, 2, 8
MX0 = 16
SLOT_OF = [SMALL] + [B + j for j in range(8)] + [MX0 + j for j in range(6)] + [B + j for j in range(6)] + [A + j for j in range(6)]
DT_ROW, GA_ROW = 32, 64
CH_GLA, CH_HGRN = 64, 16


def spread(first, last, counts):
    out, m = [], first
    for c in counts:
        out.append((m, m + c))
        m += c
    assert m == last
    return out


_HG = spread(2 * F0, 2 * S0, [2, 2, 2, 2] + [1, 1, 1, 1, 0, 0, 0, 0])
HG_PREP, HG_TILE = _HG[:4], _HG[4:]
_FX = spread(2 * S0, 2 * G0, [2, 2] + [1 if n in (3, 7, 11, 15, 19, 23, 27, 31) else 0 for n in range(33)])
FOX_PRE, FOX_UNIT = _FX[:2], _FX[2:]
_SD = spread(2 * G0, 2 * N_ITEMS, [2, 1, 1, 0] + [1] * 8)
SSD_CONV, SSD_CHUNK = _SD[:4], _SD[4:]


def mixers_block(nc, cst, a, MX, HH, HL):
    RAW, PART = 2, 2
    ident, eps, one = cst["ident"], cst["eps"], cst["one"]
    with Phase(nc, "mix") as ph:
        sem, sb = ph.sem, ph.sb
        SL = sb("slots", [P, 16, SW])
        WR = sb("wr", [P, RAW, KT, P])
        WH = sb("wh", [P, PART, KT, P], F32R)
        WL = sb("wl", [P, PART, KT, P], F32R)
        R10 = sb("scratch", [P, 2560])
        ST = sb("st", [P, NT, 3, 36])
        NEGQ = sb("negq", [P, P])
        NEGK = sb("negk", [P, P])
        M64 = sb("m64", [P, P])
        M16 = sb("m16", [P, P])
        BM = sb("bm", [P, 4, 64])
        BO64 = sb("bo64", [P, P])
        BO128 = sb("bo128", [P, P])
        HM4 = sb("hm4", [P, 4])
        HM2 = sb("hm2", [P, 2])
        CM8 = sb("cm8", [P, 8])
        PB = sb("pb", [P, 3])
        NWT = sb("nwt", [P, 8])
        CWS = sb("cws", [P, 4, 4])
        CBS = sb("cbs", [P, 4])
        DSK = sb("dsk", [P, 2])
        WG2 = sb("wg2", [P, P])
        BG2 = sb("bg2", [P, 1])
        NM = sb("nm", [P, 32])
        SUM = sb("sum", [P, 32])
        RIN = sb("rin", [P, 32])
        BT = sb("bt", [P, P])
        S_SSD = sb("s_ssd", [P, 4, 64])
        ED = sb("ed", [P, 2, 64])
        gb = [ph.ps(f"gb{i}", [P, NW]) for i in range(2)]
        M = [ph.ps(f"m{i}", [P, NW]) for i in range(6)]
        M3 = [m[:].rearrange("p (a b) -> p a b", b=P) for m in M]

        data = lambda s: SL[:, s, PAD:SW] if s < MX0 else MX[:, s - MX0, :]
        tile = lambda s, i: data(s)[:, i * P:(i + 1) * P]

        w_loaded = [sem(f"w_loaded{i}") for i in range(RAW)]
        made = {}

        def E(s):
            if s not in made:
                made[s] = sem(s)
            return made[s]

        def own(eng, s):
            count = [0]

            def link(ins):
                count[0] += 1
                ins.then_inc(E(s), 1)
                eng.wait_ge(E(s), count[0])
            return link

        half = lambda ap, h: ap[:, h * NW:(h + 1) * NW]
        mx = lambda t: MX[:, t, :]
        VT = SL[:, A:A + 2, :].rearrange("p a b -> p (a b)")[:, 0:2 * T].rearrange("p (t c) -> p t c", c=256)
        SC = [data(A + 2), data(A + 3), data(A + 4)]
        CB = [data(A + 5), data(W1)]
        FQ, FK, FV = MX0, MX0 + 2, MX0 + 4
        PTS = [R10[:, NW * i:NW * (i + 1)] for i in range(3)]
        FOX_UNITS = [(hp, i, hh) for hp in range(2) for i in range(NT) for hh in range(2)]
        PIECES = [(n, c) for n, (hp, i, hh) in enumerate(FOX_UNITS) for c in range((i * P + P + NW - 1) // NW)]
        GROUPS = [(n, g) for n, (hp, i, hh) in enumerate(FOX_UNITS) for g in range(i // 4 + 1)]
        piece_of, group_of = {u: m for m, u in enumerate(PIECES)}, {u: m for m, u in enumerate(GROUPS)}
        scr = MX[:, 4:6, :].rearrange("p a b -> p (a b)")
        D_, SCD, EA = scr[:, 0:512], [scr[:, 512:1024], scr[:, 1024:1536]], scr[:, 1536:2048]
        CA, XDT, XDTE = data(W1)[:, 0:512], data(W1)[:, 512:768], data(W1)[:, 768:1024]
        CMC = [R10[:, 256 * i:256 * i + 256].rearrange("p (g t) -> p g t", g=2) for i in range(2)]
        QX = R10[:, 0:512].rearrange("p (h t) -> p h t", h=4)
        ATT = [R10[:, 512 + 512 * i:1024 + 512 * i].rearrange("p (h t) -> p h t", h=4) for i in range(2)]
        VK = [R10[:, 1536 + 512 * i:2048 + 512 * i].rearrange("p (a c) -> p a c", c=P) for i in range(2)]
        S_GLA = S_SSD[:].rearrange("p a b -> p (a b)")
        work = SL[:, W1:W1 + 5, :].rearrange("p a b -> p (a b)")
        VX = work[:, 0:2048].rearrange("p (h c d) -> p h c d", h=4, c=8)
        S_HG = work[:, 2048:2048 + 2304].rearrange("p (q c e) -> p q c e", q=2, c=9)
        UNITS = []

        def units(places, w, ones, sq, rs):
            for t, col in zip(places, w):
                UNITS.extend((half(data(t), h), col, ones, half(data(sq), h), half(data(rs), h)) for h in range(2))
        units((MX0 + 6, MX0 + 7), (6, 6), BO64, A + 4, A + 5)
        units((FQ, FQ + 1, FK, FK + 1), (0, 0, 1, 1), BO64, B + 6, B + 7)
        units((MX0, MX0 + 1), (2, 2), BO64, B + 6, B + 7)
        units((MX0 + 2, MX0 + 3), (3, 4), BO128, B + 6, B + 7)
        units((MX0 + 4, MX0 + 5), (5, 5), BO64, B + 6, B + 7)
        block = ph.inner.enter_context(nc.Block())

        @block.sync
        def _(sp):
            w = a["w_in"][0]
            narrow = ((0, OFF_FF, 4), (DT_ROW, OFF_DT, 4), (GA_ROW, OFF_GA, 16))
            sp.wait_ge(E("zeroed"), 1)
            with nc.allow_non_contiguous_dma(reason="narrow column groups and parameter columns"):
                for row, off, n in narrow:
                    sp.dma_start(WR[:, 0, :, row:row + n], w[:, off:off + n].rearrange("(k p) c -> p k c", p=P))\
                      .then_inc(w_loaded[0], 16)
                for n in range(1, RAW):
                    sp.dma_start(WR[:, n, :, :], w[:, COLS[n]:COLS[n] + P].rearrange("(k p) c -> p k c", p=P))\
                      .then_inc(w_loaded[n], 16)
                col = lambda v: v.rearrange("(p o) -> p o", o=1)
                par = [(PB[0:4, 1:2], col(a["fox_f_bias"][0])), (PB[DT_ROW:DT_ROW + 4, 1:2], col(a["ssd_dt_bias"][0])),
                       (PB[DT_ROW:DT_ROW + 4, 2:3], col(a["ssd_a_log"][0])),
                       (WG2[GA_ROW:GA_ROW + 16, :], a["gla_w_g2"][0]), (BG2[:], col(a["gla_b_g2"][0])),
                       (CBS[:], a["ssd_conv_b"][0].rearrange("(t p) -> p t", p=P)),
                       (NWT[:, 3:5], a["ssd_norm"][0].rearrange("(t p) -> p t", p=P))]
                par += [(CWS[:, :, j], a["ssd_conv_w"][0, j].rearrange("(t p) -> p t", p=P)) for j in range(4)]
                for b in range(2):
                    par += [(NWT[64 * b:64 * b + 64, c:c + 1], col(a[k][0])) for c, k in
                            ((0, "fox_qn"), (1, "fox_kn"), (2, "fox_on"), (5, "gla_norm"), (6, "hgrn_norm"))]
                for h in range(4):
                    par.append((DSK[64 * (h % 2):64 * (h % 2) + 64, h // 2:h // 2 + 1],
                                a["ssd_d"][0, h:h + 1].rearrange("(p o) -> p o", o=1).to_broadcast([64, 1])))
                for dst, src in par:
                    sp.dma_start(dst, src).then_inc(E("params"), 16)
                assert len(par) == N_PAR
            for n in range(RAW, N_ITEMS):
                sp.wait_ge(E("g_lo"), n - RAW + 1)
                sp.dma_start(WR[:, n % RAW, :, :], w[:, COLS[n]:COLS[n] + P].rearrange("(k p) c -> p k c", p=P))\
                  .then_inc(w_loaded[n % RAW], 16)

        @block.gpsimd
        def _(pool):
            link = own(pool, "pool_own")
            link(pool.memset(WR[:, 0, :, :], 0.0))
            link(pool.memset(PB[:], 1.0))
            link(pool.memset(PB[:, 1:2], 0.0))
            link(pool.memset(PB[DT_ROW:64, 0:1], -1.0))
            pool.memset(WG2[:], 0.0).then_inc(E("zeroed"), 1)
            pool.memset(SL[:, :, 0:PAD], 0.0).then_inc(E("pads"), 1)
            pool.wait_ge(E("pads"), 1)
            pool.wait_ge(E("zeroed"), 1)
            link(pool.memset(MX[0:64, 5, :], 1.0))
            pool.memset(MX[DT_ROW:64, 5, 0:T:P], 0.0).then_inc(E("restart"), 1)
            pool.wait_ge(E("restart"), 1)
            for m, v in ((NEGQ, 0.0), (NEGK, 0.0), (M64, 1.0), (M16, 1.0), (BM, 1.0), (BO64, 1.0 / 64), (HM4, 1.0),
                         (HM2, 1.0), (CM8, 1.0)):
                link(pool.memset(m[:], v))
            link(pool.memset(BO128[:], 1.0 / P))

            def keep(m, cond, base, pattern, mult, fill=0.0):
                link(pool.affine_select(out=m, in_=m, compare_op=cond, fill=fill, base=base, pattern=pattern,
                                        channel_multiplier=mult))
            keep(NEGQ[:], ALU.is_ge, 0, [[-1, P]], 1, NEG)
            keep(NEGK[:], ALU.is_ge, 0, [[1, P]], -1, NEG)
            for m, ch in ((M64, CH_GLA), (M16, CH_HGRN)):
                v = m[:].rearrange("p (c i) -> p c i", i=ch)
                keep(m[:], ALU.is_ge, 0, [[1, P]], -1)
                keep(v, ALU.is_ge, 0, [[-ch, P // ch], [0, ch]], 1)
            for m, n in ((BM, 4), (BO64, 2)):
                w = P // n
                v = m[:] if m is BM else m[:].rearrange("p (h d) -> p h d", h=n)
                keep(v, ALU.is_ge, 0, [[-w, n], [0, 64]], 1)
                keep(v, ALU.is_ge, w - 1, [[w, n], [0, 64]], -1)
            for m, n in ((HM4, 4), (HM2, 2), (CM8, 8)):
                w = P // n
                keep(m[:], ALU.is_ge, 0, [[-w, n]], 1)
                keep(m[:], ALU.is_ge, w - 1, [[w, n]], -1)
            pool.memset(S_SSD[:], 0.0).then_inc(E("masks"), 1)
            pool.memset(R10[:, 512:1536], 0.0).then_inc(E("att_zero"), 1)
            pool.wait_ge(E("h_prep"), 2)
            pool.memset(work[:, 2048:2048 + 2304], 0.0).then_inc(E("s_zero"), 1)
            for i in range(NT):
                if i >= 1:
                    pool.wait_ge(E("h_att"), i)
                for p in range(2):
                    pool.tensor_tensor(QX[:, 2 * p:2 * p + 2, :], tile(B + p, i).unsqueeze(1).to_broadcast([P, 2, P]),
                                       HM2[:].unsqueeze(2).to_broadcast([P, 2, P]), ALU.mult).then_inc(E("h_qx"), 1)
                pool.wait_ge(E("h_vk"), i + 1)
                for h in range(4):
                    if i >= 1:
                        pool.wait_ge(E("h_ds"), 4 * (i - 1) + h + 1)
                    v = VK[i % 2][:, h // 2, 64 * (h % 2):64 * (h % 2) + 64]
                    pool.tensor_tensor(VX[:, h, :, :], v.unsqueeze(1).to_broadcast([P, 8, 64]),
                                       CM8[:].unsqueeze(2).to_broadcast([P, 8, 64]), ALU.mult).then_inc(E("h_vx"), 1)
            pool.wait_ge(E("mixed"), 2)
            link(pool.memset(R10[:, 0:512], 0.0))
            pool.wait_ge(E("conv_out"), 4)
            for c in range(NT):
                if c >= 2:
                    pool.wait_ge(E("s_g"), c - 1)
                for g in range(2):
                    q = slice(64 * g, 64 * g + 64)
                    pool.tensor_copy(CMC[c % 2][q, g, :], tile(B + 5, c)[q, :]).then_inc(E("cmc"), 1)
                    pool.wait_ge(E("cmc"), 2 * c + g + 1)
            pool.wait_ge(E("mixed"), 3)
            pool.memset(R10[:, 512:1536], 0.0).then_inc(E("att_zero"), 1)
            pool.wait_ge(E("gla_q"), 1)
            for i in range(NT):
                if i >= 1:
                    pool.wait_ge(E("a_att"), i)
                pool.tensor_tensor(QX, tile(A, i).unsqueeze(1).to_broadcast([P, 4, P]),
                                   HM4[:].unsqueeze(2).to_broadcast([P, 4, P]), ALU.mult).then_inc(E("a_qx"), 1)

        @block.scalar
        def _(act):
            link = own(act, "act_own")
            act.preload_act_table_set(LN_EXP)

            def hi(n):
                if n >= N_ITEMS:
                    return
                act.wait_ge(w_loaded[n % RAW], 16 * (n // RAW + (3 if n % RAW == 0 else 1)))
                if n >= PART:
                    act.wait_ge(E("g_mm"), 2 * (n - PART) + 2)
                act.activation(WH[:, n % PART, :, :], WR[:, n % RAW, :, :], ACT.Copy).then_inc(E("g_hi"), 1)

            next_out = [0]

            def copy_out(upto):
                while next_out[0] < upto:
                    n, h = divmod(next_out[0], 2)
                    if h == 0 and n in (S0, G0):
                        act.wait_ge(E("mixed"), 1 if n == S0 else 2)
                    act.wait_ge(E("g_mm"), 2 * n + h + 1)
                    act.activation(half(data(SLOT_OF[n]), h), gb[h][:], ACT.Copy).then_inc(E("g_ev"), 1)
                    next_out[0] += 1

            def halves(m0, m1):
                for m in range(m0, m1):
                    copy_out(m)
                    if m % 2 == 0:
                        hi(m // 2 + 1)

            def items(n0, n1):
                halves(2 * n0, 2 * n1)
                copy_out(2 * n1)

            def squares(u):
                src, _, _, sq, _ = UNITS[u]
                if u >= 2:
                    act.wait_ge(E("n_ms"), u - 1)
                act.activation(sq, src, ACT.Square).then_inc(E("n_sq"), 1)

            def norms(u0, u1):
                if u0 != 12:
                    act.preload_act_table_set(LN_EXP)
                squares(u0)
                for u in range(u0, u1):
                    if u + 1 < u1:
                        squares(u + 1)
                    act.wait_ge(E("n_ms"), u + 1)
                    if u >= 2:
                        act.wait_ge(E("n_out"), u - 1)
                    rs = UNITS[u][4]
                    act.activation(rs, M[4 + u % 2][:], ACT.Ln, bias=eps).then_inc(E("n_ln"), 1)
                    act.wait_ge(E("n_ln"), u + 1)
                    act.activation(rs, rs, ACT.Exp, scale=-0.5).then_inc(E("n_rs"), 1)

            hi(0)
            items(0, 1)
            act.wait_ge(E("params"), 16 * N_PAR)
            act.activation(PB[DT_ROW:DT_ROW + 4, 2:3], PB[DT_ROW:DT_ROW + 4, 2:3], ACT.Exp).then_inc(E("sm_a"), 1)
            act.wait_ge(E("sm_abs"), 1)
            link(act.activation(MX[0:64, 6, :], MX[0:64, 4, :], ACT.Exp, scale=-1.0))
            act.activation(MX[0:64, 6, :], MX[0:64, 6, :], ACT.Ln, bias=one[0:64, :]).then_inc(E("sm_ln"), 1)
            act.wait_ge(E("sm_te"), 1)
            act.activation(MX[0:64, 4, :], MX[0:64, 4, :], ACT.Exp).then_inc(E("sm_we"), 1)
            for i in range(NT):
                act.wait_ge(E("st_tr"), i + 1)
                act.activation(ST[:, i, :, :], M3[i % 2][:, 0:3, 0:36], ACT.Copy).then_inc(E("st_ev"), 1)

            def gate(k, z, th):
                act.activation(th, z, ACT.Tanh, scale=0.5).then_inc(E("gate_th"), 1)

            items(H0, F0)
            a0, a1, a2 = data(A), data(A + 1), data(A + 2)
            act.preload_act_table_set(LN_EXP)
            for p in range(2):
                halves(*HG_PREP[2 * p])
                act.wait_ge(E("hg_abs"), p + 1)
                link(act.activation(a0, a0, ACT.Exp, scale=-1.0))
                act.activation(a0, a0, ACT.Ln, bias=one).then_inc(E("hg_ln"), 1)
                act.wait_ge(E("hg_cum"), p + 1)
                act.activation(data(B + 2 + p), data(B + 2 + p), ACT.Exp).then_inc(E("hg_k"), 1)
                act.activation(a0, a2, ACT.Exp).then_inc(E("hg_e1"), 1)
                halves(*HG_PREP[2 * p + 1])
                act.wait_ge(E("hg_q"), p + 1)
                act.activation(a0, a2, ACT.Exp, scale=-1.0).then_inc(E("hg_e2"), 1)
                act.wait_ge(E("hg_te"), p + 1)
                act.activation(a2, a2, ACT.Exp).then_inc(E("hg_e3"), 1)
            for i in range(NT):
                act.wait_ge(E("h_tr"), i + 1)
                if i >= 2:
                    act.wait_ge(E("h_y"), i - 1)
                act.activation(VK[i % 2], M3[0], ACT.Copy).then_inc(E("h_vk"), 1)
                if i >= 1:
                    halves(*HG_TILE[i - 1])
                    act.wait_ge(E("h_y"), i)
                    act.activation(MX[:, 6:8, (i - 1) * P:i * P], M3[0][:, 0:2, :], ACT.Copy)\
                       .then_inc(E("h_yev"), 1)
            halves(*HG_TILE[NT - 1])
            act.wait_ge(E("h_y"), NT)
            link(act.activation(MX[:, 6:8, (NT - 1) * P:], M3[0][:, 0:2, :], ACT.Copy))
            copy_out(2 * S0)
            act.wait_ge(E("h_s"), 32 * NT)
            norms(0, 4)
            act.wait_ge(E("n_out"), 4)
            for p in range(2):
                gate(p, data(B + 6 + p), data(A + p))

            act.wait_ge(E("mixed"), 1)
            halves(*FOX_PRE[0])
            for i in range(NT):
                act.wait_ge(E("vt_tr"), i + 1)
                act.activation(VT[:, i, :], M[2 + i % 2][:, 0:256], ACT.Copy).then_inc(E("vt_ev"), 1)
            halves(*FOX_PRE[1])
            norms(4, 12)

            def cum_rows(hp):
                if hp:
                    act.wait_ge(E("sc_read"), len(PIECES) // 2)
                for hh in range(2):
                    for h in range(2):
                        act.wait_ge(E("cb_mm"), 4 * hp + 2 * hh + h + 1)
                        act.activation(half(CB[hh], h), M[3 + h][:], ACT.Copy).then_inc(E("cb_ev"), 1)

            def fox_exp(n):
                hp, i, hh = FOX_UNITS[n]
                act.wait_ge(E("neg_max"), n + 1)
                act.activation(SC[n % 3][:, 0:(i + 1) * P], SC[n % 3][:, 0:(i + 1) * P], ACT.Exp,
                               bias=NM[:, n:n + 1], accum_out=SUM[:, n:n + 1]).then_inc(E("expd"), 1)

            def fox_out(n):
                hp, i, hh = FOX_UNITS[n]
                for g in range(i // 4 + 1):
                    m = group_of[(n, g)]
                    w = (min(4 * g + 4, i + 1) - 4 * g) * P
                    act.wait_ge(E("p_tr"), m + 1)
                    if m >= 3:
                        act.wait_ge(E("av_mm"), m - 2)
                    act.activation(PTS[m % 3][:, 0:w], M[3 + m % 2][:, 0:w], ACT.Copy).then_inc(E("p_ev"), 1)
                act.wait_ge(E("av_mm"), group_of[(n, i // 4)] + 1)
                r = slice(64 * hh, 64 * hh + 64)
                act.activation(MX[r, hp, i * P:(i + 1) * P], M[5][r, 0:P], ACT.Copy).then_inc(E("av_ev"), 1)

            for n in range(len(FOX_UNITS) + 1):
                if n % 16 == 0 and n < 32:
                    if n:
                        fox_out(n - 1)
                    cum_rows(n // 16)
                    fox_exp(n)
                    continue
                if n < 32:
                    fox_exp(n)
                halves(*FOX_UNIT[n])
                fox_out(n - 1)
            copy_out(2 * G0)
            norms(12, 16)

            act.wait_ge(E("mixed"), 2)
            for t in range(4):
                halves(*SSD_CONV[t])
                act.wait_ge(E("half_w"), 1)
                if t >= 2:
                    act.wait_ge(E("conv_out"), t - 1)
                y, th = mx(4 + t % 2), data(B + 6 + t % 2)
                act.activation(y, data(B + 2 + t), ACT.Identity, scale=CWS[:, t, 3:4], bias=CBS[:, t:t + 1])\
                   .then_inc(E("conv_in"), 1)
                act.wait_ge(E("conv_sum"), t + 1)
                act.activation(th, y, ACT.Tanh).then_inc(E("conv_th"), 1)
            for c in range(NT):
                halves(*SSD_CHUNK[c])
                act.wait_ge(E("s_seg"), c + 1)
                if c >= 1:
                    act.wait_ge(E("s_upd"), c)
                act.activation(D_, D_, ACT.Exp).then_inc(E("s_dexp"), 1)
                act.activation(EA, M[2][:], ACT.Exp).then_inc(E("s_ea"), 1)

            act.wait_ge(E("s_upd"), NT)
            act.wait_ge(E("s_yev"), NT)
            copy_out(2 * N_ITEMS)
            for p in range(2):
                gate(2 + p, data(B + p), data(B + 6 + p))
            act.wait_ge(E("gated"), 4)
            norms(16, 20)

            act.preload_act_table_set(LN_EXP)
            act.wait_ge(E("gl_abs"), 1)
            link(act.activation(data(B + 7), data(B + 7), ACT.Exp, scale=-1.0))
            act.activation(data(B + 7), data(B + 7), ACT.Ln, bias=one).then_inc(E("gl_ln"), 1)
            act.wait_ge(E("gl_cum"), 1)
            act.activation(data(B + 6), data(B + 7), ACT.Exp, scale=1.0 / 16).then_inc(E("gl_e1"), 1)
            act.wait_ge(E("gla_q"), 1)
            act.activation(data(B + 6), data(B + 7), ACT.Exp, scale=-1.0 / 16).then_inc(E("gl_e2"), 1)
            act.wait_ge(E("gl_te"), 1)
            act.activation(data(B + 7), data(B + 7), ACT.Exp, scale=1.0 / 16).then_inc(E("gl_e3"), 1)
            for i in range(NT):
                act.wait_ge(E("a_tr"), i + 1)
                if i >= 2:
                    act.wait_ge(E("a_y"), i - 1)
                act.activation(VK[i % 2][:, 0:3, :], M3[0][:, 0:3, :], ACT.Copy).then_inc(E("a_vk"), 1)
                if i >= 1:
                    act.wait_ge(E("a_y"), i)
                    act.activation(MX[:, 4:6, (i - 1) * P:i * P], M3[4 + (i - 1) % 2][:, 0:2, :], ACT.Copy)\
                       .then_inc(E("a_yev"), 1)
            act.wait_ge(E("a_y"), NT)
            link(act.activation(MX[:, 4:6, (NT - 1) * P:], M3[4 + (NT - 1) % 2][:, 0:2, :], ACT.Copy))
            act.wait_ge(E("a_s"), 2 * NT + 1)
            norms(20, 24)
            act.wait_ge(E("n_out"), 24)
            for p in range(2):
                gate(4 + p, data(A + 4 + p), data(B + 6 + p))

        @block.vector
        def _(dve):
            link = own(dve, "dve_own")

            def halves(m0, m1):
                for m in range(m0, m1):
                    if m % 2 == 0 and m // 2 + 1 < N_ITEMS:
                        lo(m // 2 + 1)

            def items(n0, n1):
                halves(2 * n0, 2 * n1)

            def lo(n):
                dve.wait_ge(E("g_hi"), n + 1)
                dve.tensor_tensor(WL[:, n % PART, :, :], WR[:, n % RAW, :, :], WH[:, n % PART, :, :], ALU.subtract)\
                   .then_inc(E("g_lo"), 1)

            def norms(u0, u1):
                for u in range(u0, u1):
                    src, w, _, _, rs = UNITS[u]
                    dve.wait_ge(E("n_rs"), u + 1)
                    dve.scalar_tensor_tensor(src, src, NWT[:, w:w + 1], rs, ALU.mult, ALU.mult).then_inc(E("n_out"), 1)

            def gate(k, z, th, y):
                dve.wait_ge(E("gate_th"), k + 1)
                link(dve.scalar_tensor_tensor(z, th, 1.0, z, ALU.add, ALU.mult))
                dve.scalar_tensor_tensor(y, z, 0.5, y, ALU.mult, ALU.mult).then_inc(E("gated"), 1)

            lo(0)
            items(0, 1)
            r = slice(0, 64)
            x, t1, t2, e = (v[r] for v in (data(SMALL), data(W1), mx(4), mx(6)))
            dve.wait_ge(E("params"), 16 * N_PAR)
            link(dve.tensor_scalar(PB[DT_ROW:DT_ROW + 4, 1:2], PB[DT_ROW:DT_ROW + 4, 1:2], -1.0, None, ALU.mult))
            link(dve.tensor_scalar(NWT[:, 0:1], NWT[:, 0:1], 0.125, None, ALU.mult))
            link(dve.tensor_scalar(CWS[:], CWS[:], 0.5, None, ALU.mult))
            dve.tensor_scalar(CBS[:], CBS[:], 0.5, None, ALU.mult).then_inc(E("half_w"), 1)
            dve.wait_ge(E("g_ev"), 2)
            dve.wait_ge(E("pads"), 1)
            link(dve.tensor_scalar(t1, x, PB[r, 0:1], PB[r, 1:2], ALU.mult, ALU.add))
            dve.scalar_tensor_tensor(t2, t1, -1.0, t1, ALU.mult, ALU.max).then_inc(E("sm_abs"), 1)
            dve.wait_ge(E("sm_ln"), 1)
            dve.wait_ge(E("sm_a"), 1)
            link(dve.scalar_tensor_tensor(t1, t1, 0.0, e, ALU.min, ALU.subtract))
            link(dve.tensor_scalar(t2, t1, PB[r, 2:3], None, ALU.mult))
            dve.wait_ge(E("restart"), 1)
            link(dve.tensor_tensor_scan(x, MX[r, 5, :], t2, 0.0, ALU.mult, ALU.add))
            chunks = lambda v, ch: v.rearrange("p (c i) -> p c i", i=ch)
            ends = lambda v, ch: chunks(v, ch)[:, :, ch - 1:ch].to_broadcast([v.shape[0], T // ch, ch])
            dve.tensor_tensor(chunks(t2, P), ends(x, P), chunks(x, P), ALU.subtract).then_inc(E("sm_te"), 1)
            dve.wait_ge(E("sm_we"), 1)
            link(dve.scalar_tensor_tensor(t2, t1, -1.0, t2, ALU.mult, ALU.mult))
            dve.tensor_scalar(t1, t1, -1.0, None, ALU.mult).then_inc(E("sm_rows"), 1)

            items(H0, F0)
            a0, a1, a2, a3 = (data(A + j) for j in range(4))
            link(dve.memset(a3, 1.0))
            link(dve.memset(SL[:, A + 3, PAD:SW:CH_HGRN], 0.0))
            for p in range(2):
                z, q, kin = data(B + 2 + p), data(B + p), data(A + 4 + p)
                dve.wait_ge(E("g_ev"), 2 * F0)
                dve.scalar_tensor_tensor(a0, z, -1.0, z, ALU.mult, ALU.max).then_inc(E("hg_abs"), 1)
                halves(*HG_PREP[2 * p])
                dve.wait_ge(E("hg_ln"), p + 1)
                link(dve.scalar_tensor_tensor(a1, z, 0.0, a0, ALU.min, ALU.subtract))
                link(dve.tensor_tensor(z, a1, z, ALU.subtract))
                dve.tensor_tensor_scan(a2, a3, a1, 0.0, ALU.mult, ALU.add).then_inc(E("hg_cum"), 1)
                dve.wait_ge(E("hg_e1"), p + 1)
                link(dve.tensor_copy(ED[:, p, :], SL[:, A, PAD + CH_HGRN - 1:SW:CH_HGRN]))
                dve.tensor_tensor(q, q, a0, ALU.mult).then_inc(E("hg_q"), 1)
                halves(*HG_PREP[2 * p + 1])
                dve.wait_ge(E("hg_e2"), p + 1)
                link(dve.tensor_tensor(kin, z, a0, ALU.mult))
                link(dve.tensor_copy(a1[:, 0:64], SL[:, A + 2, PAD + CH_HGRN - 1:SW:CH_HGRN]))
                dve.tensor_tensor(chunks(a2, CH_HGRN), a1[:, 0:64].unsqueeze(2).to_broadcast([P, 64, CH_HGRN]),
                                  chunks(a2, CH_HGRN), ALU.subtract).then_inc(E("hg_te"), 1)
                dve.wait_ge(E("hg_e3"), p + 1)
                dve.tensor_tensor(z, z, a2, ALU.mult).then_inc(E("h_prep"), 1)
            dve.wait_ge(E("att_zero"), 1)
            dve.wait_ge(E("s_zero"), 1)
            for i in range(NT):
                dve.wait_ge(E("h_att"), i + 1)
                if i >= 2:
                    dve.wait_ge(E("h_y"), i - 1)
                dve.copy_predicated(ATT[i % 2], M16[:].bitcast(mybir.dt.uint32).unsqueeze(1).to_broadcast([P, 4, P]),
                                    M3[1]).then_inc(E("h_am"), 1)
                halves(*HG_TILE[i])
                for p in range(2):
                    dve.wait_ge(E("h_ds"), 4 * i + 2 * p + 2)
                    if i >= 1:
                        dve.wait_ge(E("h_y"), i)
                    for c in range(8):
                        n = 8 * i + c
                        for hh in range(2):
                            q = slice(64 * hh, 64 * hh + 64)
                            m = 16 * (2 * i + p) + 2 * c + hh
                            if n >= 1 and c >= 1:
                                dve.wait_ge(E("h_s"), m - 1)
                            dve.scalar_tensor_tensor(S_HG[q, p, (n + 1) % 9, 64 * hh:64 * hh + 64],
                                                     S_HG[q, p, n % 9, 64 * hh:64 * hh + 64], ED[q, p, n:n + 1],
                                                     M[2 + 2 * p + hh][q, 64 * c:64 * c + 64], ALU.mult, ALU.add)\
                               .then_inc(E("h_s"), 1)
            norms(0, 4)
            for p in range(2):
                gate(p, data(B + 6 + p), data(A + p), mx(6 + p))
            dve.wait_ge(E("gated"), 2)
            dve.nop().then_inc(E("mixed"), 1)

            halves(*FOX_PRE[0])
            halves(*FOX_PRE[1])
            norms(4, 12)
            dve.wait_ge(E("st_ev"), NT)
            dve.wait_ge(E("masks"), 1)

            def logits(n):
                hp, i, hh = FOX_UNITS[n]
                h, sc, keys = 2 * hp + hh, SC[n % 3], (i + 1) * P
                dve.wait_ge(E("cb_ev"), 4 * hp + 2 * hh + 2)
                if n >= 3:
                    dve.wait_ge(E("p_tr"), group_of[(n - 3, FOX_UNITS[n - 3][1] // 4)] + 1)
                for c in range((keys + NW - 1) // NW):
                    m, w = piece_of[(n, c)], min(NW, keys - c * NW)
                    dve.wait_ge(E("sc_mm"), m + 1)
                    dve.scalar_tensor_tensor(sc[:, c * NW:c * NW + w], M[m % 3][:, 0:w], ST[:, i, 0, h:h + 1],
                                             CB[hh][:, c * NW:c * NW + w], ALU.add, ALU.subtract).then_inc(E("sc_read"), 1)
                dve.wait_ge(E("sc_read"), m + 1)
                link(dve.tensor_tensor(sc[:, keys - P:keys], sc[:, keys - P:keys], NEGQ[:], ALU.add))
                dve.tensor_reduce(NM[:, n:n + 1], sc[:, 0:keys], AX.X, ALU.max, negate=True).then_inc(E("neg_max"), 1)

            def probabilities(n):
                sc, keys = SC[n % 3], (FOX_UNITS[n][1] + 1) * P
                dve.wait_ge(E("expd"), n + 1)
                link(dve.reciprocal(RIN[:, n:n + 1], SUM[:, n:n + 1]))
                dve.tensor_scalar(sc[:, 0:keys], sc[:, 0:keys], RIN[:, n:n + 1], None, ALU.mult).then_inc(E("probs"), 1)

            for n in range(33):
                if n < 32 and n % 16:
                    logits(n)
                halves(*FOX_UNIT[n])
                if n:
                    probabilities(n - 1)
                if n in (0, 16):
                    logits(n)
            norms(12, 16)
            dve.wait_ge(E("n_out"), 16)
            dve.wait_ge(E("av_ev"), 32)
            dve.nop().then_inc(E("mixed"), 1)

            for t in range(4):
                s = B + 2 + t
                y, th = mx(4 + t % 2), data(B + 6 + t % 2)
                halves(*SSD_CONV[t])
                dve.wait_ge(E("conv_in"), t + 1)
                for j in (2, 1):
                    link(dve.scalar_tensor_tensor(y, SL[:, s, PAD - 3 + j:PAD - 3 + j + T], CWS[:, t, j:j + 1], y,
                                                  ALU.mult, ALU.add))
                dve.scalar_tensor_tensor(y, SL[:, s, PAD - 3:PAD - 3 + T], CWS[:, t, 0:1], y, ALU.mult, ALU.add)\
                   .then_inc(E("conv_sum"), 1)
                dve.wait_ge(E("conv_th"), t + 1)
                dve.scalar_tensor_tensor(data(s), th, 1.0, y, ALU.add, ALU.mult).then_inc(E("conv_out"), 1)
            dve.wait_ge(E("conv_out"), 4)
            S = S_SSD
            for c in range(NT):
                sd = SCD[c % 2]
                halves(*SSD_CHUNK[c])
                dve.wait_ge(E("s_tr"), c + 1)
                if c >= 1:
                    dve.wait_ge(E("s_ds"), c)
                by_head = lambda v: v.rearrange("p (h d) -> p h d", h=4)
                rows = lambda k: ST[:, c, k, DT_ROW:DT_ROW + 4].unsqueeze(2)
                dve.tensor_tensor(by_head(XDT), by_head(M[0][:, 0:256]), rows(1).to_broadcast([P, 4, 64]), ALU.mult)\
                   .then_inc(E("s_x"), 1)
                dve.tensor_tensor(by_head(XDTE), by_head(M[0][:, 0:256]), rows(2).to_broadcast([P, 4, 64]), ALU.mult)\
                   .then_inc(E("s_x"), 1)
                dve.tensor_copy(BT[:], M[0][:, 256:384]).then_inc(E("s_x"), 1)
                dve.wait_ge(E("s_ab"), c + 1)
                link(dve.tensor_tensor(by_head(D_), M3[2], rows(0).to_broadcast([P, 4, P]), ALU.subtract))
                dve.tensor_tensor(by_head(D_), by_head(D_), NEGK[:].unsqueeze(1).to_broadcast([P, 4, P]), ALU.add)\
                   .then_inc(E("s_seg"), 1)
                dve.wait_ge(E("s_dexp"), c + 1)
                dve.wait_ge(E("s_g"), c + 1)
                for g in range(2):
                    v = slice(256 * g, 256 * g + 256)
                    dve.tensor_tensor(sd[:, v].rearrange("p (h t) -> p h t", h=2),
                                      M[1][:, P * g:P * g + P].unsqueeze(1).to_broadcast([P, 2, P]),
                                      D_[:, v].rearrange("p (h t) -> p h t", h=2), ALU.mult).then_inc(E("s_scd"), 1)
                dve.wait_ge(E("s_ea"), c + 1)
                dve.tensor_tensor(by_head(CA), tile(B + 5, c).unsqueeze(1).to_broadcast([P, 4, P]), by_head(EA),
                                  ALU.mult).then_inc(E("s_ca"), 1)
                dve.wait_ge(E("s_y"), c + 1)
                for p in range(2):
                    dve.scalar_tensor_tensor(MX[:, 2 + p, c * P:(c + 1) * P], tile(B + 2 + p, c), DSK[:, p:p + 1],
                                             M3[3][:, p, :], ALU.mult, ALU.add).then_inc(E("s_yp"), 1)
                dve.wait_ge(E("s_yp"), 2 * c + 2)
                dve.nop().then_inc(E("s_yev"), 1)
                dve.wait_ge(E("s_ds"), c + 1)
                for g in range(2):
                    q, hs = slice(64 * g, 64 * g + 64), slice(2 * g, 2 * g + 2)
                    end = by_head(EA)[q, hs, P - 1:P].to_broadcast([64, 2, 64])
                    link(dve.tensor_tensor(S[q, hs, :], S[q, hs, :], end, ALU.mult))
                    link(dve.tensor_tensor(S[q, hs, :], S[q, hs, :], M[5][q, 0:256].rearrange(
                        "p (h d) -> p h d", h=4)[:, hs, :], ALU.add))
                dve.nop().then_inc(E("s_upd"), 1)
            for p in range(2):
                gate(2 + p, data(B + p), data(B + 6 + p), mx(2 + p))
            norms(16, 20)
            dve.wait_ge(E("n_out"), 20)
            dve.nop().then_inc(E("mixed"), 1)

            z, u, k, kin = data(B + 6), data(B + 7), data(A + 1), data(W1)
            for h in range(2):
                dve.wait_ge(E("gate_mm"), h + 1)
                link(dve.tensor_scalar(half(z, h), M[h][:], BG2[:], None, ALU.add))
            dve.scalar_tensor_tensor(u, z, -1.0, z, ALU.mult, ALU.max).then_inc(E("gl_abs"), 1)
            link(dve.memset(kin, 1.0))
            link(dve.memset(SL[:, W1, PAD:SW:CH_GLA], 0.0))
            dve.wait_ge(E("gl_ln"), 1)
            link(dve.scalar_tensor_tensor(z, z, 0.0, u, ALU.min, ALU.subtract))
            dve.tensor_tensor_scan(u, kin, z, 0.0, ALU.mult, ALU.add).then_inc(E("gl_cum"), 1)
            dve.wait_ge(E("gl_e1"), 1)
            dve.wait_ge(E("g_ev"), 2 * N_ITEMS)
            link(dve.tensor_copy(ED[:, 0, 0:16], SL[:, B + 6, PAD + CH_GLA - 1:SW:CH_GLA]))
            dve.scalar_tensor_tensor(data(A), data(A), 32.0 ** -0.5, z, ALU.mult, ALU.mult).then_inc(E("gla_q"), 1)
            dve.wait_ge(E("gl_e2"), 1)
            dve.tensor_tensor(kin, k, z, ALU.mult).then_inc(E("gl_kin"), 1)
            dve.wait_ge(E("gl_kin"), 1)
            link(dve.tensor_copy(z[:, 0:16], SL[:, B + 7, PAD + CH_GLA - 1:SW:CH_GLA]))
            dve.tensor_tensor(chunks(u, CH_GLA), z[:, 0:16].unsqueeze(2).to_broadcast([P, 16, CH_GLA]),
                              chunks(u, CH_GLA), ALU.subtract).then_inc(E("gl_te"), 1)
            dve.wait_ge(E("gl_e3"), 1)
            dve.tensor_tensor(k, k, u, ALU.mult).then_inc(E("gl_kend"), 1)
            S = lambda n: z[:, 256 * (n % 4):256 * (n % 4) + 256]
            DM = lambda n: u[:, 256 * (n % 2):256 * (n % 2) + 256]
            dve.wait_ge(E("gl_te"), 1)
            dve.wait_ge(E("gl_kend"), 1)
            dve.memset(S(0), 0.0).then_inc(E("a_s"), 1)
            dve.wait_ge(E("att_zero"), 2)
            for i in range(NT):
                dve.wait_ge(E("a_att"), i + 1)
                if i >= 2:
                    dve.wait_ge(E("a_y"), i - 1)
                dve.copy_predicated(ATT[i % 2], M64[:].bitcast(mybir.dt.uint32).unsqueeze(1).to_broadcast([P, 4, P]),
                                    M3[1]).then_inc(E("a_am"), 1)
                dve.wait_ge(E("a_ds"), i + 1)
                for c in range(2):
                    n = 2 * i + c
                    link(dve.tensor_tensor(DM(n), M[2 + c][:, 0:256], BM[:].rearrange("p h d -> p (h d)"), ALU.mult))
                    dve.wait_ge(E("a_s"), n + 1)
                    dve.scalar_tensor_tensor(S(n + 1), S(n), ED[:, 0, n:n + 1], DM(n), ALU.mult, ALU.add)\
                       .then_inc(E("a_s"), 1)
            norms(20, 24)
            for p in range(2):
                gate(4 + p, data(A + 4 + p), data(B + 6 + p), mx(4 + p))

        @block.tensor
        def _(pe):
            def halves(m0, m1):
                for m in range(m0, m1):
                    n, h = divmod(m, 2)
                    if h == 0:
                        pe.wait_ge(E("g_lo"), n + 1)
                    if n >= 1:
                        pe.wait_ge(E("g_ev"), m - 1)
                    for k in range(KT):
                        mm = split_matmuls(pe, gb[h][:], WH[:, n % PART, k, :], WL[:, n % PART, k, :],
                                           half(HH[:, k, :], h), half(HL[:, k, :], h), k == 0, k == KT - 1)
                    mm.then_inc(E("g_mm"), 1)

            def items(n0, n1):
                halves(2 * n0, 2 * n1)

            def norms(u0, u1):
                for u in range(u0, u1):
                    _, _, ones, sq, _ = UNITS[u]
                    pe.wait_ge(E("n_sq"), u + 1)
                    if u >= 2:
                        pe.wait_ge(E("n_ln"), u - 1)
                    pe.matmul(M[4 + u % 2][:], ones[:], sq, start=True, stop=True).then_inc(E("n_ms"), 1)

            def row(r):
                return ident[:, r:r + 1].to_broadcast([P, P])

            items(0, 1)
            pe.wait_ge(E("sm_rows"), 1)
            for i in range(NT):
                if i >= 2:
                    pe.wait_ge(E("st_ev"), i - 1)
                tok = slice(i * P, (i + 1) * P)
                for j, v in enumerate((data(SMALL), data(W1), mx(4))):
                    last = pe.transpose(M3[i % 2][:, j, 0:64], v[0:64, tok], ident[0:64, 0:64])
                last.then_inc(E("st_tr"), 1)

            items(H0, F0)
            for j in range(4):
                halves(*HG_PREP[j])
            pe.wait_ge(E("h_prep"), 2)

            def hgrn_scores(i):
                if i >= 1:
                    pe.wait_ge(E("h_vk"), i)
                if i >= 2:
                    pe.wait_ge(E("h_yev"), i - 1)
                for j in range(4):
                    last = pe.transpose(M3[0][:, j, :], tile((B + 4, B + 5, B + 2, B + 3)[j], i), ident)
                last.then_inc(E("h_tr"), 1)
                pe.wait_ge(E("h_qx"), 2 * i + 2)
                if i >= 1:
                    pe.wait_ge(E("h_am"), i)
                for p in range(2):
                    mm = pe.matmul(M[1][:, 256 * p:256 * p + 256], tile(A + 4 + p, i),
                                   QX[:, 2 * p:2 * p + 2, :].rearrange("p h t -> p (h t)"), start=True, stop=True)
                mm.then_inc(E("h_att"), 1)

            def hgrn_states(i):
                for h in range(4):
                    p, hh = h // 2, h % 2
                    pe.wait_ge(E("h_vx"), 4 * i + h + 1)
                    if i >= 1:
                        pe.wait_ge(E("h_s"), 16 * (2 * (i - 1) + p + 1))
                    pe.matmul(M[2 + h][:], VK[i % 2][:, 2 + p, :], VX[:, h, :, :].rearrange("p c d -> p (c d)"),
                              start=True, stop=True).then_inc(E("h_ds"), 1)

            def hgrn_outputs(i):
                vk = VK[i % 2]
                pe.wait_ge(E("h_am"), i + 1)
                pe.wait_ge(E("h_s"), 32 * i + 32)
                pe.wait_ge(E("h_vk"), min(i + 2, NT))
                if i >= 1:
                    pe.wait_ge(E("h_yev"), i)
                yb = M3[0]
                for p in range(2):
                    for hh in range(2):
                        pe.matmul(yb[64 * hh:64 * hh + 64, p, :], vk[:, p, 64 * hh:64 * hh + 64], ATT[i % 2][:, 2 * p + hh, :],
                                  start=True, stop=False, skip_group_check=True)
                    for c in range(8):
                        mm = pe.matmul(yb[:, p, 16 * c:16 * c + 16], S_HG[:, p, (8 * i + c) % 9, :],
                                       tile(B + p, i)[:, 16 * c:16 * c + 16], start=False, stop=True,
                                       skip_group_check=True)
                mm.then_inc(E("h_y"), 1)

            hgrn_scores(0)
            for i in range(NT):
                hgrn_states(i)
                if i + 1 < NT:
                    hgrn_scores(i + 1)
                halves(*HG_TILE[i])
                hgrn_outputs(i)
            norms(0, 4)

            pe.wait_ge(E("g_ev"), 2 * S0)
            pe.wait_ge(E("mixed"), 1)
            for i in range(NT):
                if i >= 2:
                    pe.wait_ge(E("vt_ev"), i - 1)
                for j in range(2):
                    last = pe.transpose(M3[2 + i % 2][:, j, :], tile(FV + j, i), ident)
                last.then_inc(E("vt_tr"), 1)
                if i == 1:
                    halves(*FOX_PRE[0])
            halves(*FOX_PRE[1])
            norms(4, 12)

            def cum_rows(hp):
                for hh in range(2):
                    for h in range(2):
                        m = 4 * hp + 2 * hh + h
                        if hp:
                            pe.wait_ge(E("p_ev"), len(GROUPS) // 2)
                        elif m < 2:
                            pe.wait_ge(E("n_ln"), 12)
                        if m % 4 >= 2:
                            pe.wait_ge(E("cb_ev"), m - 1)
                        pe.matmul(M[3 + h][:], row(2 * hp + hh), half(data(SMALL), h), start=True, stop=True)\
                          .then_inc(E("cb_mm"), 1)

            def scores(n):
                hp, i, hh = FOX_UNITS[n]
                r, keys = slice(64 * hh, 64 * hh + 64), (i + 1) * P
                for c in range((keys + NW - 1) // NW):
                    m, w = piece_of[(n, c)], min(NW, keys - c * NW)
                    if m >= 3:
                        pe.wait_ge(E("sc_read"), m - 2)
                    pe.matmul(M[m % 3][:, 0:w], tile(FQ + hp, i)[r, :], data(FK + hp)[r, c * NW:c * NW + w],
                              start=True, stop=True).then_inc(E("sc_mm"), 1)

            def outputs(n):
                hp, i, hh = FOX_UNITS[n]
                r = slice(64 * hh, 64 * hh + 64)
                pe.wait_ge(E("probs"), n + 1)
                for g in range(i // 4 + 1):
                    m, kb = group_of[(n, g)], range(4 * g, min(4 * g + 4, i + 1))
                    if m >= 2:
                        pe.wait_ge(E("p_ev"), m - 1)
                    if m <= 1 or n == 16:
                        pe.wait_ge(E("cb_ev"), 4 * hp + 4)
                    for k in kb:
                        last = pe.transpose(M3[3 + m % 2][:, k % 4, :], SC[n % 3][:, k * P:(k + 1) * P], ident)
                    last.then_inc(E("p_tr"), 1)
                if n >= 1:
                    pe.wait_ge(E("av_ev"), n)
                for g in range(i // 4 + 1):
                    m, kb = group_of[(n, g)], range(4 * g, min(4 * g + 4, i + 1))
                    pe.wait_ge(E("p_ev"), m + 1)
                    for k in kb:
                        mm = pe.matmul(M[5][r, 0:P], VT[:, k, 128 * hp + 64 * hh:128 * hp + 64 * hh + 64],
                                       PTS[m % 3][:, (k % 4) * P:(k % 4 + 1) * P], start=(k == 0), stop=(k == i))
                    mm.then_inc(E("av_mm"), 1)

            pe.wait_ge(E("n_out"), 12)
            for n in range(33):
                if n % 16 == 0 and n < 32:
                    if n:
                        outputs(n - 1)
                    cum_rows(n // 16)
                    scores(n)
                    continue
                if n < 32:
                    scores(n)
                halves(*FOX_UNIT[n])
                outputs(n - 1)
            norms(12, 16)

            pe.wait_ge(E("mixed"), 2)
            for t in range(4):
                halves(*SSD_CONV[t])
            pe.wait_ge(E("conv_out"), 4)
            for c in range(NT):
                if c >= 1:
                    pe.wait_ge(E("s_x"), 3 * c)
                for j, s in enumerate((B + 2, B + 3, B + 4)):
                    last = pe.transpose(M3[0][:, j, :], tile(s, c), ident)
                last.then_inc(E("s_tr"), 1)
                if c >= 1:
                    pe.wait_ge(E("s_ea"), c)
                for h in range(4):
                    mm = pe.matmul(M3[2][:, h, :], row(DT_ROW + h), tile(SMALL, c), start=True, stop=True)
                mm.then_inc(E("s_ab"), 1)
                pe.wait_ge(E("cmc"), 2 * c + 2)
                if c >= 1:
                    pe.wait_ge(E("s_scd"), 2 * c)
                pe.matmul(M[1][:, 0:256], tile(B + 4, c), CMC[c % 2].rearrange("p g t -> p (g t)"),
                          start=True, stop=True).then_inc(E("s_g"), 1)
                halves(*SSD_CHUNK[c])
                pe.wait_ge(E("s_x"), 3 * c + 3)
                pe.wait_ge(E("s_scd"), 2 * c + 2)
                pe.wait_ge(E("s_ca"), c + 1)
                if c >= 1:
                    pe.wait_ge(E("s_upd"), c)
                    pe.wait_ge(E("s_yev"), c)
                for h in range(4):
                    y = M3[3][64 * (h % 2):64 * (h % 2) + 64, h // 2, :]
                    pe.matmul(y, XDT[:, 64 * h:64 * h + 64], SCD[c % 2][:, P * h:P * h + P], start=True, stop=False,
                              skip_group_check=True)
                    mm = pe.matmul(y, S_SSD[:, h, :], CA[:, P * h:P * h + P], start=False, stop=True,
                                   skip_group_check=True)
                mm.then_inc(E("s_y"), 1)
                pe.matmul(M[5][:, 0:256], BT[:], XDTE, start=True, stop=True).then_inc(E("s_ds"), 1)
            pe.wait_ge(E("s_upd"), NT)
            norms(16, 20)

            pe.wait_ge(E("mixed"), 3)
            for h in range(2):
                pe.matmul(M[h][:], WG2[:], half(data(SMALL), h), start=True, stop=True).then_inc(E("gate_mm"), 1)
            pe.wait_ge(E("gl_kin"), 1)
            pe.wait_ge(E("gl_kend"), 1)

            def gla_scores(i):
                if i >= 1:
                    pe.wait_ge(E("a_vk"), i)
                for j in range(3):
                    last = pe.transpose(M3[0][:, j, :], tile((A + 2, A + 3, A + 1)[j], i), ident)
                last.then_inc(E("a_tr"), 1)
                pe.wait_ge(E("a_qx"), i + 1)
                if i >= 1:
                    pe.wait_ge(E("a_am"), i)
                pe.matmul(M[1][:], tile(W1, i), QX.rearrange("p h t -> p (h t)"), start=True, stop=True)\
                  .then_inc(E("a_att"), 1)

            def gla_states(i):
                pe.wait_ge(E("a_vk"), i + 1)
                if i >= 1:
                    pe.wait_ge(E("a_s"), 2 * i + 1)
                vk = VK[i % 2]
                for c in range(2):
                    q = slice(64 * c, 64 * c + 64)
                    mm = pe.matmul(M[2 + c][:, 0:256], vk[q, 2, :], vk[q, 0:2, :].rearrange("p a b -> p (a b)"),
                                   start=True, stop=True)
                mm.then_inc(E("a_ds"), 1)

            def gla_outputs(i):
                vk = VK[i % 2]
                pe.wait_ge(E("a_am"), i + 1)
                pe.wait_ge(E("a_s"), 2 * i + 2)
                if i >= 2:
                    pe.wait_ge(E("a_yev"), i - 1)
                yb = M3[4 + i % 2]
                for p in range(2):
                    for hh in range(2):
                        pe.matmul(yb[64 * hh:64 * hh + 64, p, :], vk[:, p, 64 * hh:64 * hh + 64], ATT[i % 2][:, 2 * p + hh, :],
                                  start=True, stop=False, skip_group_check=True)
                    for c in range(2):
                        n = 2 * i + c
                        mm = pe.matmul(yb[:, p, 64 * c:64 * c + 64],
                                       data(B + 6)[:, 256 * (n % 4) + P * p:256 * (n % 4) + P * p + P],
                                       tile(A, i)[:, 64 * c:64 * c + 64], start=False, stop=True, skip_group_check=True)
                mm.then_inc(E("a_y"), 1)

            gla_scores(0)
            for i in range(NT):
                gla_states(i)
                if i + 1 < NT:
                    gla_scores(i + 1)
                gla_outputs(i)
            norms(20, 24)


def constants_block(nc, cst_tiles, a, CW, CB):
    ident, ones, eps = cst_tiles
    with Phase(nc, "const") as ph, ExitStack() as ctx:
        sem = ph.sem
        zeroed, filled, loaded = sem("zeroed"), sem("filled"), sem("loaded")
        block = ctx.enter_context(nc.Block())

        @block.gpsimd
        def _(pool):
            pool.memset(ident[:], 0.0).then_inc(zeroed, 1)
            pool.wait_ge(zeroed, 1)
            pool.affine_select(out=ident[:], in_=ident[:], compare_op=ALU.not_equal, fill=1.0, base=0,
                               pattern=[[-1, P]], channel_multiplier=1).then_inc(filled, 1)
            pool.memset(eps[:], EPS).then_inc(filled, 1)
            pool.memset(ones[:], 1.0).then_inc(filled, 1)

        @block.sync
        def _(sp):
            with nc.allow_non_contiguous_dma(reason="small parameter columns"):
                for j in range(3):
                    sp.dma_start(CW[:, :, j], a["ffn_conv_w"][0, j].rearrange("(f p) -> p f", p=P)).then_inc(loaded, 16)
                sp.dma_start(CB[:], a["ffn_conv_b"][0].rearrange("(f p) -> p f", p=P)).then_inc(loaded, 16)
            sp.wait_ge(loaded, 64)


def build(nc, a, out):
    x, mem = a["x"][0], a["mem"][0]
    with ExitStack() as ctx:
        sb = lambda c, s, shape, dt=F32: c.enter_context(nc.sbuf_tensor(s, shape, dt))
        ident, ones, eps = sb(ctx, "ident", [P, P]), sb(ctx, "ones1", [P, 1]), sb(ctx, "eps", [P, 1])
        CW, CB = sb(ctx, "CW", [P, NF, 3]), sb(ctx, "CB", [P, NF])
        HALO = sb(ctx, "HALO", [P, NF, 2])
        stored = ctx.enter_context(nc.semaphore("stored"))
        cst = {"ident": ident[:], "eps": eps[:], "one": ones[:]}
        XR = sb(ctx, "XR", [P, NT, D])
        constants_block(nc, (ident, ones, eps), a, CW, CB)
        with ExitStack() as attn:
            HH, HL = sb(attn, "HH", [P, KT, T], F32R), sb(attn, "HL", [P, KT, T], F32R)
            norm_block(nc, "n1", cst, XR, HH, HL, a["ln_mix"][0], range(NT), x)
            if MIXERS:
                mixers_block(nc, cst, a, XR, HH, HL)
            token_major_product(nc, "wo", HH, HL, a["w_out"][0], NT, 2, residual_evac(XR, x),
                                presplit=XR if MIXERS else None)
            QN, KN, V = sb(attn, "QN", [P, NT, D]), sb(attn, "KN", [P, 2, D]), sb(attn, "V", [P, 2, D])
            norm_block(nc, "nm", cst, KN, HH, HL, a["mem_norm"], range(2), mem)
            token_major_product(nc, "kv", HH, HL, a["xa_wkv"][0], 2, 4,
                                head_norm_evac(nc, "kn", cst, KN, 2, a["xa_kn"][0], 1.0, 2, V))
            norm_block(nc, "n2", cst, XR, HH, HL, a["ln_xattn"][0], range(NT))
            token_major_product(nc, "q", HH, HL, a["xa_wq"][0], NT, 2,
                                head_norm_evac(nc, "qn", cst, QN, NT, a["xa_qn"][0], XA_DIM ** -0.5, 2))
            memory_attention_block(nc, cst, QN, KN, V, HH, HL)
            token_major_product(nc, "xo", HH, HL, a["xa_wo"][0], NT, 2, residual_evac(XR))
        for u in range(2):
            with ExitStack() as c:
                H2, L2 = sb(c, f"HH{u}", [P, KT, T // 2], F32R), sb(c, f"HL{u}", [P, KT, T // 2], F32R)
                norm_block(nc, f"n3{u}", cst, XR, H2, L2, a["ln_ffn"][0], range(4 * u, 4 * u + 4))
                ffn_block(nc, u, cst, XR, H2, L2, HALO, CW, CB, a["ffn_w_up"][0], a["ffn_w_down"][0], out,
                          stored)


def kernel(**inputs):
    import numpy as _np
    import concourse.bacc as _bacc
    from concourse import mybir as _mybir
    from concourse.bass_utils import run_bass_kernel_spmd as _run

    nc = _bacc.Bacc("TRN2", target_bir_lowering=False, num_devices=1)
    arrays, args = {}, {}
    for name, value in inputs.items():
        arrays[f"in_{name}"] = _np.ascontiguousarray(value)
        args[name] = nc.dram_tensor(f"in_{name}", arrays[f"in_{name}"].shape, _mybir.dt.float32,
                                    kind="ExternalInput").ap()
    out = nc.dram_tensor("out", (1, T, D), _mybir.dt.float32, kind="ExternalOutput").ap()
    build(nc, args, out[0])
    return _run(nc, [arrays], core_ids=[0]).results[0]["out"]
```

```python
from contextlib import ExitStack

import concourse.bass as bass
from concourse import mybir

F32 = mybir.dt.float32
F32R = mybir.dt.float32r
ACT = mybir.ActivationFunctionType
ALU = mybir.AluOpType
AX = mybir.AxisListType

P = 128
D = 1024
T = 1024
KT = D // P
NT = T // P
NW = 512
EPS = 1e-6
LN_EXP = "natural_log_exp_and_others"
N_MEM = 256
XA_HEADS = 4
XA_DIM = D // XA_HEADS
D_FF = 2816
NF = D_FF // P


class Phase:
    done = None

    def __init__(self, nc, name):
        self.nc, self.name, self.sems = nc, name, []
        self.stack, self.inner, self.sem_stack = ExitStack(), ExitStack(), ExitStack()

    def __enter__(self):
        return self

    def sem(self, s):
        one = self.sem_stack.enter_context(self.nc.semaphore(f"{self.name}_{s}"))
        self.sems.append(one)
        return one

    def sb(self, s, shape, dtype=F32):
        return self.stack.enter_context(self.nc.sbuf_tensor(f"{self.name}_{s}", shape, dtype))

    def ps(self, s, shape):
        return self.stack.enter_context(self.nc.psum_tensor(f"{self.name}_{s}", shape, F32))

    def clear_done(self, pool):
        for one in Phase.done.sems if Phase.done else ():
            pool.sem_clear(one)

    def clears(self, block):
        if Phase.done:
            @block.gpsimd
            def _(pool):
                self.clear_done(pool)

    def __exit__(self, *error):
        self.inner.__exit__(*error)
        if Phase.done:
            Phase.done.sem_stack.close()
        Phase.done = self
        self.stack.__exit__(*error)

    @staticmethod
    def finish(nc):
        with nc.Block() as block:
            Phase.done.clears(block)
        Phase.done.sem_stack.close()
        Phase.done = None


def split_matmuls(pe, out, hi_w, lo_w, hi_x, lo_x, first, last):
    pe.matmul(out, hi_w, hi_x, start=first, stop=False)
    pe.matmul(out, hi_w, lo_x, start=False, stop=False)
    return pe.matmul(out, lo_w, hi_x, start=False, stop=last)


def norm_block(nc, name, cst, XR, HH, HL, LNB, tiles, x_loaded, parameters_loaded):
    n = len(tiles)
    with Phase(nc, name) as ph, ExitStack() as ctx:
        sem = ph.sem
        XS = ctx.enter_context(nc.sbuf_tensor(f"{name}_xs", [P, 2, D], F32))
        SQ = ctx.enter_context(nc.sbuf_tensor(f"{name}_sq", [P, D], F32))
        SS = ctx.enter_context(nc.sbuf_tensor(f"{name}_ss", [P, n], F32))
        LG = ctx.enter_context(nc.sbuf_tensor(f"{name}_lg", [P, n], F32))
        RS = ctx.enter_context(nc.sbuf_tensor(f"{name}_rs", [P, n], F32))
        tr_bank = [ctx.enter_context(nc.psum_tensor(f"{name}_tr{i}", [P, 4, P], F32)) for i in range(4)]
        squared, logged, rstd_ready, scaled, transposed, hi_ready, lo_ready = (
            sem(s) for s in ("squared", "logged", "rstd", "scaled", "transposed", "hi", "lo"))
        block = ctx.enter_context(nc.Block())
        ph.clears(block)

        @block.sync
        def _(sp):
            sp.wait_ge(parameters_loaded, 64)

        @block.scalar
        def _(act):
            act.preload_act_table_set(LN_EXP)

            def stats(i):
                act.wait_ge(x_loaded[i], 32 if i == 0 else 16)
                act.activation(SQ[:], XR[:, tiles[i], :], ACT.Square, accum_out=SS[:, i:i + 1]).then_inc(squared, 1)
                act.wait_ge(squared, i + 1)
                act.activation(LG[:, i:i + 1], SS[:, i:i + 1], ACT.Ln, scale=1.0 / D,
                               bias=cst["eps"]).then_inc(logged, 1)
                act.wait_ge(logged, i + 1)
                act.activation(RS[:, i:i + 1], LG[:, i:i + 1], ACT.Exp, scale=-0.5).then_inc(rstd_ready, 1)

            stats(0)
            for i in range(n):
                if i + 1 < n:
                    stats(i + 1)
                for g in range(2):
                    u = 2 * i + g
                    act.wait_ge(transposed, u + 1)
                    act.activation(HH[:, 4 * g:4 * g + 4, i * P:(i + 1) * P], tr_bank[u % 4][:], ACT.Copy)\
                       .then_inc(hi_ready, 1)

        @block.vector
        def _(dve):
            def scale(i):
                if i == 0:
                    dve.wait_ge(x_loaded[0], 32)
                dve.wait_ge(rstd_ready, i + 1)
                if i >= 2:
                    dve.wait_ge(transposed, 2 * (i - 1))
                dve.scalar_tensor_tensor(XS[:, i % 2, :], XR[:, tiles[i], :], RS[:, i:i + 1], LNB,
                                         ALU.mult, ALU.mult).then_inc(scaled, 1)

            scale(0)
            for i in range(n):
                if i + 1 < n:
                    scale(i + 1)
                for g in range(2):
                    u = 2 * i + g
                    dve.wait_ge(hi_ready, u + 1)
                    dve.tensor_tensor(HL[:, 4 * g:4 * g + 4, i * P:(i + 1) * P], tr_bank[u % 4][:],
                                      HH[:, 4 * g:4 * g + 4, i * P:(i + 1) * P], ALU.subtract).then_inc(lo_ready, 1)

        @block.tensor
        def _(pe):
            for i in range(n):
                pe.wait_ge(scaled, i + 1)
                for g in range(2):
                    u = 2 * i + g
                    if u >= 4:
                        pe.wait_ge(lo_ready, u - 3)
                    for k in range(4):
                        c = (4 * g + k) * P
                        last = pe.transpose(tr_bank[u % 4][:, k, :], XS[:, i % 2, c:c + P], cst["ident"])
                    last.then_inc(transposed, 1)


def token_major_product(nc, name, HH, HL, w, n_tok, chunks, evac):
    RAW, PART = 4, 3
    steps = [(c, k) for c in range(chunks) for k in range(KT)]
    with Phase(nc, name) as ph, ExitStack() as ctx:
        sem = ph.sem
        WR = ctx.enter_context(nc.sbuf_tensor(f"{name}_wr", [P, RAW, NW], F32))
        WH = ctx.enter_context(nc.sbuf_tensor(f"{name}_wh", [P, PART, NW], F32R))
        WL = ctx.enter_context(nc.sbuf_tensor(f"{name}_wl", [P, PART, NW], F32R))
        bank = [ctx.enter_context(nc.psum_tensor(f"{name}_acc{i}", [P, NW], F32)) for i in range(8)]
        w_loaded = [sem(f"w_loaded{i}") for i in range(RAW)]
        w_hi, w_lo, step_done, bank_done, evacuated = (
            sem(s) for s in ("w_hi", "w_lo", "step_done", "bank_done", "evacuated"))
        ev = evac(ctx, sem, bank, bank_done, evacuated)
        block = ctx.enter_context(nc.Block())
        ph.clears(block)
        per = 8 // n_tok

        def wait_step(eng, s):
            c, k = steps[s]
            if k == KT - 1:
                eng.wait_ge(bank_done, n_tok * (c + 1))
            else:
                eng.wait_ge(step_done, s - c + 1)

        @block.sync
        def _(sp):
            for s, (c, k) in enumerate(steps):
                if s >= RAW:
                    sp.wait_ge(w_lo, s - RAW + 1)
                sp.dma_start(WR[:, s % RAW, :], w[k * P:(k + 1) * P, c * NW:(c + 1) * NW])\
                  .then_inc(w_loaded[s % RAW], 16)

        @block.scalar
        def _(act):
            act.preload_act_table_set(LN_EXP)
            ev["act_start"](act)
            for s in range(len(steps)):
                act.wait_ge(w_loaded[s % RAW], 16 * (s // RAW + 1))
                if s >= PART:
                    wait_step(act, s - PART)
                act.activation(WH[:, s % PART, :], WR[:, s % RAW, :], ACT.Copy).then_inc(w_hi, 1)
                if s == 3:
                    ev["act_early"](act)
                if s >= KT + 1 and s % KT == 1:
                    ev["act"](act, s // KT - 1)
            ev["act"](act, chunks - 1)

        @block.vector
        def _(dve):
            for s in range(len(steps)):
                dve.wait_ge(w_hi, s + 1)
                dve.tensor_tensor(WL[:, s % PART, :], WR[:, s % RAW, :], WH[:, s % PART, :], ALU.subtract)\
                   .then_inc(w_lo, 1)
                if s == 3:
                    ev["dve_early"](dve)
                if s >= KT + 1 and s % KT == 1:
                    ev["dve"](dve, s // KT - 1)
            ev["dve"](dve, chunks - 1)

        @block.tensor
        def _(pe):
            for s, (c, k) in enumerate(steps):
                pe.wait_ge(w_lo, s + 1)
                for t in range(n_tok):
                    if k == 0 and c >= per:
                        pe.wait_ge(evacuated, n_tok * (c - per) + t + 1)
                    tok = slice(t * P, (t + 1) * P)
                    mm = split_matmuls(pe, bank[(c % per) * n_tok + t][:], HH[:, k, tok], HL[:, k, tok],
                                       WH[:, s % PART, :], WL[:, s % PART, :], k == 0, k == KT - 1)
                    if k == KT - 1:
                        mm.then_inc(bank_done, 1)
                if k < KT - 1:
                    mm.then_inc(step_done, 1)


def residual_product_norm(nc, name, cst, XR, HH, HL, w, ln, n_norm, XS, LNB, presplit=None, x_dram=None):
    RAW = 4
    with Phase(nc, name) as ph:
        sem = ph.sem
        WR = ph.sb("wr", [P, RAW, NW])
        WH, WL = ph.sb("wh", [P, KT, NW], F32R), ph.sb("wl", [P, KT, NW], F32R)
        SS, LG, RS = ph.sb("ss", [P, NT]), ph.sb("lg", [P, NT]), ph.sb("rs", [P, NT])
        bank = [ph.ps(f"acc{i}", [P, NW]) for i in range(NT)]
        w_loaded = [sem(f"w_loaded{i}") for i in range(RAW)]
        (w_hi, w_lo, row_done, bank_done, added, src_hi, src_lo, x_loaded, ln_loaded, squared, logged, rstd_ready,
         scaled, transposed, hi_ready, lo_ready) = (
            sem(s) for s in ("w_hi", "w_lo", "row_done", "bank_done", "added", "src_hi", "src_lo", "x_loaded",
                             "ln_loaded", "squared", "logged", "rstd", "scaled", "transposed", "hi", "lo"))
        block = ph.inner.enter_context(nc.Block())
        ph.clears(block)

        def tr_bank(i, g):
            return bank[i if g == 0 else max(i - 1, 0)]

        @block.sync
        def _(sp):
            sp.dma_start(LNB, ln.partition_broadcast(P)).then_inc(ln_loaded, 16)
            for s in range(2 * KT):
                c, k = divmod(s, KT)
                if s >= RAW:
                    sp.wait_ge(w_lo, s - RAW + 1)
                sp.dma_start(WR[:, s % RAW, :], w[k * P:(k + 1) * P, c * NW:(c + 1) * NW])\
                  .then_inc(w_loaded[s % RAW], 16)

        @block.scalar
        def _(act):
            act.preload_act_table_set(LN_EXP)
            for s in range(2 * KT):
                if presplit is not None and s < KT:
                    act.activation(HH[:, s, :], presplit[:, s, :], ACT.Copy).then_inc(src_hi, 1)
                if s == KT and x_dram is not None:
                    act.wait_ge(src_lo, KT)
                    act.dma_start(XR[:], x_dram.rearrange("(t p) d -> p t d", p=P)).then_inc(x_loaded, 16)
                act.wait_ge(w_loaded[s % RAW], 16 * (s // RAW + 1))
                if s >= KT:
                    act.wait_ge(row_done, s - KT + 1)
                act.activation(WH[:, s % KT, :], WR[:, s % RAW, :], ACT.Copy).then_inc(w_hi, 1)

            def stats(i):
                act.wait_ge(added, NT + i + 1)
                if i >= 2:
                    act.wait_ge(transposed, 2 * (i - 1))
                act.activation(XS[:, i % 2, :], XR[:, i, :], ACT.Square, accum_out=SS[:, i:i + 1]).then_inc(squared, 1)
                act.wait_ge(squared, i + 1)
                act.activation(LG[:, i:i + 1], SS[:, i:i + 1], ACT.Ln, scale=1.0 / D,
                               bias=cst["eps"]).then_inc(logged, 1)
                act.wait_ge(logged, i + 1)
                act.activation(RS[:, i:i + 1], LG[:, i:i + 1], ACT.Exp, scale=-0.5).then_inc(rstd_ready, 1)

            for j in range(n_norm + 2):
                if j >= 2:
                    for g in range(2):
                        i = j - 2
                        act.wait_ge(transposed, 2 * i + g + 1)
                        act.activation(HH[:, 4 * g:4 * g + 4, i * P:(i + 1) * P],
                                       tr_bank(i, g)[:].rearrange("p (a b) -> p a b", b=P), ACT.Copy).then_inc(hi_ready, 1)
                if j < n_norm:
                    stats(j)

        @block.vector
        def _(dve):
            def weight_lo(s):
                if presplit is not None and s < KT:
                    dve.wait_ge(src_hi, s + 1)
                    dve.tensor_tensor(HL[:, s, :], presplit[:, s, :], HH[:, s, :], ALU.subtract).then_inc(src_lo, 1)
                dve.wait_ge(w_hi, s + 1)
                dve.tensor_tensor(WL[:, s % KT, :], WR[:, s % RAW, :], WH[:, s % KT, :], ALU.subtract)\
                   .then_inc(w_lo, 1)

            def add(c, t):
                dve.wait_ge(bank_done, NT * c + t + 1)
                xs = XR[:, t, c * NW:(c + 1) * NW]
                dve.tensor_tensor(xs, bank[t][:], xs, ALU.add).then_inc(added, 1)

            for s in range(2 * KT - 1):
                weight_lo(s)
            if x_dram is not None:
                dve.wait_ge(x_loaded, 16)
            add(0, 0)
            weight_lo(2 * KT - 1)
            for t in range(1, NT):
                add(0, t)
            dve.wait_ge(ln_loaded, 16)
            for j in range(max(NT, n_norm + 2)):
                i = j - 1
                if 0 <= i < n_norm:
                    dve.wait_ge(rstd_ready, i + 1)
                    dve.scalar_tensor_tensor(XS[:, i % 2, :], XR[:, i, :], RS[:, i:i + 1], LNB,
                                             ALU.mult, ALU.mult).then_inc(scaled, 1)
                i = j - 2
                if 0 <= i < n_norm:
                    for g in range(2):
                        dve.wait_ge(hi_ready, 2 * i + g + 1)
                        hh = HH[:, 4 * g:4 * g + 4, i * P:(i + 1) * P]
                        dve.tensor_tensor(HL[:, 4 * g:4 * g + 4, i * P:(i + 1) * P],
                                          tr_bank(i, g)[:].rearrange("p (a b) -> p a b", b=P), hh, ALU.subtract)\
                           .then_inc(lo_ready, 1)
                if j < NT:
                    add(1, j)

        @block.tensor
        def _(pe):
            def row(c, k, t):
                tok = slice(t * P, (t + 1) * P)
                return split_matmuls(pe, bank[t][:], HH[:, k, tok], HL[:, k, tok], WH[:, k, :], WL[:, k, :],
                                     k == 0, k == KT - 1)

            def transposes(i, g):
                pe.wait_ge(scaled, i + 1)
                if g == 1:
                    pe.wait_ge(lo_ready, max(2 * i, 1))
                for k in range(4):
                    c = (4 * g + k) * P
                    last = pe.transpose(tr_bank(i, g)[:, k * P:(k + 1) * P], XS[:, i % 2, c:c + P], cst["ident"])
                last.then_inc(transposed, 1)

            for k in range(KT):
                if presplit is not None:
                    pe.wait_ge(src_lo, k + 1)
                pe.wait_ge(w_lo, k + 1)
                for t in range(NT):
                    mm = row(0, k, t)
                    if k == KT - 1:
                        mm.then_inc(bank_done, 1)
                        if t == NT - 1:
                            pe.wait_ge(bank_done, NT)
                            pe.nop().then_inc(row_done, 1)
                if k < KT - 1:
                    mm.then_inc(row_done, 1)
            for h in range(max(2 * NT, 2 * n_norm + 3)):
                t, half = divmod(h, 2)
                if t < NT:
                    if half == 0:
                        pe.wait_ge(added, t + 1)
                    for k in range(4 * half, 4 * half + 4):
                        if t == 0:
                            pe.wait_ge(w_lo, KT + k + 1)
                        mm = row(1, k, t)
                    if half == 1:
                        mm.then_inc(bank_done, 1)
                if 0 <= h - 3 < 2 * n_norm:
                    transposes(*divmod(h - 3, 2))


def head_norm_evac(nc, name, cst, OUT, n_tok, w_norm, scale, KN, wk_norm):
    HPC = NW // XA_DIM

    def make(ctx, sem, bank, bank_done, evacuated):
        n = n_tok * 2
        sb = lambda s, shape: ctx.enter_context(nc.sbuf_tensor(f"{name}_{s}", shape, F32))
        WB, WS, WK, SQ = (sb(s, [P, XA_DIM]) for s in ("wb", "ws", "wk", "sqv"))
        SS, LG, RS = (sb(s, [P, n, HPC]) for s in ("ss", "lg", "rs"))
        KSS, KLG, KRS = (sb(s, [P, 2, XA_HEADS]) for s in ("kss", "klg", "krs"))
        w_loaded, w_scaled, squared, logged, rstd = (sem(s) for s in ("nw", "nws", "sq", "lg", "rs"))
        k_squared, k_logged, k_rstd, k_normed = (sem(s) for s in ("ksq", "klg", "krs", "kn"))

        def act_start(eng):
            eng.dma_start(WB[:], w_norm.partition_broadcast(P)).then_inc(w_loaded, 16)
            eng.dma_start(WK[:], wk_norm.partition_broadcast(P)).then_inc(w_loaded, 16)

        def act_keys(eng):
            for t in range(2):
                for h in range(XA_HEADS):
                    eng.activation(SQ[:], KN[:, t, h * XA_DIM:(h + 1) * XA_DIM], ACT.Square,
                                   accum_out=KSS[:, t, h:h + 1]).then_inc(k_squared, 1)
                    eng.wait_ge(k_squared, XA_HEADS * t + h + 1)
            eng.activation(KLG[:], KSS[:], ACT.Ln, scale=1.0 / XA_DIM, bias=cst["eps"]).then_inc(k_logged, 1)
            eng.wait_ge(k_logged, 1)
            eng.activation(KRS[:], KLG[:], ACT.Exp, scale=-0.5).then_inc(k_rstd, 1)

        def dve_keys(eng):
            eng.wait_ge(w_loaded, 32)
            eng.tensor_scalar(WS[:], WB[:], scale, None, ALU.mult).then_inc(w_scaled, 1)
            eng.wait_ge(w_scaled, 1)
            eng.wait_ge(k_rstd, 1)
            for t in range(2):
                for h in range(XA_HEADS):
                    k = KN[:, t, h * XA_DIM:(h + 1) * XA_DIM]
                    eng.scalar_tensor_tensor(k, k, KRS[:, t, h:h + 1], WK[:], ALU.mult, ALU.mult).then_inc(k_normed, 1)

        def act(eng, c):
            for t in range(n_tok):
                u = n_tok * c + t
                eng.wait_ge(bank_done, u + 1)
                b = bank[(c % (8 // n_tok)) * n_tok + t]
                for h in range(HPC):
                    eng.activation(SQ[:], b[:, h * XA_DIM:(h + 1) * XA_DIM], ACT.Square,
                                   accum_out=SS[:, u, h:h + 1]).then_inc(squared, 1)
                    eng.wait_ge(squared, HPC * u + h + 1)
                eng.activation(LG[:, u, :], SS[:, u, :], ACT.Ln, scale=1.0 / XA_DIM, bias=cst["eps"]).then_inc(logged, 1)
                eng.wait_ge(logged, u + 1)
                eng.activation(RS[:, u, :], LG[:, u, :], ACT.Exp, scale=-0.5).then_inc(rstd, 1)

        def dve(eng, c):
            for t in range(n_tok):
                u = n_tok * c + t
                eng.wait_ge(rstd, u + 1)
                b = bank[(c % (8 // n_tok)) * n_tok + t]
                for h in range(HPC):
                    o = c * NW + h * XA_DIM
                    ins = eng.scalar_tensor_tensor(OUT[:, t, o:o + XA_DIM], b[:, h * XA_DIM:(h + 1) * XA_DIM],
                                                   RS[:, u, h:h + 1], WS[:], ALU.mult, ALU.mult)
                ins.then_inc(evacuated, 1)
        return {"act_start": act_start, "act": act, "dve": dve, "act_early": act_keys, "dve_early": dve_keys}
    return make


def memory_attention_block(nc, cst, QN, KN, V, OH, OL):
    with Phase(nc, "xa") as ph, ExitStack() as ctx:
        sem = ph.sem
        sb = lambda s, shape: ctx.enter_context(nc.sbuf_tensor(f"xa_{s}", shape, F32))
        KTR = sb("ktr", [P, KT, N_MEM])
        QT = sb("qt", [P, 2, KT, P])
        PR = sb("pr", [P, 2, XA_HEADS, N_MEM])
        PT = sb("pt", [P, 2, 2, XA_HEADS, P])
        NM = sb("nm", [P, NT, XA_HEADS])
        SM = sb("sm", [P, NT, XA_HEADS])
        RI = sb("ri", [P, NT, XA_HEADS])
        ps = lambda s: ctx.enter_context(nc.psum_tensor(f"xa_{s}", [P, 4, P], F32))
        q_bank, s_bank, p_bank, o_bank = ([ps(f"{s}{i}") for i in range(2)] for s in "qspo")
        k_tr, k_ready, q_tr, q_ready, scored, neg_max, expd, inv, normed, p_tr, p_ready, o_done, o_hi, o_lo = (
            sem(s) for s in ("k_tr", "k_ready", "q_tr", "q_ready", "scored", "neg_max", "expd", "inv", "normed",
                             "p_tr", "p_ready", "o_done", "o_hi", "o_lo"))
        block = ctx.enter_context(nc.Block())
        ph.clears(block)

        @block.tensor
        def _(pe):
            for u in range(4):
                if u >= 2:
                    pe.wait_ge(k_ready, u - 1)
                for j in range(4):
                    last = pe.transpose(q_bank[u % 2][:, j, :], KN[:, u // 2, ((u % 2) * 4 + j) * P:((u % 2) * 4 + j + 1) * P],
                                        cst["ident"])
                last.then_inc(k_tr, 1)

            def queries(i):
                for g in range(2):
                    if i == 0:
                        pe.wait_ge(k_ready, 3 + g)
                    else:
                        pe.wait_ge(q_ready, 2 * (i - 1) + g + 1)
                    for j in range(4):
                        c = (4 * g + j) * P
                        last = pe.transpose(q_bank[g][:, j, :], QN[:, i, c:c + P], cst["ident"])
                    last.then_inc(q_tr, 1)

            def scores(i):
                pe.wait_ge(q_ready, 2 * i + 2)
                for g in range(2):
                    if i >= 1:
                        pe.wait_ge(expd, 4 * (i - 1) + 2 * g + 2)
                    for hh in range(2):
                        h = 2 * g + hh
                        for kk in range(2):
                            mm = pe.matmul(s_bank[g][:].rearrange("p a b -> p (a b)")[:, hh * N_MEM:(hh + 1) * N_MEM],
                                           QT[:, i % 2, 2 * h + kk, :], KTR[:, 2 * h + kk, :],
                                           start=(kk == 0), stop=(kk == 1))
                    mm.then_inc(scored, 1)

            def transposes(i):
                pe.wait_ge(normed, i + 1)
                for m in range(2):
                    if i >= 1:
                        pe.wait_ge(p_ready, 2 * (i - 1) + m + 1)
                    for h in range(XA_HEADS):
                        last = pe.transpose(p_bank[m][:, h, :], PR[:, i % 2, h, m * P:(m + 1) * P], cst["ident"])
                    last.then_inc(p_tr, 1)

            def outputs(i):
                pe.wait_ge(p_ready, 2 * i + 2)
                for g in range(2):
                    if i >= 1:
                        pe.wait_ge(o_lo, 2 * (i - 1) + g + 1)
                    for j in range(4):
                        d = 4 * g + j
                        for m in range(2):
                            mm = pe.matmul(o_bank[g][:, j, :], V[:, m, d * P:(d + 1) * P], PT[:, i % 2, m, d // 2, :],
                                           start=(m == 0), stop=(m == 1))
                    mm.then_inc(o_done, 1)

            queries(0)
            for i in range(NT):
                scores(i)
                if i >= 1:
                    transposes(i - 1)
                if i + 1 < NT:
                    queries(i + 1)
                if i >= 1:
                    outputs(i - 1)
            transposes(NT - 1)
            outputs(NT - 1)

        @block.scalar
        def _(act):
            for u in range(4):
                act.wait_ge(k_tr, u + 1)
                act.activation(KTR[:, (u % 2) * 4:(u % 2) * 4 + 4, (u // 2) * P:(u // 2 + 1) * P], q_bank[u % 2][:],
                               ACT.Copy).then_inc(k_ready, 1)

            def queries(i):
                for g in range(2):
                    act.wait_ge(q_tr, 2 * i + g + 1)
                    if i >= 2:
                        act.wait_ge(scored, 2 * (i - 1))
                    act.activation(QT[:, i % 2, 4 * g:4 * g + 4, :], q_bank[g][:], ACT.Copy).then_inc(q_ready, 1)

            def exps(i):
                for g in range(2):
                    act.wait_ge(neg_max, 2 * i + g + 1)
                    if i >= 2:
                        act.wait_ge(p_tr, 2 * (i - 1))
                    for hh in range(2):
                        h = 2 * g + hh
                        act.activation(PR[:, i % 2, h, :], s_bank[g][:].rearrange("p a b -> p (a b)")[:, hh * N_MEM:(hh + 1) * N_MEM],
                                       ACT.Exp, bias=NM[:, i, h:h + 1], accum_out=SM[:, i, h:h + 1]).then_inc(expd, 1)

            def out_hi(i):
                for g in range(2):
                    act.wait_ge(o_done, 2 * i + g + 1)
                    act.activation(OH[:, 4 * g:4 * g + 4, i * P:(i + 1) * P], o_bank[g][:], ACT.Copy).then_inc(o_hi, 1)

            queries(0)
            for i in range(NT):
                exps(i)
                if i + 1 < NT:
                    queries(i + 1)
                if i >= 1:
                    out_hi(i - 1)
            out_hi(NT - 1)

        @block.vector
        def _(dve):
            def maxima(i):
                for g in range(2):
                    dve.wait_ge(scored, 2 * i + g + 1)
                    dve.tensor_reduce(NM[:, i, 2 * g:2 * g + 2],
                                      s_bank[g][:].rearrange("p (h a) b -> p h (a b)", h=2), AX.X, ALU.max,
                                      negate=True).then_inc(neg_max, 1)

            def normalise(i):
                dve.wait_ge(expd, 4 * i + 4)
                dve.reciprocal(RI[:, i, :], SM[:, i, :]).then_inc(inv, 1)
                dve.wait_ge(inv, i + 1)
                for h in range(XA_HEADS):
                    ins = dve.tensor_scalar(PR[:, i % 2, h, :], PR[:, i % 2, h, :], RI[:, i, h:h + 1], None, ALU.mult)
                ins.then_inc(normed, 1)

            def probabilities(i):
                for m in range(2):
                    dve.wait_ge(p_tr, 2 * i + m + 1)
                    if i >= 2:
                        dve.wait_ge(o_done, 2 * (i - 1))
                    dve.tensor_copy(PT[:, i % 2, m, :, :], p_bank[m][:]).then_inc(p_ready, 1)

            def out_lo(i):
                for g in range(2):
                    dve.wait_ge(o_hi, 2 * i + g + 1)
                    o = (slice(None), slice(4 * g, 4 * g + 4), slice(i * P, (i + 1) * P))
                    dve.tensor_tensor(OL[o], o_bank[g][:], OH[o], ALU.subtract).then_inc(o_lo, 1)

            for i in range(NT):
                maxima(i)
                if i >= 1:
                    probabilities(i - 1)
                normalise(i)
                if i >= 1:
                    out_lo(i - 1)
            probabilities(NT - 1)
            out_lo(NT - 1)


def ffn_block(nc, u, cst, XR, HH, HL, HALO, CW, CB, w_up, w_down, ln, out, stored):
    RAW, PART = 4, 3
    HT = T // 2
    NTH = HT // P
    UP = 2 * NF
    ITEMS = UP + 2 * NF
    with Phase(nc, f"ff{u}") as ph, ExitStack() as ctx:
        sem = ph.sem
        WR = ctx.enter_context(nc.sbuf_tensor(f"ff{u}_wr", [P, RAW, KT, P], F32))
        WH = ctx.enter_context(nc.sbuf_tensor(f"ff{u}_wh", [P, PART, KT, P], F32R))
        WL = ctx.enter_context(nc.sbuf_tensor(f"ff{u}_wl", [P, PART, KT, P], F32R))
        AH = ctx.enter_context(nc.sbuf_tensor(f"ff{u}_ah", [P, NF, HT], F32R))
        AX = ctx.enter_context(nc.sbuf_tensor(f"ff{u}_ax", [P, NF - 2 * KT, HT], F32R))
        XS = ctx.enter_context(nc.sbuf_tensor(f"ff{u}_xs", [P, 2, D], F32))
        LNB = ctx.enter_context(nc.sbuf_tensor(f"ff{u}_lnb", [P, D], F32))
        SS, LG, RS = (ctx.enter_context(nc.sbuf_tensor(f"ff{u}_{s}", [P, NTH], F32)) for s in ("ss", "lg", "rs"))
        G = ctx.enter_context(nc.sbuf_tensor(f"ff{u}_g", [P, HT + 2], F32))
        Y = XS[:, 0, :].rearrange("p (a b) -> p a b", b=HT)
        TH, AF = XS[:, 1, 0:HT], XS[:, 1, HT:2 * HT]
        bank = [ctx.enter_context(nc.psum_tensor(f"ff{u}_b{i}", [P, NW], F32)) for i in range(8)]
        w_loaded = [sem(f"w_loaded{i}") for i in range(RAW)]
        w_hi, w_lo, item_done, g_copied, g_scaled, halo_set, conv, tanh_ready, gated, act_f, act_hi, act_lo, evac = (
            sem(s) for s in ("w_hi", "w_lo", "item_done", "g_copied", "g_scaled", "halo", "conv", "tanh", "gated",
                             "act_f", "act_hi", "act_lo", "evac"))
        ln_loaded, squared, logged, rstd_ready, scaled, transposed, hi_ready, lo_ready = (
            sem(s) for s in ("ln_loaded", "squared", "logged", "rstd", "scaled", "transposed", "hi", "lo"))
        block = ctx.enter_context(nc.Block())
        ph.clears(block)

        def al(g):
            return AX[:, g - 2 * KT, :] if g >= 2 * KT else (HH, HL)[g // KT][:, g % KT, HT:T]

        def tr_bank(i, g):
            return bank[4 + i] if g == 0 else bank[4 + max(i - 1, 0)]

        norm_at = (lambda k, first: (k - first) // 4 if u == 0 and k >= first and (k - first) % 4 == 0
                   and (k - first) // 4 < NTH else None)

        def part(buf, ring, n):
            if n < UP:
                return buf[:, n % ring, :, :]
            return buf[:, n % ring, 0:NW // P, :]

        @block.sync
        def _(sp):
            if u == 0:
                sp.dma_start(LNB[:], ln.partition_broadcast(P)).then_inc(ln_loaded, 16)
            for n in range(ITEMS):
                if n >= RAW:
                    sp.wait_ge(w_lo, n - RAW + 1)
                if n < UP:
                    col = (n % 2) * D_FF + (n // 2) * P
                    src = w_up[:, col:col + P].rearrange("(k p) c -> p k c", p=P)
                else:
                    c, k = divmod(n - UP, NF)
                    src = w_down[k * P:(k + 1) * P, c * NW:(c + 1) * NW].rearrange("p (a b) -> p a b", b=P)
                sp.dma_start(part(WR, RAW, n), src).then_inc(w_loaded[n % RAW], 16)
            for c in range(2):
                for t in range(NTH):
                    row = (u * NTH + t) * P
                    sp.wait_ge(evac, c * NTH + t + 1)
                    sp.dma_start(out[row:row + P, c * NW:(c + 1) * NW], XR[:, u * NTH + t, c * NW:(c + 1) * NW])\
                      .then_inc(stored, 16)
            sp.wait_ge(stored, 16 * 2 * NTH * (u + 1))

        def hi(act, n):
            if n >= ITEMS:
                return
            act.wait_ge(w_loaded[n % RAW], 16 * (n // RAW + 1))
            if n >= PART:
                act.wait_ge(item_done, n - PART + 1)
            act.activation(part(WH, PART, n), part(WR, RAW, n), ACT.Copy).then_inc(w_hi, 1)

        def lo(dve, n):
            if n >= ITEMS:
                return
            dve.wait_ge(w_hi, n + 1)
            dve.tensor_tensor(part(WL, PART, n), part(WR, RAW, n), part(WH, PART, n), ALU.subtract).then_inc(w_lo, 1)

        @block.scalar
        def _(act):
            hi(act, 0)
            hi(act, 1)
            for f in range(NF + 1):
                hi(act, 2 * f + 2)
                if f >= 1:
                    g = f - 1
                    act.wait_ge(item_done, 2 * g + 1)
                    if g >= 1:
                        act.wait_ge(conv, 2 * g)
                        act.wait_ge(halo_set, 2 * g)
                    act.activation(G[:, 2:HT + 2], bank[(2 * g) % 4][:], ACT.Copy).then_inc(g_copied, 1)
                    if g >= 2:
                        act.wait_ge(gated, g - 1)
                    act.activation(Y[:, g % 2, :], bank[(2 * g) % 4][:], ACT.Identity, scale=CW[:, g, 2:3],
                                   bias=CB[:, g:g + 1]).then_inc(g_scaled, 1)
                hi(act, 2 * f + 3)
                if f >= 1:
                    act.wait_ge(conv, 2 * g + 2)
                    if g >= 1:
                        act.wait_ge(gated, g)
                    act.activation(TH, Y[:, g % 2, :], ACT.Tanh, scale=0.5).then_inc(tanh_ready, 1)
                    act.wait_ge(act_f, g + 1)
                    act.activation(AH[:, g, :], AF, ACT.Copy).then_inc(act_hi, 1)
            for n in range(2 * NF + 4, ITEMS):
                hi(act, n)
                k = n - UP - NF
                i = norm_at(k, 2)
                if i is not None:
                    if i == 0:
                        act.wait_ge(act_lo, NF)
                    if i >= 2:
                        act.wait_ge(transposed, 2 * (i - 1))
                    act.activation(XS[:, i % 2, :], XR[:, NTH + i, :], ACT.Square, accum_out=SS[:, i:i + 1])\
                       .then_inc(squared, 1)
                    act.wait_ge(squared, i + 1)
                    act.activation(LG[:, i:i + 1], SS[:, i:i + 1], ACT.Ln, scale=1.0 / D, bias=cst["eps"])\
                       .then_inc(logged, 1)
                    act.wait_ge(logged, i + 1)
                    act.activation(RS[:, i:i + 1], LG[:, i:i + 1], ACT.Exp, scale=-0.5).then_inc(rstd_ready, 1)
                for g in range(2):
                    i = norm_at(k, 6 + 2 * g)
                    if i is not None:
                        act.wait_ge(transposed, 2 * i + g + 1)
                        act.activation(HH[:, 4 * g:4 * g + 4, i * P:(i + 1) * P],
                                       tr_bank(i, g)[:].rearrange("p (a b) -> p a b", b=P), ACT.Copy).then_inc(hi_ready, 1)

        @block.vector
        def _(dve):
            lo(dve, 0)
            lo(dve, 1)
            for f in range(NF + 1):
                lo(dve, 2 * f + 2)
                if f >= 1:
                    g = f - 1
                    if u == 0 and g == 0:
                        dve.memset(G[:, 0:2], 0.0).then_inc(halo_set, 1)
                    elif u == 0:
                        dve.nop().then_inc(halo_set, 1)
                    else:
                        if g >= 1:
                            dve.wait_ge(conv, 2 * g)
                        dve.tensor_copy(G[:, 0:2], HALO[:, g, :]).then_inc(halo_set, 1)
                    dve.wait_ge(halo_set, 2 * g + 1)
                    dve.wait_ge(g_copied, g + 1)
                    dve.wait_ge(g_scaled, g + 1)
                    y = Y[:, g % 2, :]
                    dve.scalar_tensor_tensor(y, G[:, 1:HT + 1], CW[:, g, 1:2], y, ALU.mult, ALU.add).then_inc(conv, 1)
                    dve.wait_ge(conv, 2 * g + 1)
                    dve.scalar_tensor_tensor(y, G[:, 0:HT], CW[:, g, 0:1], y, ALU.mult, ALU.add).then_inc(conv, 1)
                    if u == 0:
                        dve.tensor_copy(HALO[:, g, :], G[:, HT:HT + 2]).then_inc(halo_set, 1)
                    else:
                        dve.nop().then_inc(halo_set, 1)
                lo(dve, 2 * f + 3)
                if f >= 1:
                    dve.wait_ge(tanh_ready, g + 1)
                    dve.scalar_tensor_tensor(y, TH, 1.0, y, ALU.add, ALU.mult).then_inc(gated, 1)
                    dve.wait_ge(gated, g + 1)
                    dve.wait_ge(item_done, 2 * g + 2)
                    dve.scalar_tensor_tensor(AF, y, 0.5, bank[(2 * g + 1) % 4][:], ALU.mult, ALU.mult)\
                       .then_inc(act_f, 1)
                    dve.wait_ge(act_f, g + 1)
                    dve.wait_ge(act_hi, g + 1)
                    dve.tensor_tensor(al(g), AF, AH[:, g, :], ALU.subtract).then_inc(act_lo, 1)

            def residual(c):
                dve.wait_ge(item_done, UP + NF * (c + 1))
                for t in range(NTH):
                    xs = XR[:, u * NTH + t, c * NW:(c + 1) * NW]
                    dve.tensor_tensor(xs, bank[4 * (1 - c) + t][:], xs, ALU.add).then_inc(evac, 1)

            for n in range(2 * NF + 4, ITEMS):
                lo(dve, n)
                if n == UP + NF + 1:
                    residual(0)
                k = n - UP - NF
                i = norm_at(k, 3)
                if i is not None:
                    if i == 0:
                        dve.wait_ge(ln_loaded, 16)
                    dve.wait_ge(rstd_ready, i + 1)
                    dve.scalar_tensor_tensor(XS[:, i % 2, :], XR[:, NTH + i, :], RS[:, i:i + 1], LNB[:],
                                             ALU.mult, ALU.mult).then_inc(scaled, 1)
                for g in range(2):
                    i = norm_at(k, 7 + 2 * g)
                    if i is not None:
                        dve.wait_ge(hi_ready, 2 * i + g + 1)
                        hh = HH[:, 4 * g:4 * g + 4, i * P:(i + 1) * P]
                        dve.tensor_tensor(HL[:, 4 * g:4 * g + 4, i * P:(i + 1) * P],
                                          tr_bank(i, g)[:].rearrange("p (a b) -> p a b", b=P), hh, ALU.subtract)\
                           .then_inc(lo_ready, 1)
            residual(1)

        @block.tensor
        def _(pe):
            for n in range(UP):
                pe.wait_ge(w_lo, n + 1)
                if n >= 4:
                    pe.wait_ge(act_f if n % 2 else g_scaled, (n - 4) // 2 + 1)
                for k in range(KT):
                    mm = split_matmuls(pe, bank[n % 4][:], WH[:, n % PART, k, :], WL[:, n % PART, k, :],
                                       HH[:, k, 0:HT], HL[:, k, 0:HT], k == 0, k == KT - 1)
                mm.then_inc(item_done, 1)
            for n in range(UP, ITEMS):
                c, k = divmod(n - UP, NF)
                pe.wait_ge(w_lo, n + 1)
                if c == 0:
                    pe.wait_ge(act_lo, k + 1)
                for t in range(NTH):
                    tok = slice(t * P, (t + 1) * P)
                    mm = split_matmuls(pe, bank[4 * (1 - c) + t][:], AH[:, k, tok], al(k)[:, tok],
                                       part(WH, PART, n).rearrange("p a b -> p (a b)"),
                                       part(WL, PART, n).rearrange("p a b -> p (a b)"), k == 0, k == NF - 1)
                mm.then_inc(item_done, 1)
                for g in range(2):
                    i = norm_at(k, 4 + 2 * g) if c == 1 else None
                    if i is not None:
                        pe.wait_ge(scaled, i + 1)
                        pe.wait_ge(evac, NTH)
                        if g == 1:
                            pe.wait_ge(lo_ready, max(2 * i, 1))
                        for j in range(4):
                            col = (4 * g + j) * P
                            last = pe.transpose(tr_bank(i, g)[:, j * P:(j + 1) * P], XS[:, i % 2, col:col + P],
                                                cst["ident"])
                        last.then_inc(transposed, 1)


NEG = -1e30
N_PAR = 7 + 4 + 10 + 4

OFF_FOX, OFF_FF = 0, 768
OFF_SZ, OFF_SX, OFF_DT = 772, 1028, 1540
OFF_GQ, OFF_GV, OFF_GA, OFF_GR = 1544, 1800, 2056, 2072
OFF_HQ = 2328
FOX_ITEMS = [OFF_FOX + P * j for j in range(6)]
SSD_ITEMS = [OFF_SZ + P * j for j in range(2)] + [OFF_SX + P * j for j in range(4)]
GLA_ITEMS = [OFF_GQ + P * j for j in range(4)] + [OFF_GR + P * j for j in range(2)]
HGRN_ITEMS = [OFF_HQ + P * j for j in range(8)]
COLS = [None] + HGRN_ITEMS + FOX_ITEMS + SSD_ITEMS + GLA_ITEMS
N_ITEMS = len(COLS)
H0, F0, S0, G0 = 1, 9, 15, 21
PAD = 4
SW = PAD + T
SMALL, W1, A, B = 0, 1, 2, 8
MX0 = 16
SLOT_OF = [SMALL] + [B + j for j in range(8)] + [MX0 + j for j in range(6)] + [B + j for j in range(6)] + [A + j for j in range(6)]
DT_ROW, GA_ROW = 32, 64
CH_GLA, CH_HGRN = 64, 16


def spread(first, last, counts):
    out, m = [], first
    for c in counts:
        out.append((m, m + c))
        m += c
    assert m == last
    return out


_HG = spread(2 * F0, 2 * S0, [2, 2, 2, 2] + [1, 1, 1, 1, 0, 0, 0, 0])
HG_PREP, HG_TILE = _HG[:4], _HG[4:]
_FX = spread(2 * S0, 2 * G0, [1] * 6 + [1 if n in (4, 9, 14, 20, 25, 30) else 0 for n in range(33)])
FOX_PRE, FOX_UNIT = _FX[:6], _FX[6:]
_SD = spread(2 * G0, 2 * N_ITEMS, [2, 2, 1, 1] + [1] * 6 + [0] * 2)
SSD_CONV, SSD_CHUNK = _SD[:4], _SD[4:]


KV_ITEMS = 4 * KT // 2
MEM_STATS, MEM_TR = NT - 3, NT - 2


def mixers_block(nc, cst, a, SL, MX, HH, HL):
    RAW, PART = 2, 2
    ident, eps, one = cst["ident"], cst["eps"], cst["one"]
    with Phase(nc, "mix") as ph:
        sem, sb = ph.sem, ph.sb
        WR = sb("wr", [P, RAW, KT, P])
        WH = sb("wh", [P, PART, KT, P], F32R)
        WL = sb("wl", [P, PART, KT, P], F32R)
        R10 = sb("scratch", [P, 2560])
        ST = sb("st", [P, NT, 3, 36])
        NEGQ = sb("negq", [P, P])
        NEGK = sb("negk", [P, P])
        M64 = sb("m64", [P, P])
        M16 = sb("m16", [P, P])
        BM = sb("bm", [P, 4, 64])
        BO64 = sb("bo64", [P, P])
        BO128 = sb("bo128", [P, P])
        HM4 = sb("hm4", [P, 4])
        HM2 = sb("hm2", [P, 2])
        CM8 = sb("cm8", [P, 8])
        PB = sb("pb", [P, 3])
        NWT = sb("nwt", [P, 8])
        CWS = sb("cws", [P, 4, 4])
        CBS = sb("cbs", [P, 4])
        DSK = sb("dsk", [P, 2])
        WG2 = sb("wg2", [P, P])
        BG2 = sb("bg2", [P, 1])
        NM = sb("nm", [P, 32])
        SUM = sb("sum", [P, 32])
        RIN = sb("rin", [P, 32])
        BT = sb("bt", [P, P])
        MST = sb("mst", [P, 3, 2])
        S_SSD = sb("s_ssd", [P, 4, 64])
        ED = sb("ed", [P, 2, 64])
        gb = [ph.ps(f"gb{i}", [P, NW]) for i in range(2)]
        M = [ph.ps(f"m{i}", [P, NW]) for i in range(6)]
        M3 = [m[:].rearrange("p (a b) -> p a b", b=P) for m in M]

        data = lambda s: SL[:, s, PAD:SW] if s < MX0 else MX[:, s - MX0, :]
        tile = lambda s, i: data(s)[:, i * P:(i + 1) * P]

        w_loaded = [sem(f"w_loaded{i}") for i in range(RAW)]
        made = {}

        def E(s):
            if s not in made:
                made[s] = sem(s)
            return made[s]

        def own(eng, s):
            count = [0]

            def link(ins):
                count[0] += 1
                ins.then_inc(E(s), 1)
                eng.wait_ge(E(s), count[0])
            return link

        def two_rows(buf, slot):
            return buf[:, slot, :, :].rearrange("p a b -> p (a b)").rearrange("p (k c) -> p k c", k=2)

        half = lambda ap, h: ap[:, h * NW:(h + 1) * NW]
        mx = lambda t: MX[:, t, :]
        VT = SL[:, A:A + 2, :].rearrange("p a b -> p (a b)")[:, 0:2 * T].rearrange("p (t c) -> p t c", c=256)
        SC = [data(A + 2), data(A + 3), data(A + 4)]
        CB = [data(A + 5), data(W1)]
        FQ, FK, FV = MX0, MX0 + 2, MX0 + 4
        PTS = [R10[:, NW * i:NW * (i + 1)] for i in range(3)]
        FOX_UNITS = [(hp, i, hh) for hp in range(2) for i in range(NT) for hh in range(2)]
        PIECES = [(n, c) for n, (hp, i, hh) in enumerate(FOX_UNITS) for c in range((i * P + P + NW - 1) // NW)]
        GROUPS = [(n, g) for n, (hp, i, hh) in enumerate(FOX_UNITS) for g in range(i // 4 + 1)]
        piece_of, group_of = {u: m for m, u in enumerate(PIECES)}, {u: m for m, u in enumerate(GROUPS)}
        scr = MX[:, 4:6, :].rearrange("p a b -> p (a b)")
        D_, SCD, EA = scr[:, 0:512], [scr[:, 512:1024], scr[:, 1024:1536]], scr[:, 1536:2048]
        CA, XDT, XDTE = data(W1)[:, 0:512], data(W1)[:, 512:768], data(W1)[:, 768:1024]
        CMC = [R10[:, 256 * i:256 * i + 256].rearrange("p (g t) -> p g t", g=2) for i in range(2)]
        QX = R10[:, 0:512].rearrange("p (h t) -> p h t", h=4)
        ATT = [R10[:, 512 + 512 * i:1024 + 512 * i].rearrange("p (h t) -> p h t", h=4) for i in range(2)]
        VK = [R10[:, 1536 + 512 * i:2048 + 512 * i].rearrange("p (a c) -> p a c", c=P) for i in range(2)]
        MEM_LN, MEM_SQ = R10[:, 512:1536], R10[:, 1536:2560]
        work = SL[:, W1:W1 + 5, :].rearrange("p a b -> p (a b)")
        VX = work[:, 0:2048].rearrange("p (h c d) -> p h c d", h=4, c=8)
        S_HG = work[:, 2048:2048 + 2304].rearrange("p (q c e) -> p q c e", q=2, c=9)
        UNITS = []

        def units(places, w, ones, sq, rs):
            for t, col in zip(places, w):
                UNITS.extend((half(data(t), h), col, ones, half(data(sq), h), half(data(rs), h)) for h in range(2))
        units((MX0 + 6, MX0 + 7), (6, 6), BO64, A + 4, A + 5)
        units((FQ, FQ + 1, FK, FK + 1), (0, 0, 1, 1), BO64, A + 2, A + 3)
        units((MX0, MX0 + 1), (2, 2), BO64, B + 6, B + 7)
        units((MX0 + 2, MX0 + 3), (3, 4), BO128, B + 6, B + 7)
        units((MX0 + 4, MX0 + 5), (5, 5), BO64, B + 6, B + 7)
        block = ph.inner.enter_context(nc.Block())

        @block.sync
        def _(sp):
            w = a["w_in"][0]
            narrow = ((0, OFF_FF, 4), (DT_ROW, OFF_DT, 4), (GA_ROW, OFF_GA, 16))
            sp.wait_ge(E("zeroed"), 1)
            with nc.allow_non_contiguous_dma(reason="narrow column groups and parameter columns"):
                for row, off, n in narrow:
                    sp.dma_start(WR[:, 0, :, row:row + n], w[:, off:off + n].rearrange("(k p) c -> p k c", p=P))\
                      .then_inc(w_loaded[0], 16)
                for n in range(1, RAW):
                    sp.dma_start(WR[:, n, :, :], w[:, COLS[n]:COLS[n] + P].rearrange("(k p) c -> p k c", p=P))\
                      .then_inc(w_loaded[n], 16)
                col = lambda v: v.rearrange("(p o) -> p o", o=1)
                par = [(PB[0:4, 1:2], col(a["fox_f_bias"][0])), (PB[DT_ROW:DT_ROW + 4, 1:2], col(a["ssd_dt_bias"][0])),
                       (PB[DT_ROW:DT_ROW + 4, 2:3], col(a["ssd_a_log"][0])),
                       (WG2[GA_ROW:GA_ROW + 16, :], a["gla_w_g2"][0]), (BG2[:], col(a["gla_b_g2"][0])),
                       (CBS[:], a["ssd_conv_b"][0].rearrange("(t p) -> p t", p=P)),
                       (NWT[:, 3:5], a["ssd_norm"][0].rearrange("(t p) -> p t", p=P))]
                par += [(CWS[:, :, j], a["ssd_conv_w"][0, j].rearrange("(t p) -> p t", p=P)) for j in range(4)]
                for b in range(2):
                    par += [(NWT[64 * b:64 * b + 64, c:c + 1], col(a[k][0])) for c, k in
                            ((0, "fox_qn"), (1, "fox_kn"), (2, "fox_on"), (5, "gla_norm"), (6, "hgrn_norm"))]
                for h in range(4):
                    par.append((DSK[64 * (h % 2):64 * (h % 2) + 64, h // 2:h // 2 + 1],
                                a["ssd_d"][0, h:h + 1].rearrange("(p o) -> p o", o=1).to_broadcast([64, 1])))
                for dst, src in par:
                    sp.dma_start(dst, src).then_inc(E("params"), 16)
                assert len(par) == N_PAR
            for n in range(RAW, N_ITEMS):
                sp.wait_ge(E("g_lo"), n - RAW + 1)
                sp.dma_start(WR[:, n % RAW, :, :], w[:, COLS[n]:COLS[n] + P].rearrange("(k p) c -> p k c", p=P))\
                  .then_inc(w_loaded[n % RAW], 16)
            for j in range(KV_ITEMS):
                n, (c, kk) = N_ITEMS + j, divmod(j, KT // 2)
                if j == 0:
                    sp.wait_ge(E("conv_out"), 4)
                    for t in range(2):
                        sp.dma_start(data(B + 6 + t), a["mem"][0, t * P:(t + 1) * P, :]).then_inc(E("mem_loaded"), 16)
                    sp.dma_start(MEM_LN, a["mem_norm"].partition_broadcast(P)).then_inc(E("mem_loaded"), 16)
                sp.wait_ge(E("g_lo"), n - RAW + 1)
                sp.dma_start(two_rows(WR, n % RAW), a["xa_wkv"][0][2 * kk * P:2 * (kk + 1) * P, c * NW:(c + 1) * NW]
                             .rearrange("(k p) c -> p k c", p=P)).then_inc(w_loaded[n % RAW], 16)

        @block.gpsimd
        def _(pool):
            link = own(pool, "pool_own")
            link(pool.memset(WR[:, 0, :, :], 0.0))
            link(pool.memset(PB[:], 1.0))
            link(pool.memset(PB[:, 1:2], 0.0))
            link(pool.memset(PB[DT_ROW:64, 0:1], -1.0))
            pool.memset(WG2[:], 0.0).then_inc(E("zeroed"), 1)
            ph.clear_done(pool)
            pool.memset(SL[:, :, 0:PAD], 0.0).then_inc(E("pads"), 1)
            pool.wait_ge(E("pads"), 1)
            pool.wait_ge(E("zeroed"), 1)
            link(pool.memset(MX[0:64, 5, :], 1.0))
            pool.memset(MX[DT_ROW:64, 5, 0:T:P], 0.0).then_inc(E("restart"), 1)
            pool.wait_ge(E("restart"), 1)
            for m, v in ((NEGQ, 0.0), (NEGK, 0.0), (M64, 1.0), (M16, 1.0), (BM, 1.0), (BO64, 1.0 / 64), (HM4, 1.0),
                         (HM2, 1.0), (CM8, 1.0)):
                link(pool.memset(m[:], v))
            link(pool.memset(BO128[:], 1.0 / P))

            def keep(m, cond, base, pattern, mult, fill=0.0):
                link(pool.affine_select(out=m, in_=m, compare_op=cond, fill=fill, base=base, pattern=pattern,
                                        channel_multiplier=mult))
            keep(NEGQ[:], ALU.is_ge, 0, [[-1, P]], 1, NEG)
            keep(NEGK[:], ALU.is_ge, 0, [[1, P]], -1, NEG)
            for m, ch in ((M64, CH_GLA), (M16, CH_HGRN)):
                v = m[:].rearrange("p (c i) -> p c i", i=ch)
                keep(m[:], ALU.is_ge, 0, [[1, P]], -1)
                keep(v, ALU.is_ge, 0, [[-ch, P // ch], [0, ch]], 1)
            for m, n in ((BM, 4), (BO64, 2)):
                w = P // n
                v = m[:] if m is BM else m[:].rearrange("p (h d) -> p h d", h=n)
                keep(v, ALU.is_ge, 0, [[-w, n], [0, 64]], 1)
                keep(v, ALU.is_ge, w - 1, [[w, n], [0, 64]], -1)
            for m, n in ((HM4, 4), (HM2, 2), (CM8, 8)):
                w = P // n
                keep(m[:], ALU.is_ge, 0, [[-w, n]], 1)
                keep(m[:], ALU.is_ge, w - 1, [[w, n]], -1)
            pool.memset(S_SSD[:], 0.0).then_inc(E("masks"), 1)
            pool.memset(R10[:, 512:1536], 0.0).then_inc(E("att_zero"), 1)
            pool.wait_ge(E("h_prep"), 2)
            pool.memset(work[:, 2048:2048 + 2304], 0.0).then_inc(E("s_zero"), 1)
            for i in range(NT):
                if i >= 1:
                    pool.wait_ge(E("h_att"), i)
                for p in range(2):
                    pool.tensor_tensor(QX[:, 2 * p:2 * p + 2, :], tile(B + p, i).unsqueeze(1).to_broadcast([P, 2, P]),
                                       HM2[:].unsqueeze(2).to_broadcast([P, 2, P]), ALU.mult).then_inc(E("h_qx"), 1)
                pool.wait_ge(E("h_vk"), i + 1)
                for h in range(4):
                    if i >= 1:
                        pool.wait_ge(E("h_ds"), 4 * (i - 1) + h + 1)
                    v = VK[i % 2][:, h // 2, 64 * (h % 2):64 * (h % 2) + 64]
                    pool.tensor_tensor(VX[:, h, :, :], v.unsqueeze(1).to_broadcast([P, 8, 64]),
                                       CM8[:].unsqueeze(2).to_broadcast([P, 8, 64]), ALU.mult).then_inc(E("h_vx"), 1)
            pool.wait_ge(E("mixed"), 2)
            link(pool.memset(R10[:, 0:512], 0.0))
            pool.wait_ge(E("conv_out"), 4)
            for c in range(NT):
                if c >= 2:
                    pool.wait_ge(E("s_g"), c - 1)
                for g in range(2):
                    q = slice(64 * g, 64 * g + 64)
                    pool.tensor_copy(CMC[c % 2][q, g, :], tile(B + 5, c)[q, :]).then_inc(E("cmc"), 1)
                    pool.wait_ge(E("cmc"), 2 * c + g + 1)
            pool.wait_ge(E("mixed"), 3)
            pool.memset(R10[:, 512:1536], 0.0).then_inc(E("att_zero"), 1)
            pool.wait_ge(E("gla_q"), 1)
            for i in range(NT):
                if i >= 1:
                    pool.wait_ge(E("a_att"), i)
                pool.tensor_tensor(QX, tile(A, i).unsqueeze(1).to_broadcast([P, 4, P]),
                                   HM4[:].unsqueeze(2).to_broadcast([P, 4, P]), ALU.mult).then_inc(E("a_qx"), 1)

        @block.scalar
        def _(act):
            link = own(act, "act_own")
            act.preload_act_table_set(LN_EXP)

            def hi(n):
                if n >= N_ITEMS + KV_ITEMS:
                    return
                act.wait_ge(w_loaded[n % RAW], 16 * (n // RAW + (3 if n % RAW == 0 else 1)))
                if n >= PART:
                    act.wait_ge(E("g_mm"), 2 * (n - PART) + 2)
                act.activation(WH[:, n % PART, :, :], WR[:, n % RAW, :, :], ACT.Copy).then_inc(E("g_hi"), 1)

            next_out = [0]

            def copy_out(upto):
                while next_out[0] < upto:
                    n, h = divmod(next_out[0], 2)
                    if h == 0 and n == G0:
                        act.wait_ge(E("mixed"), 2)
                    act.wait_ge(E("g_mm"), 2 * n + h + 1)
                    act.activation(half(data(SLOT_OF[n]), h), gb[h][:], ACT.Copy).then_inc(E("g_ev"), 1)
                    next_out[0] += 1

            def halves(m0, m1):
                for m in range(m0, m1):
                    copy_out(m)
                    if m % 2 == 0:
                        hi(m // 2 + 1)

            def items(n0, n1):
                halves(2 * n0, 2 * n1)
                copy_out(2 * n1)

            def kv_out(c):
                for t in range(2):
                    act.wait_ge(E("g_mm"), 2 * (N_ITEMS + (c + 1) * KT // 2) - 1 + t)
                    act.activation(half(data(B + 2 * (c // 2) + t), c % 2), gb[t][:], ACT.Copy).then_inc(E("g_ev"), 1)

            def kv(j0, j1):
                for j in range(j0, j1):
                    if j % (KT // 2) == 0 and j:
                        kv_out(j // (KT // 2) - 1)
                    hi(N_ITEMS + j + 1)

            def memory_stats():
                act.preload_act_table_set(LN_EXP)
                act.wait_ge(E("mem_loaded"), 48)
                for t in range(2):
                    link(act.activation(MEM_SQ, data(B + 6 + t), ACT.Square, accum_out=MST[:, 0, t:t + 1]))
                link(act.activation(MST[:, 1, :], MST[:, 0, :], ACT.Ln, scale=1.0 / D, bias=eps))
                act.activation(MST[:, 2, :], MST[:, 1, :], ACT.Exp, scale=-0.5).then_inc(E("mem_rs"), 1)

            def memory_hi(t):
                for g in range(2):
                    act.wait_ge(E("mem_tr"), 2 * t + g + 1)
                    act.activation(HH[:, 4 * g:4 * g + 4, t * P:(t + 1) * P], gb[g][:].rearrange("p (a b) -> p a b", b=P),
                                   ACT.Copy).then_inc(E("mem_hi"), 1)

            def squares(u):
                src, _, _, sq, _ = UNITS[u]
                if u >= 2:
                    act.wait_ge(E("n_ms"), u - 1)
                act.activation(sq, src, ACT.Square).then_inc(E("n_sq"), 1)

            def rstd(u):
                act.wait_ge(E("n_ms"), u + 1)
                if u >= 2:
                    act.wait_ge(E("n_out"), u - 1)
                rs = UNITS[u][4]
                act.activation(rs, M[4 + u % 2][:], ACT.Ln, bias=eps).then_inc(E("n_ln"), 1)
                act.wait_ge(E("n_ln"), u + 1)
                act.activation(rs, rs, ACT.Exp, scale=-0.5).then_inc(E("n_rs"), 1)

            def norms(u0, u1):
                squares(u0)
                for u in range(u0, u1):
                    if u + 1 < u1:
                        squares(u + 1)
                    rstd(u)

            hi(0)
            items(0, 1)
            act.wait_ge(E("params"), 16 * N_PAR)
            act.activation(PB[DT_ROW:DT_ROW + 4, 2:3], PB[DT_ROW:DT_ROW + 4, 2:3], ACT.Exp).then_inc(E("sm_a"), 1)
            act.wait_ge(E("sm_abs"), 1)
            link(act.activation(MX[0:64, 6, :], MX[0:64, 4, :], ACT.Exp, scale=-1.0))
            act.activation(MX[0:64, 6, :], MX[0:64, 6, :], ACT.Ln, bias=one[0:64, :]).then_inc(E("sm_ln"), 1)
            act.wait_ge(E("sm_te"), 1)
            act.activation(MX[0:64, 4, :], MX[0:64, 4, :], ACT.Exp).then_inc(E("sm_we"), 1)
            for i in range(NT):
                act.wait_ge(E("st_tr"), i + 1)
                act.activation(ST[:, i, :, :], M3[i % 2][:, 0:3, 0:36], ACT.Copy).then_inc(E("st_ev"), 1)

            def gate(k, z, th):
                act.activation(th, z, ACT.Tanh, scale=0.5).then_inc(E("gate_th"), 1)

            items(H0, F0)
            a0, a1, a2 = data(A), data(A + 1), data(A + 2)
            act.preload_act_table_set(LN_EXP)
            for p in range(2):
                halves(*HG_PREP[2 * p])
                act.wait_ge(E("hg_abs"), p + 1)
                link(act.activation(a0, a0, ACT.Exp, scale=-1.0))
                act.activation(a0, a0, ACT.Ln, bias=one).then_inc(E("hg_ln"), 1)
                act.wait_ge(E("hg_cum"), p + 1)
                act.activation(data(B + 2 + p), data(B + 2 + p), ACT.Exp).then_inc(E("hg_k"), 1)
                act.activation(a0, a2, ACT.Exp).then_inc(E("hg_e1"), 1)
                halves(*HG_PREP[2 * p + 1])
                act.wait_ge(E("hg_q"), p + 1)
                act.activation(a0, a2, ACT.Exp, scale=-1.0).then_inc(E("hg_e2"), 1)
                act.wait_ge(E("hg_te"), p + 1)
                act.activation(a2, a2, ACT.Exp).then_inc(E("hg_e3"), 1)
            for i in range(NT):
                act.wait_ge(E("h_tr"), i + 1)
                if i >= 2:
                    act.wait_ge(E("h_y"), 2 * (i - 1))
                act.activation(VK[i % 2], M3[0], ACT.Copy).then_inc(E("h_vk"), 1)
                if i >= 1:
                    halves(*HG_TILE[i - 1])
                    act.wait_ge(E("h_y"), 2 * i)
                    act.activation(MX[:, 6:8, (i - 1) * P:i * P], M3[0][:, 0:2, :], ACT.Copy)\
                       .then_inc(E("h_yev"), 1)
            halves(*HG_TILE[NT - 1])
            act.wait_ge(E("h_y"), 2 * NT)
            link(act.activation(MX[:, 6:8, (NT - 1) * P:], M3[0][:, 0:2, :], ACT.Copy))
            copy_out(2 * S0)
            act.wait_ge(E("h_s"), 32 * NT)
            act.preload_act_table_set(LN_EXP)
            squares(0)
            squares(1)
            for j in range(6):
                rstd(2 * j)
                rstd(2 * j + 1)
                if j < 5:
                    squares(2 * j + 2)
                    squares(2 * j + 3)
                halves(*FOX_PRE[j])
                for i in (2 * j, 2 * j + 1):
                    if i < NT:
                        act.wait_ge(E("vt_tr"), i + 1)
                        act.activation(VT[:, i, :], M[2 + i % 2][:, 0:256], ACT.Copy).then_inc(E("vt_ev"), 1)
            for p in range(2):
                gate(p, data(B + 6 + p), data(FV + p))


            def cum_rows(hp):
                if hp:
                    act.wait_ge(E("sc_read"), len(PIECES) // 2)
                for hh in range(2):
                    for h in range(2):
                        act.wait_ge(E("cb_mm"), 4 * hp + 2 * hh + h + 1)
                        act.activation(half(CB[hh], h), M[3 + h][:], ACT.Copy).then_inc(E("cb_ev"), 1)

            def fox_exp(n):
                hp, i, hh = FOX_UNITS[n]
                act.wait_ge(E("neg_max"), n + 1)
                act.activation(SC[n % 3][:, 0:(i + 1) * P], SC[n % 3][:, 0:(i + 1) * P], ACT.Exp,
                               bias=NM[:, n:n + 1], accum_out=SUM[:, n:n + 1]).then_inc(E("expd"), 1)

            def fox_out(n):
                hp, i, hh = FOX_UNITS[n]
                for g in range(i // 4 + 1):
                    m = group_of[(n, g)]
                    w = (min(4 * g + 4, i + 1) - 4 * g) * P
                    act.wait_ge(E("p_tr"), m + 1)
                    if m >= 3:
                        act.wait_ge(E("av_mm"), m - 2)
                    act.activation(PTS[m % 3][:, 0:w], M[3 + m % 2][:, 0:w], ACT.Copy).then_inc(E("p_ev"), 1)
                act.wait_ge(E("av_mm"), group_of[(n, i // 4)] + 1)
                r = slice(64 * hh, 64 * hh + 64)
                act.activation(MX[r, hp, i * P:(i + 1) * P], M[5][r, 0:P], ACT.Copy).then_inc(E("av_ev"), 1)

            for n in range(len(FOX_UNITS) + 1):
                if n % 16 == 0 and n < 32:
                    if n:
                        fox_out(n - 1)
                    cum_rows(n // 16)
                    fox_exp(n)
                    continue
                if n < 32:
                    fox_exp(n)
                halves(*FOX_UNIT[n])
                fox_out(n - 1)
            copy_out(2 * G0)
            act.wait_ge(E("mixed"), 1)
            act.preload_act_table_set(LN_EXP)
            norms(12, 16)

            act.wait_ge(E("mixed"), 2)
            for t in range(4):
                halves(*SSD_CONV[t])
                act.wait_ge(E("half_w"), 1)
                if t >= 2:
                    act.wait_ge(E("conv_out"), t - 1)
                y, th = mx(4 + t % 2), data(B + 6 + t % 2)
                act.activation(y, data(B + 2 + t), ACT.Identity, scale=CWS[:, t, 3:4], bias=CBS[:, t:t + 1])\
                   .then_inc(E("conv_in"), 1)
                act.wait_ge(E("conv_sum"), t + 1)
                act.activation(th, y, ACT.Tanh).then_inc(E("conv_th"), 1)
            for c in range(NT):
                halves(*SSD_CHUNK[c])
                if c == MEM_TR:
                    copy_out(2 * N_ITEMS)
                act.wait_ge(E("s_seg"), c + 1)
                if c >= 1:
                    act.wait_ge(E("s_upd"), c)
                act.activation(D_, D_, ACT.Exp).then_inc(E("s_dexp"), 1)
                act.activation(EA, M[2][:], ACT.Exp).then_inc(E("s_ea"), 1)
                if c == MEM_STATS:
                    memory_stats()
                if c >= MEM_TR:
                    memory_hi(c - MEM_TR)

            act.wait_ge(E("s_upd"), NT)
            act.wait_ge(E("s_yev"), NT)
            kv(0, 1)
            for p in range(2):
                gate(2 + p, data(B + p), data(B + 6 + p))
            kv(1, 2)
            act.wait_ge(E("gated"), 4)
            act.preload_act_table_set(LN_EXP)
            squares(16)
            squares(17)
            rstd(16)
            rstd(17)
            squares(18)
            squares(19)
            kv(2, 4)
            rstd(18)
            rstd(19)
            kv(4, 6)

            act.wait_ge(E("gl_abs"), 1)
            link(act.activation(data(B + 7), data(B + 7), ACT.Exp, scale=-1.0))
            act.activation(data(B + 7), data(B + 7), ACT.Ln, bias=one).then_inc(E("gl_ln"), 1)
            kv(6, 7)
            act.wait_ge(E("gl_cum"), 1)
            act.activation(data(B + 6), data(B + 7), ACT.Exp, scale=1.0 / 16).then_inc(E("gl_e1"), 1)
            kv(7, 8)
            act.wait_ge(E("gla_q"), 1)
            act.activation(data(B + 6), data(B + 7), ACT.Exp, scale=-1.0 / 16).then_inc(E("gl_e2"), 1)
            kv(8, 9)
            act.wait_ge(E("gl_te"), 1)
            act.activation(data(B + 7), data(B + 7), ACT.Exp, scale=1.0 / 16).then_inc(E("gl_e3"), 1)
            kv(9, 11)
            for i in range(NT):
                act.wait_ge(E("a_tr"), i + 1)
                if i >= 2:
                    act.wait_ge(E("a_y"), i - 1)
                act.activation(VK[i % 2][:, 0:3, :], M3[0][:, 0:3, :], ACT.Copy).then_inc(E("a_vk"), 1)
                if i >= 1:
                    act.wait_ge(E("a_y"), i)
                    act.activation(MX[:, 4:6, (i - 1) * P:i * P], M3[4 + (i - 1) % 2][:, 0:2, :], ACT.Copy)\
                       .then_inc(E("a_yev"), 1)
            kv(11, 12)
            act.wait_ge(E("a_y"), NT)
            link(act.activation(MX[:, 4:6, (NT - 1) * P:], M3[4 + (NT - 1) % 2][:, 0:2, :], ACT.Copy))
            act.wait_ge(E("a_s"), 2 * NT + 1)
            squares(20)
            squares(21)
            rstd(20)
            rstd(21)
            squares(22)
            squares(23)
            kv(12, 14)
            rstd(22)
            rstd(23)
            kv(14, 15)
            act.wait_ge(E("n_out"), 24)
            for p in range(2):
                gate(4 + p, data(A + 4 + p), data(B + 6 + p))
            kv_out(3)

        @block.vector
        def _(dve):
            link = own(dve, "dve_own")

            def halves(m0, m1):
                for m in range(m0, m1):
                    if m % 2 == 0:
                        lo(m // 2 + 1)

            def items(n0, n1):
                halves(2 * n0, 2 * n1)

            def lo(n):
                if n >= N_ITEMS + KV_ITEMS:
                    return
                dve.wait_ge(E("g_hi"), n + 1)
                dve.tensor_tensor(WL[:, n % PART, :, :], WR[:, n % RAW, :, :], WH[:, n % PART, :, :], ALU.subtract)\
                   .then_inc(E("g_lo"), 1)

            def kv(j0, j1):
                for j in range(j0, j1):
                    lo(N_ITEMS + j + 1)

            def norms(u0, u1):
                for u in range(u0, u1):
                    src, w, _, _, rs = UNITS[u]
                    dve.wait_ge(E("n_rs"), u + 1)
                    dve.scalar_tensor_tensor(src, src, NWT[:, w:w + 1], rs, ALU.mult, ALU.mult).then_inc(E("n_out"), 1)

            def gate(k, z, th, y):
                dve.wait_ge(E("gate_th"), k + 1)
                link(dve.scalar_tensor_tensor(z, th, 1.0, z, ALU.add, ALU.mult))
                dve.scalar_tensor_tensor(y, z, 0.5, y, ALU.mult, ALU.mult).then_inc(E("gated"), 1)

            lo(0)
            items(0, 1)
            r = slice(0, 64)
            x, t1, t2, e = (v[r] for v in (data(SMALL), data(W1), mx(4), mx(6)))
            dve.wait_ge(E("params"), 16 * N_PAR)
            link(dve.tensor_scalar(PB[DT_ROW:DT_ROW + 4, 1:2], PB[DT_ROW:DT_ROW + 4, 1:2], -1.0, None, ALU.mult))
            link(dve.tensor_scalar(NWT[:, 0:1], NWT[:, 0:1], 0.125, None, ALU.mult))
            link(dve.tensor_scalar(CWS[:], CWS[:], 0.5, None, ALU.mult))
            dve.tensor_scalar(CBS[:], CBS[:], 0.5, None, ALU.mult).then_inc(E("half_w"), 1)
            dve.wait_ge(E("g_ev"), 2)
            dve.wait_ge(E("pads"), 1)
            link(dve.tensor_scalar(t1, x, PB[r, 0:1], PB[r, 1:2], ALU.mult, ALU.add))
            dve.scalar_tensor_tensor(t2, t1, -1.0, t1, ALU.mult, ALU.max).then_inc(E("sm_abs"), 1)
            dve.wait_ge(E("sm_ln"), 1)
            dve.wait_ge(E("sm_a"), 1)
            link(dve.scalar_tensor_tensor(t1, t1, 0.0, e, ALU.min, ALU.subtract))
            link(dve.tensor_scalar(t2, t1, PB[r, 2:3], None, ALU.mult))
            dve.wait_ge(E("restart"), 1)
            link(dve.tensor_tensor_scan(x, MX[r, 5, :], t2, 0.0, ALU.mult, ALU.add))
            chunks = lambda v, ch: v.rearrange("p (c i) -> p c i", i=ch)
            ends = lambda v, ch: chunks(v, ch)[:, :, ch - 1:ch].to_broadcast([v.shape[0], T // ch, ch])
            dve.tensor_tensor(chunks(t2, P), ends(x, P), chunks(x, P), ALU.subtract).then_inc(E("sm_te"), 1)
            dve.wait_ge(E("sm_we"), 1)
            link(dve.scalar_tensor_tensor(t2, t1, -1.0, t2, ALU.mult, ALU.mult))
            dve.tensor_scalar(t1, t1, -1.0, None, ALU.mult).then_inc(E("sm_rows"), 1)

            items(H0, F0)
            a0, a1, a2, a3 = (data(A + j) for j in range(4))
            link(dve.memset(a3, 1.0))
            link(dve.memset(SL[:, A + 3, PAD:SW:CH_HGRN], 0.0))
            for p in range(2):
                z, q, kin = data(B + 2 + p), data(B + p), data(A + 4 + p)
                dve.wait_ge(E("g_ev"), 2 * F0)
                dve.scalar_tensor_tensor(a0, z, -1.0, z, ALU.mult, ALU.max).then_inc(E("hg_abs"), 1)
                halves(*HG_PREP[2 * p])
                dve.wait_ge(E("hg_ln"), p + 1)
                link(dve.scalar_tensor_tensor(a1, z, 0.0, a0, ALU.min, ALU.subtract))
                link(dve.tensor_tensor(z, a1, z, ALU.subtract))
                dve.tensor_tensor_scan(a2, a3, a1, 0.0, ALU.mult, ALU.add).then_inc(E("hg_cum"), 1)
                dve.wait_ge(E("hg_e1"), p + 1)
                link(dve.tensor_copy(ED[:, p, :], SL[:, A, PAD + CH_HGRN - 1:SW:CH_HGRN]))
                dve.tensor_tensor(q, q, a0, ALU.mult).then_inc(E("hg_q"), 1)
                halves(*HG_PREP[2 * p + 1])
                dve.wait_ge(E("hg_e2"), p + 1)
                link(dve.tensor_tensor(kin, z, a0, ALU.mult))
                link(dve.tensor_copy(a1[:, 0:64], SL[:, A + 2, PAD + CH_HGRN - 1:SW:CH_HGRN]))
                dve.tensor_tensor(chunks(a2, CH_HGRN), a1[:, 0:64].unsqueeze(2).to_broadcast([P, 64, CH_HGRN]),
                                  chunks(a2, CH_HGRN), ALU.subtract).then_inc(E("hg_te"), 1)
                dve.wait_ge(E("hg_e3"), p + 1)
                dve.tensor_tensor(z, z, a2, ALU.mult).then_inc(E("h_prep"), 1)
            dve.wait_ge(E("att_zero"), 1)
            dve.wait_ge(E("s_zero"), 1)
            for i in range(NT):
                dve.wait_ge(E("h_att"), i + 1)
                if i >= 2:
                    dve.wait_ge(E("h_y"), 2 * (i - 1))
                dve.copy_predicated(ATT[i % 2], M16[:].bitcast(mybir.dt.uint32).unsqueeze(1).to_broadcast([P, 4, P]),
                                    M3[1]).then_inc(E("h_am"), 1)
                halves(*HG_TILE[i])
                for p in range(2):
                    dve.wait_ge(E("h_ds"), 4 * i + 2 * p + 2)
                    if i >= 1:
                        dve.wait_ge(E("h_y"), 2 * (i - 1) + p + 1)
                    for c in range(8):
                        n = 8 * i + c
                        for hh in range(2):
                            q = slice(64 * hh, 64 * hh + 64)
                            m = 16 * (2 * i + p) + 2 * c + hh
                            if n >= 1 and c >= 1:
                                dve.wait_ge(E("h_s"), m - 1)
                            dve.scalar_tensor_tensor(S_HG[q, p, (n + 1) % 9, 64 * hh:64 * hh + 64],
                                                     S_HG[q, p, n % 9, 64 * hh:64 * hh + 64], ED[q, p, n:n + 1],
                                                     M[2 + 2 * p + hh][q, 64 * c:64 * c + 64], ALU.mult, ALU.add)\
                               .then_inc(E("h_s"), 1)
            for j in range(6):
                norms(2 * j, 2 * j + 2)
                halves(*FOX_PRE[j])
            for p in range(2):
                gate(p, data(B + 6 + p), data(FV + p), mx(6 + p))
            dve.wait_ge(E("gated"), 2)
            dve.nop().then_inc(E("mixed"), 1)

            dve.wait_ge(E("st_ev"), NT)
            dve.wait_ge(E("masks"), 1)

            def logits(n):
                hp, i, hh = FOX_UNITS[n]
                h, sc, keys = 2 * hp + hh, SC[n % 3], (i + 1) * P
                dve.wait_ge(E("cb_ev"), 4 * hp + 2 * hh + 2)
                if n >= 3:
                    dve.wait_ge(E("p_tr"), group_of[(n - 3, FOX_UNITS[n - 3][1] // 4)] + 1)
                for c in range((keys + NW - 1) // NW):
                    m, w = piece_of[(n, c)], min(NW, keys - c * NW)
                    dve.wait_ge(E("sc_mm"), m + 1)
                    dve.scalar_tensor_tensor(sc[:, c * NW:c * NW + w], M[m % 3][:, 0:w], ST[:, i, 0, h:h + 1],
                                             CB[hh][:, c * NW:c * NW + w], ALU.add, ALU.subtract).then_inc(E("sc_read"), 1)
                dve.wait_ge(E("sc_read"), m + 1)
                link(dve.tensor_tensor(sc[:, keys - P:keys], sc[:, keys - P:keys], NEGQ[:], ALU.add))
                dve.tensor_reduce(NM[:, n:n + 1], sc[:, 0:keys], AX.X, ALU.max, negate=True).then_inc(E("neg_max"), 1)

            def probabilities(n):
                sc, keys = SC[n % 3], (FOX_UNITS[n][1] + 1) * P
                dve.wait_ge(E("expd"), n + 1)
                link(dve.reciprocal(RIN[:, n:n + 1], SUM[:, n:n + 1]))
                dve.tensor_scalar(sc[:, 0:keys], sc[:, 0:keys], RIN[:, n:n + 1], None, ALU.mult).then_inc(E("probs"), 1)

            for n in range(33):
                if n < 32 and n % 16:
                    logits(n)
                halves(*FOX_UNIT[n])
                if n:
                    probabilities(n - 1)
                if n in (0, 16):
                    logits(n)
            norms(12, 16)
            dve.wait_ge(E("n_out"), 16)
            dve.wait_ge(E("av_ev"), 32)
            dve.nop().then_inc(E("mixed"), 1)

            for t in range(4):
                s = B + 2 + t
                y, th = mx(4 + t % 2), data(B + 6 + t % 2)
                halves(*SSD_CONV[t])
                dve.wait_ge(E("conv_in"), t + 1)
                for j in (2, 1):
                    link(dve.scalar_tensor_tensor(y, SL[:, s, PAD - 3 + j:PAD - 3 + j + T], CWS[:, t, j:j + 1], y,
                                                  ALU.mult, ALU.add))
                dve.scalar_tensor_tensor(y, SL[:, s, PAD - 3:PAD - 3 + T], CWS[:, t, 0:1], y, ALU.mult, ALU.add)\
                   .then_inc(E("conv_sum"), 1)
                dve.wait_ge(E("conv_th"), t + 1)
                dve.scalar_tensor_tensor(data(s), th, 1.0, y, ALU.add, ALU.mult).then_inc(E("conv_out"), 1)
            dve.wait_ge(E("conv_out"), 4)
            S = S_SSD
            for c in range(NT):
                sd = SCD[c % 2]
                halves(*SSD_CHUNK[c])
                dve.wait_ge(E("s_tr"), c + 1)
                if c >= 1:
                    dve.wait_ge(E("s_ds"), c)
                by_head = lambda v: v.rearrange("p (h d) -> p h d", h=4)
                rows = lambda k: ST[:, c, k, DT_ROW:DT_ROW + 4].unsqueeze(2)
                dve.tensor_tensor(by_head(XDT), by_head(M[0][:, 0:256]), rows(1).to_broadcast([P, 4, 64]), ALU.mult)\
                   .then_inc(E("s_x"), 1)
                dve.tensor_tensor(by_head(XDTE), by_head(M[0][:, 0:256]), rows(2).to_broadcast([P, 4, 64]), ALU.mult)\
                   .then_inc(E("s_x"), 1)
                dve.tensor_copy(BT[:], M[0][:, 256:384]).then_inc(E("s_x"), 1)
                dve.wait_ge(E("s_ab"), c + 1)
                link(dve.tensor_tensor(by_head(D_), M3[2], rows(0).to_broadcast([P, 4, P]), ALU.subtract))
                dve.tensor_tensor(by_head(D_), by_head(D_), NEGK[:].unsqueeze(1).to_broadcast([P, 4, P]), ALU.add)\
                   .then_inc(E("s_seg"), 1)
                dve.wait_ge(E("s_dexp"), c + 1)
                dve.wait_ge(E("s_g"), c + 1)
                for g in range(2):
                    v = slice(256 * g, 256 * g + 256)
                    dve.tensor_tensor(sd[:, v].rearrange("p (h t) -> p h t", h=2),
                                      M[1][:, P * g:P * g + P].unsqueeze(1).to_broadcast([P, 2, P]),
                                      D_[:, v].rearrange("p (h t) -> p h t", h=2), ALU.mult).then_inc(E("s_scd"), 1)
                dve.wait_ge(E("s_ea"), c + 1)
                dve.tensor_tensor(by_head(CA), tile(B + 5, c).unsqueeze(1).to_broadcast([P, 4, P]), by_head(EA),
                                  ALU.mult).then_inc(E("s_ca"), 1)
                dve.wait_ge(E("s_y"), c + 1)
                for p in range(2):
                    dve.scalar_tensor_tensor(MX[:, 2 + p, c * P:(c + 1) * P], tile(B + 2 + p, c), DSK[:, p:p + 1],
                                             M3[3][:, p, :], ALU.mult, ALU.add).then_inc(E("s_yp"), 1)
                dve.wait_ge(E("s_yp"), 2 * c + 2)
                dve.nop().then_inc(E("s_yev"), 1)
                dve.wait_ge(E("s_ds"), c + 1)
                for g in range(2):
                    q, hs = slice(64 * g, 64 * g + 64), slice(2 * g, 2 * g + 2)
                    end = by_head(EA)[q, hs, P - 1:P].to_broadcast([64, 2, 64])
                    link(dve.tensor_tensor(S[q, hs, :], S[q, hs, :], end, ALU.mult))
                    link(dve.tensor_tensor(S[q, hs, :], S[q, hs, :], M[5][q, 0:256].rearrange(
                        "p (h d) -> p h d", h=4)[:, hs, :], ALU.add))
                dve.nop().then_inc(E("s_upd"), 1)
                if c == MEM_STATS:
                    dve.wait_ge(E("mem_rs"), 1)
                    dve.wait_ge(E("mem_loaded"), 48)
                    for t in range(2):
                        m = data(B + 6 + t)
                        dve.scalar_tensor_tensor(m, m, MST[:, 2, t:t + 1], MEM_LN, ALU.mult, ALU.mult)\
                           .then_inc(E("mem_sc"), 1)
                    dve.wait_ge(E("mem_sc"), 2)
                if c >= MEM_TR:
                    t = c - MEM_TR
                    for g in range(2):
                        dve.wait_ge(E("mem_hi"), 2 * t + g + 1)
                        dve.tensor_tensor(HL[:, 4 * g:4 * g + 4, t * P:(t + 1) * P],
                                          gb[g][:].rearrange("p (a b) -> p a b", b=P),
                                          HH[:, 4 * g:4 * g + 4, t * P:(t + 1) * P], ALU.subtract).then_inc(E("mem_lo"), 1)
            kv(0, 1)
            gate(2, data(B), data(B + 6), mx(2))
            kv(1, 2)
            gate(3, data(B + 1), data(B + 7), mx(3))
            norms(16, 18)
            kv(2, 4)
            norms(18, 20)
            dve.wait_ge(E("n_out"), 20)
            dve.nop().then_inc(E("mixed"), 1)
            kv(4, 6)

            z, u, k, kin = data(B + 6), data(B + 7), data(A + 1), data(W1)
            for h in range(2):
                dve.wait_ge(E("gate_mm"), h + 1)
                link(dve.tensor_scalar(half(z, h), M[h][:], BG2[:], None, ALU.add))
            dve.scalar_tensor_tensor(u, z, -1.0, z, ALU.mult, ALU.max).then_inc(E("gl_abs"), 1)
            link(dve.memset(kin, 1.0))
            link(dve.memset(SL[:, W1, PAD:SW:CH_GLA], 0.0))
            dve.wait_ge(E("gl_ln"), 1)
            link(dve.scalar_tensor_tensor(z, z, 0.0, u, ALU.min, ALU.subtract))
            dve.tensor_tensor_scan(u, kin, z, 0.0, ALU.mult, ALU.add).then_inc(E("gl_cum"), 1)
            kv(6, 7)
            dve.wait_ge(E("gl_e1"), 1)
            dve.wait_ge(E("g_ev"), 2 * N_ITEMS)
            link(dve.tensor_copy(ED[:, 0, 0:16], SL[:, B + 6, PAD + CH_GLA - 1:SW:CH_GLA]))
            dve.scalar_tensor_tensor(data(A), data(A), 32.0 ** -0.5, z, ALU.mult, ALU.mult).then_inc(E("gla_q"), 1)
            kv(7, 8)
            dve.wait_ge(E("gl_e2"), 1)
            dve.tensor_tensor(kin, k, z, ALU.mult).then_inc(E("gl_kin"), 1)
            dve.wait_ge(E("gl_kin"), 1)
            link(dve.tensor_copy(z[:, 0:16], SL[:, B + 7, PAD + CH_GLA - 1:SW:CH_GLA]))
            dve.tensor_tensor(chunks(u, CH_GLA), z[:, 0:16].unsqueeze(2).to_broadcast([P, 16, CH_GLA]),
                              chunks(u, CH_GLA), ALU.subtract).then_inc(E("gl_te"), 1)
            kv(8, 9)
            dve.wait_ge(E("gl_e3"), 1)
            dve.tensor_tensor(k, k, u, ALU.mult).then_inc(E("gl_kend"), 1)
            kv(9, 11)
            S = lambda n: z[:, 256 * (n % 4):256 * (n % 4) + 256]
            DM = lambda n: u[:, 256 * (n % 2):256 * (n % 2) + 256]
            dve.wait_ge(E("gl_te"), 1)
            dve.wait_ge(E("gl_kend"), 1)
            dve.memset(S(0), 0.0).then_inc(E("a_s"), 1)
            dve.wait_ge(E("att_zero"), 2)
            for i in range(NT):
                dve.wait_ge(E("a_att"), i + 1)
                if i >= 2:
                    dve.wait_ge(E("a_y"), i - 1)
                dve.copy_predicated(ATT[i % 2], M64[:].bitcast(mybir.dt.uint32).unsqueeze(1).to_broadcast([P, 4, P]),
                                    M3[1]).then_inc(E("a_am"), 1)
                dve.wait_ge(E("a_ds"), i + 1)
                for c in range(2):
                    n = 2 * i + c
                    link(dve.tensor_tensor(DM(n), M[2 + c][:, 0:256], BM[:].rearrange("p h d -> p (h d)"), ALU.mult))
                    dve.wait_ge(E("a_s"), n + 1)
                    dve.scalar_tensor_tensor(S(n + 1), S(n), ED[:, 0, n:n + 1], DM(n), ALU.mult, ALU.add)\
                       .then_inc(E("a_s"), 1)
            kv(11, 12)
            norms(20, 22)
            kv(12, 14)
            norms(22, 24)
            kv(14, 15)
            for p in range(2):
                gate(4 + p, data(A + 4 + p), data(B + 6 + p), mx(4 + p))

        @block.tensor
        def _(pe):
            def halves(m0, m1):
                for m in range(m0, m1):
                    n, h = divmod(m, 2)
                    if h == 0:
                        pe.wait_ge(E("g_lo"), n + 1)
                    if n >= 1:
                        pe.wait_ge(E("g_ev"), m - 1)
                    for k in range(KT):
                        mm = split_matmuls(pe, gb[h][:], WH[:, n % PART, k, :], WL[:, n % PART, k, :],
                                           half(HH[:, k, :], h), half(HL[:, k, :], h), k == 0, k == KT - 1)
                    mm.then_inc(E("g_mm"), 1)

            def items(n0, n1):
                halves(2 * n0, 2 * n1)

            def kv(j0, j1):
                for j in range(j0, j1):
                    n, (c, kk) = N_ITEMS + j, divmod(j, KT // 2)
                    pe.wait_ge(E("g_lo"), n + 1)
                    if kk == 0:
                        pe.wait_ge(E("g_ev"), 2 * (N_ITEMS + c))
                    for t in range(2):
                        tok = slice(t * P, (t + 1) * P)
                        for b in range(2):
                            k = 2 * kk + b
                            mm = split_matmuls(pe, gb[t][:], HH[:, k, tok], HL[:, k, tok], two_rows(WH, n % PART)[:, b, :],
                                               two_rows(WL, n % PART)[:, b, :], k == 0, k == KT - 1)
                        mm.then_inc(E("g_mm"), 1)

            def norms(u0, u1):
                for u in range(u0, u1):
                    _, _, ones, sq, _ = UNITS[u]
                    pe.wait_ge(E("n_sq"), u + 1)
                    if u >= 2:
                        pe.wait_ge(E("n_ln"), u - 1)
                    pe.matmul(M[4 + u % 2][:], ones[:], sq, start=True, stop=True).then_inc(E("n_ms"), 1)

            def row(r):
                return ident[:, r:r + 1].to_broadcast([P, P])

            items(0, 1)
            halves(2, 4)
            pe.wait_ge(E("sm_rows"), 1)
            for i in range(NT):
                if i >= 2:
                    pe.wait_ge(E("st_ev"), i - 1)
                tok = slice(i * P, (i + 1) * P)
                for j, v in enumerate((data(SMALL), data(W1), mx(4))):
                    last = pe.transpose(M3[i % 2][:, j, 0:64], v[0:64, tok], ident[0:64, 0:64])
                last.then_inc(E("st_tr"), 1)

            halves(4, 2 * F0)
            for j in range(4):
                halves(*HG_PREP[j])
            pe.wait_ge(E("h_prep"), 2)

            def hgrn_scores(i):
                if i >= 1:
                    pe.wait_ge(E("h_vk"), i)
                if i >= 2:
                    pe.wait_ge(E("h_yev"), i - 1)
                for j in range(4):
                    last = pe.transpose(M3[0][:, j, :], tile((B + 4, B + 5, B + 2, B + 3)[j], i), ident)
                last.then_inc(E("h_tr"), 1)
                pe.wait_ge(E("h_qx"), 2 * i + 2)
                if i >= 1:
                    pe.wait_ge(E("h_am"), i)
                for p in range(2):
                    mm = pe.matmul(M[1][:, 256 * p:256 * p + 256], tile(A + 4 + p, i),
                                   QX[:, 2 * p:2 * p + 2, :].rearrange("p h t -> p (h t)"), start=True, stop=True)
                mm.then_inc(E("h_att"), 1)

            def hgrn_states(i, p):
                for h in (2 * p, 2 * p + 1):
                    pe.wait_ge(E("h_vx"), 4 * i + h + 1)
                    if i >= 1:
                        pe.wait_ge(E("h_s"), 16 * (2 * (i - 1) + p + 1))
                    pe.matmul(M[2 + h][:], VK[i % 2][:, 2 + p, :], VX[:, h, :, :].rearrange("p c d -> p (c d)"),
                              start=True, stop=True).then_inc(E("h_ds"), 1)

            def hgrn_outputs(i, p):
                vk = VK[i % 2]
                pe.wait_ge(E("h_am"), i + 1)
                pe.wait_ge(E("h_s"), 32 * i + 16 * p + 16)
                pe.wait_ge(E("h_vk"), min(i + 2, NT))
                if i >= 1:
                    pe.wait_ge(E("h_yev"), i)
                yb = M3[0]
                for hh in range(2):
                    pe.matmul(yb[64 * hh:64 * hh + 64, p, :], vk[:, p, 64 * hh:64 * hh + 64], ATT[i % 2][:, 2 * p + hh, :],
                              start=True, stop=False, skip_group_check=True)
                for c in range(8):
                    mm = pe.matmul(yb[:, p, 16 * c:16 * c + 16], S_HG[:, p, (8 * i + c) % 9, :],
                                   tile(B + p, i)[:, 16 * c:16 * c + 16], start=False, stop=True,
                                   skip_group_check=True)
                mm.then_inc(E("h_y"), 1)

            hgrn_scores(0)
            for p in range(2):
                hgrn_states(0, p)
            for i in range(NT):
                if i + 1 < NT:
                    hgrn_scores(i + 1)
                halves(*HG_TILE[i])
                for p in range(2):
                    hgrn_outputs(i, p)
                    if i + 1 < NT:
                        hgrn_states(i + 1, p)
            pe.wait_ge(E("g_ev"), 2 * S0)
            for j in range(6):
                norms(2 * j, 2 * j + 2)
                halves(*FOX_PRE[j])
                for i in (2 * j, 2 * j + 1):
                    if i >= NT:
                        continue
                    if i >= 2:
                        pe.wait_ge(E("vt_ev"), i - 1)
                    for v in range(2):
                        last = pe.transpose(M3[2 + i % 2][:, v, :], tile(FV + v, i), ident)
                    last.then_inc(E("vt_tr"), 1)


            def cum_rows(hp):
                for hh in range(2):
                    for h in range(2):
                        m = 4 * hp + 2 * hh + h
                        if hp:
                            pe.wait_ge(E("p_ev"), len(GROUPS) // 2)
                        elif m < 2:
                            pe.wait_ge(E("n_ln"), 12)
                        if m % 4 >= 2:
                            pe.wait_ge(E("cb_ev"), m - 1)
                        pe.matmul(M[3 + h][:], row(2 * hp + hh), half(data(SMALL), h), start=True, stop=True)\
                          .then_inc(E("cb_mm"), 1)

            def scores(n):
                hp, i, hh = FOX_UNITS[n]
                r, keys = slice(64 * hh, 64 * hh + 64), (i + 1) * P
                for c in range((keys + NW - 1) // NW):
                    m, w = piece_of[(n, c)], min(NW, keys - c * NW)
                    if m >= 3:
                        pe.wait_ge(E("sc_read"), m - 2)
                    pe.matmul(M[m % 3][:, 0:w], tile(FQ + hp, i)[r, :], data(FK + hp)[r, c * NW:c * NW + w],
                              start=True, stop=True).then_inc(E("sc_mm"), 1)

            def outputs(n):
                hp, i, hh = FOX_UNITS[n]
                r = slice(64 * hh, 64 * hh + 64)
                pe.wait_ge(E("probs"), n + 1)
                for g in range(i // 4 + 1):
                    m, kb = group_of[(n, g)], range(4 * g, min(4 * g + 4, i + 1))
                    if m >= 2:
                        pe.wait_ge(E("p_ev"), m - 1)
                    if m <= 1 or n == 16:
                        pe.wait_ge(E("cb_ev"), 4 * hp + 4)
                    for k in kb:
                        last = pe.transpose(M3[3 + m % 2][:, k % 4, :], SC[n % 3][:, k * P:(k + 1) * P], ident)
                    last.then_inc(E("p_tr"), 1)
                if n >= 1:
                    pe.wait_ge(E("av_ev"), n)
                for g in range(i // 4 + 1):
                    m, kb = group_of[(n, g)], range(4 * g, min(4 * g + 4, i + 1))
                    pe.wait_ge(E("p_ev"), m + 1)
                    for k in kb:
                        mm = pe.matmul(M[5][r, 0:P], VT[:, k, 128 * hp + 64 * hh:128 * hp + 64 * hh + 64],
                                       PTS[m % 3][:, (k % 4) * P:(k % 4 + 1) * P], start=(k == 0), stop=(k == i))
                    mm.then_inc(E("av_mm"), 1)

            pe.wait_ge(E("n_out"), 12)
            for n in range(33):
                if n % 16 == 0 and n < 32:
                    if n:
                        outputs(n - 1)
                    cum_rows(n // 16)
                    scores(n)
                    scores(n + 1)
                    continue
                if n < 32 and (n + 1) % 16:
                    scores(n + 1)
                halves(*FOX_UNIT[n])
                outputs(n - 1)
            norms(12, 16)

            pe.wait_ge(E("mixed"), 2)
            for t in range(4):
                halves(*SSD_CONV[t])
            pe.wait_ge(E("conv_out"), 4)
            def ssd_inputs(c):
                if c >= 1:
                    pe.wait_ge(E("s_x"), 3 * c)
                for j, s in enumerate((B + 2, B + 3, B + 4)):
                    last = pe.transpose(M3[0][:, j, :], tile(s, c), ident)
                last.then_inc(E("s_tr"), 1)
                if c >= 1:
                    pe.wait_ge(E("s_ea"), c)
                for h in range(4):
                    mm = pe.matmul(M3[2][:, h, :], row(DT_ROW + h), tile(SMALL, c), start=True, stop=True)
                mm.then_inc(E("s_ab"), 1)
                pe.wait_ge(E("cmc"), 2 * c + 2)
                if c >= 1:
                    pe.wait_ge(E("s_scd"), 2 * c)
                pe.matmul(M[1][:, 0:256], tile(B + 4, c), CMC[c % 2].rearrange("p g t -> p (g t)"),
                          start=True, stop=True).then_inc(E("s_g"), 1)

            ssd_inputs(0)
            for c in range(NT):
                halves(*SSD_CHUNK[c])
                if c >= MEM_TR:
                    t = c - MEM_TR
                    pe.wait_ge(E("mem_sc"), t + 1)
                    pe.wait_ge(E("g_ev"), 2 * N_ITEMS)
                    for g in range(2):
                        if t == 1:
                            pe.wait_ge(E("mem_lo"), g + 1)
                        for k in range(4):
                            last = pe.transpose(gb[g][:, k * P:(k + 1) * P], tile(B + 6 + t, 4 * g + k), ident)
                        last.then_inc(E("mem_tr"), 1)
                if c + 1 < NT:
                    ssd_inputs(c + 1)
                pe.wait_ge(E("s_x"), 3 * c + 3)
                pe.wait_ge(E("s_scd"), 2 * c + 2)
                pe.wait_ge(E("s_ca"), c + 1)
                if c >= 1:
                    pe.wait_ge(E("s_upd"), c)
                    pe.wait_ge(E("s_yev"), c)
                for h in range(4):
                    y = M3[3][64 * (h % 2):64 * (h % 2) + 64, h // 2, :]
                    pe.matmul(y, XDT[:, 64 * h:64 * h + 64], SCD[c % 2][:, P * h:P * h + P], start=True, stop=False,
                              skip_group_check=True)
                    mm = pe.matmul(y, S_SSD[:, h, :], CA[:, P * h:P * h + P], start=False, stop=True,
                                   skip_group_check=True)
                mm.then_inc(E("s_y"), 1)
                pe.matmul(M[5][:, 0:256], BT[:], XDTE, start=True, stop=True).then_inc(E("s_ds"), 1)
            pe.wait_ge(E("s_upd"), NT)
            for h in range(2):
                pe.matmul(M[h][:], WG2[:], half(data(SMALL), h), start=True, stop=True).then_inc(E("gate_mm"), 1)
            pe.wait_ge(E("mem_lo"), 4)
            kv(0, 2)
            norms(16, 18)
            kv(2, 4)
            norms(18, 20)
            kv(4, 6)

            kv(6, 11)
            pe.wait_ge(E("gl_kin"), 1)
            pe.wait_ge(E("gl_kend"), 1)

            def gla_scores(i):
                if i >= 1:
                    pe.wait_ge(E("a_vk"), i)
                for j in range(3):
                    last = pe.transpose(M3[0][:, j, :], tile((A + 2, A + 3, A + 1)[j], i), ident)
                last.then_inc(E("a_tr"), 1)
                pe.wait_ge(E("a_qx"), i + 1)
                if i >= 1:
                    pe.wait_ge(E("a_am"), i)
                pe.matmul(M[1][:], tile(W1, i), QX.rearrange("p h t -> p (h t)"), start=True, stop=True)\
                  .then_inc(E("a_att"), 1)

            def gla_states(i):
                pe.wait_ge(E("a_vk"), i + 1)
                if i >= 1:
                    pe.wait_ge(E("a_s"), 2 * i + 1)
                vk = VK[i % 2]
                for c in range(2):
                    q = slice(64 * c, 64 * c + 64)
                    mm = pe.matmul(M[2 + c][:, 0:256], vk[q, 2, :], vk[q, 0:2, :].rearrange("p a b -> p (a b)"),
                                   start=True, stop=True)
                mm.then_inc(E("a_ds"), 1)

            def gla_outputs(i):
                vk = VK[i % 2]
                pe.wait_ge(E("a_am"), i + 1)
                pe.wait_ge(E("a_s"), 2 * i + 2)
                if i >= 2:
                    pe.wait_ge(E("a_yev"), i - 1)
                yb = M3[4 + i % 2]
                for p in range(2):
                    for hh in range(2):
                        pe.matmul(yb[64 * hh:64 * hh + 64, p, :], vk[:, p, 64 * hh:64 * hh + 64], ATT[i % 2][:, 2 * p + hh, :],
                                  start=True, stop=False, skip_group_check=True)
                    for c in range(2):
                        n = 2 * i + c
                        mm = pe.matmul(yb[:, p, 64 * c:64 * c + 64],
                                       data(B + 6)[:, 256 * (n % 4) + P * p:256 * (n % 4) + P * p + P],
                                       tile(A, i)[:, 64 * c:64 * c + 64], start=False, stop=True, skip_group_check=True)
                mm.then_inc(E("a_y"), 1)

            gla_scores(0)
            for i in range(NT):
                gla_states(i)
                if i + 1 < NT:
                    gla_scores(i + 1)
                gla_outputs(i)
            kv(11, 12)
            norms(20, 22)
            kv(12, 14)
            norms(22, 24)
            kv(14, KV_ITEMS)


def constants_block(nc, cst_tiles, a, CW, CB, loaded, XR, LNB, x, x_loaded):
    ident, ones, eps = cst_tiles
    with Phase(nc, "const") as ph, ExitStack() as ctx:
        sem = ph.sem
        zeroed, filled = sem("zeroed"), sem("filled")
        block = ctx.enter_context(nc.Block())

        @block.gpsimd
        def _(pool):
            pool.memset(ident[:], 0.0).then_inc(zeroed, 1)
            pool.wait_ge(zeroed, 1)
            pool.affine_select(out=ident[:], in_=ident[:], compare_op=ALU.not_equal, fill=1.0, base=0,
                               pattern=[[-1, P]], channel_multiplier=1).then_inc(filled, 1)
            pool.memset(eps[:], EPS).then_inc(filled, 1)
            pool.memset(ones[:], 1.0).then_inc(filled, 1)

        @block.sync
        def _(sp):
            for i in range(NT):
                sp.dma_start(XR[:, i, :], x[i * P:(i + 1) * P, :]).then_inc(x_loaded[i], 16)
                if i == 0:
                    sp.dma_start(LNB, a["ln_mix"][0].partition_broadcast(P)).then_inc(x_loaded[0], 16)
            with nc.allow_non_contiguous_dma(reason="small parameter columns"):
                for j in range(3):
                    sp.dma_start(CW[:, :, j], a["ffn_conv_w"][0, j].rearrange("(f p) -> p f", p=P)).then_inc(loaded, 16)
                sp.dma_start(CB[:], a["ffn_conv_b"][0].rearrange("(f p) -> p f", p=P)).then_inc(loaded, 16)


def build(nc, a, out):
    x, mem = a["x"][0], a["mem"][0]
    with ExitStack() as ctx:
        sb = lambda c, s, shape, dt=F32: c.enter_context(nc.sbuf_tensor(s, shape, dt))
        ident, ones, eps = sb(ctx, "ident", [P, P]), sb(ctx, "ones1", [P, 1]), sb(ctx, "eps", [P, 1])
        CW, CB = sb(ctx, "CW", [P, NF, 3]), sb(ctx, "CB", [P, NF])
        HALO = sb(ctx, "HALO", [P, NF, 2])
        stored = ctx.enter_context(nc.semaphore("stored"))
        cst = {"ident": ident[:], "eps": eps[:], "one": ones[:]}
        XR = sb(ctx, "XR", [P, NT, D])
        x_loaded = [ctx.enter_context(nc.semaphore(f"x_loaded{i}")) for i in range(NT)]
        loaded = ctx.enter_context(nc.semaphore("ffn_parameters_loaded"))
        HH, HL = sb(ctx, "HH", [P, KT, T], F32R), sb(ctx, "HL", [P, KT, T], F32R)
        with ExitStack() as attn:
            SL = sb(attn, "slots", [P, 16, SW])
            LNB = SL[:, 0, 0:D]
            constants_block(nc, (ident, ones, eps), a, CW, CB, loaded, XR, LNB, x, x_loaded)
            norm_block(nc, "n1", cst, XR, HH, HL, LNB, range(NT), x_loaded, loaded)
            QN, KN, V, XS, LNB = (SL[:, s:s + n, PAD:SW] for s, n in ((0, NT), (B, 2), (B + 2, 2), (B + 4, 2), (B + 6, 1)))
            mixers_block(nc, cst, a, SL, XR, HH, HL)
            residual_product_norm(nc, "wo", cst, XR, HH, HL, a["w_out"][0], a["ln_xattn"][0], NT, XS, LNB[:, 0, :],
                                  XR, x)
            token_major_product(nc, "q", HH, HL, a["xa_wq"][0], NT, 2,
                                head_norm_evac(nc, "qn", cst, QN, NT, a["xa_qn"][0], XA_DIM ** -0.5, KN, a["xa_kn"][0]))
            memory_attention_block(nc, cst, QN, KN, V, HH, HL)
            residual_product_norm(nc, "xo", cst, XR, HH, HL, a["xa_wo"][0], a["ln_ffn"][0], NT // 2, XS, LNB[:, 0, :])
        for u in range(2):
            ffn_block(nc, u, cst, XR, HH, HL, HALO, CW, CB, a["ffn_w_up"][0], a["ffn_w_down"][0],
                      a["ln_ffn"][0], out, stored)
        Phase.finish(nc)


def kernel(**inputs):
    import numpy as _np
    import concourse.bacc as _bacc
    from concourse import mybir as _mybir
    from concourse.bass_utils import run_bass_kernel_spmd as _run

    nc = _bacc.Bacc("TRN2", target_bir_lowering=False, num_devices=1)
    arrays, args = {}, {}
    for name, value in inputs.items():
        arrays[f"in_{name}"] = _np.ascontiguousarray(value)
        args[name] = nc.dram_tensor(f"in_{name}", arrays[f"in_{name}"].shape, _mybir.dt.float32,
                                    kind="ExternalInput").ap()
    out = nc.dram_tensor("out", (1, T, D), _mybir.dt.float32, kind="ExternalOutput").ap()
    build(nc, args, out[0])
    return _run(nc, [arrays], core_ids=[0]).results[0]["out"]
```
